# Optimizing a Trainium2 kernel written in Bass

```python
import jax, jax.numpy as jnp
from jax import lax
import numpy as np

D_MODEL = 1024
BATCH = 1
SEQ = 1024
DEPTH = 1

HEAD_DIM = 64
N_Q_HEADS = D_MODEL // HEAD_DIM
N_KV_HEADS = 2
GQA_GROUP = N_Q_HEADS // N_KV_HEADS
WINDOW = 128
ATTN_WIDTH = N_Q_HEADS * HEAD_DIM
KV_WIDTH = N_KV_HEADS * HEAD_DIM
N_BUCKETS = 32
MAX_DISTANCE = 128
SGU_WIDTH = D_MODEL
SGU_GROUPS = 8
SGU_GROUP_DIM = SGU_WIDTH // SGU_GROUPS
CHUNK = 128
N_BRANCHES = 2
EPS = 1e-6
NEG_INF = -1e30
SPLITS = (ATTN_WIDTH, KV_WIDTH, KV_WIDTH, ATTN_WIDTH, SGU_WIDTH, SGU_WIDTH, SGU_WIDTH, D_MODEL, D_MODEL)
IN_COLS = 2 * ATTN_WIDTH + 2 * KV_WIDTH + 3 * SGU_WIDTH + N_BRANCHES * D_MODEL

kernel_name = "hybrid_swa_sink_gmlp_gated_block"

def rms_norm(x, g):
    xf = x.astype(jnp.float32)
    y = xf * lax.rsqrt(jnp.mean(xf * xf, axis=-1, keepdims=True) + EPS)
    return (y * g.astype(jnp.float32)).astype(x.dtype)

def layer_norm(x, g, b):
    xf = x.astype(jnp.float32)
    mu = jnp.mean(xf, axis=-1, keepdims=True)
    xc = xf - mu
    y = xc * lax.rsqrt(jnp.mean(xc * xc, axis=-1, keepdims=True) + EPS)
    return (y * g.astype(jnp.float32) + b.astype(jnp.float32)).astype(x.dtype)

def t5_bucket(dist):
    max_exact = N_BUCKETS // 2
    large = max_exact + (np.log(np.maximum(dist, max_exact) / max_exact)
                         / np.log(MAX_DISTANCE / max_exact)
                         * (N_BUCKETS - max_exact)).astype(np.int32)
    large = np.minimum(large, N_BUCKETS - 1)
    return np.where(dist < max_exact, dist, large).astype(np.int32)

def sliding_window_attention(q, k, v, sinks, rel_bias):
    B, S = q.shape[0], q.shape[1]
    nb = S // WINDOW
    qb = q.reshape(B, nb, WINDOW, N_KV_HEADS, GQA_GROUP, HEAD_DIM)

    def band(t):
        tb = t.reshape(B, nb, WINDOW, N_KV_HEADS, HEAD_DIM)
        prev = jnp.pad(tb, ((0, 0), (1, 0), (0, 0), (0, 0), (0, 0)))[:, :-1]
        return jnp.concatenate([prev, tb], axis=2)

    kb, vb = band(k), band(v)
    scores = jnp.einsum('bnqhgd,bnkhd->bnhgqk', qb, kb,
                        preferred_element_type=jnp.float32) * (HEAD_DIM ** -0.5)

    qi = np.arange(WINDOW)[:, None]
    kj = np.arange(2 * WINDOW)[None, :]
    dist = qi + WINDOW - kj
    in_window = (dist >= 0) & (dist < WINDOW)
    bucket = t5_bucket(np.clip(dist, 0, None))
    bias = jnp.transpose(rel_bias[bucket].astype(jnp.float32), (2, 0, 1))
    bias = bias.reshape(N_KV_HEADS, GQA_GROUP, WINDOW, 2 * WINDOW)
    block_ok = (np.arange(nb)[:, None] > 0) | (np.arange(2 * WINDOW)[None, :] >= WINDOW)
    mask = in_window[None, None, None] & block_ok[:, None, None, None, :]
    scores = jnp.where(mask, scores + bias, NEG_INF)

    sink = sinks.astype(jnp.float32).reshape(N_KV_HEADS, GQA_GROUP, 1, 1)
    m = jnp.maximum(jnp.max(scores, axis=-1, keepdims=True), sink)
    p = jnp.exp(scores - m)
    denom = jnp.sum(p, axis=-1, keepdims=True) + jnp.exp(sink - m)
    probs = (p / denom).astype(vb.dtype)
    out = jnp.einsum('bnhgqk,bnkhd->bnqhgd', probs, vb)
    return out.reshape(B, S, ATTN_WIDTH)

def spatial_gating(u, v, ln_g, ln_b, w_s, b_s):
    B, S = u.shape[0], u.shape[1]
    nc = S // CHUNK
    vn = layer_norm(v, ln_g, ln_b)
    vc = vn.reshape(B, nc, CHUNK, SGU_GROUPS, SGU_GROUP_DIM)
    causal = np.tril(np.ones((CHUNK, CHUNK), dtype=bool))
    w = jnp.where(causal[None], w_s, jnp.zeros_like(w_s))
    mixed = jnp.einsum('gts,bnsgd->bntgd', w, vc) + b_s.T[:, :, None]
    return u * mixed.reshape(B, S, SGU_WIDTH)

def setup_inputs(seed: int = 0) -> dict:
    key = jax.random.key(seed)
    ks = jax.random.split(key, 16)
    f32 = jnp.float32
    nrm = lambda k, shape, s: jax.random.normal(k, shape, f32) * s
    return {
        "x": nrm(ks[0], (BATCH, SEQ, D_MODEL), 1.0),
        "rel_bias": nrm(ks[1], (N_BUCKETS, N_Q_HEADS), 0.5),
        "pre_norm": 1.0 + nrm(ks[2], (DEPTH, D_MODEL), 0.05),
        "post_norm": 1.0 + nrm(ks[3], (DEPTH, D_MODEL), 0.05),
        "w_in": nrm(ks[4], (DEPTH, D_MODEL, IN_COLS), D_MODEL ** -0.5),
        "sinks": nrm(ks[5], (DEPTH, N_Q_HEADS), 0.5),
        "sgu_ln_g": 1.0 + nrm(ks[6], (DEPTH, SGU_WIDTH), 0.05),
        "sgu_ln_b": nrm(ks[7], (DEPTH, SGU_WIDTH), 0.02),
        "w_spatial": nrm(ks[8], (DEPTH, SGU_GROUPS, CHUNK, CHUNK), CHUNK ** -0.5),
        "b_spatial": 1.0 + nrm(ks[9], (DEPTH, SGU_GROUPS, CHUNK), 0.1),
        "w_branch_a": nrm(ks[10], (DEPTH, ATTN_WIDTH, D_MODEL), ATTN_WIDTH ** -0.5),
        "w_branch_b": nrm(ks[11], (DEPTH, SGU_WIDTH, D_MODEL), SGU_WIDTH ** -0.5),
        "w_out": nrm(ks[12], (DEPTH, D_MODEL, D_MODEL), D_MODEL ** -0.5),
    }

def reference(x, rel_bias, pre_norm, post_norm, w_in, sinks, sgu_ln_g, sgu_ln_b,
              w_spatial, b_spatial, w_branch_a, w_branch_b, w_out):
    B, S = x.shape[0], x.shape[1]
    offsets = [int(o) for o in np.cumsum(SPLITS)[:-1]]
    for l in range(DEPTH):
        h = rms_norm(x, pre_norm[l])
        proj = h @ w_in[l]
        q, k, v, gate_a, u_b, v_b, gate_b, mg_a, mg_b = jnp.split(proj, offsets, axis=-1)
        o_a = sliding_window_attention(
            q.reshape(B, S, N_Q_HEADS, HEAD_DIM),
            k.reshape(B, S, N_KV_HEADS, HEAD_DIM),
            v.reshape(B, S, N_KV_HEADS, HEAD_DIM),
            sinks[l], rel_bias)
        y_a = (o_a * jax.nn.silu(gate_a)) @ w_branch_a[l]
        o_b = spatial_gating(jax.nn.gelu(u_b, approximate=False), jax.nn.gelu(v_b, approximate=False),
                             sgu_ln_g[l], sgu_ln_b[l], w_spatial[l], b_spatial[l])
        y_b = (o_b * jax.nn.silu(gate_b)) @ w_branch_b[l]
        merged = jax.nn.sigmoid(mg_a) * y_a + jax.nn.sigmoid(mg_b) * y_b
        out = merged @ w_out[l]
        x = x + rms_norm(out, post_norm[l])
    return x


_drawn_inputs = setup_inputs


def setup_inputs(seed=0):
    import zlib

    import numpy as np

    out = dict(_drawn_inputs(seed))
    spreads = {}
    factors = {'sinks': 8.0, 'sgu_ln_g': 2.929, 'sgu_ln_b': 7.314}
    for name, (base, spread) in spreads.items():
        noise = np.random.default_rng([zlib.crc32(name.encode()), seed]).standard_normal(out[name].shape)
        drawn = base * np.exp(spread * noise) if base else spread * noise
        out[name] = __import__('jax').numpy.asarray(drawn.astype(out[name].dtype))
    for name, factor in factors.items():
        out[name] = (out[name] * factor).astype(out[name].dtype)
    return out
```

```python
import numpy as np
import concourse.bass as bass
from concourse import mybir
from contextlib import ExitStack

P = 128
D_MODEL = 1024
SEQ = 1024
HEAD_DIM = 64
N_HEADS = D_MODEL // HEAD_DIM
N_KV = 2
KT = D_MODEL // P
NT = SEQ // P
HALF = 512
N_BUCKETS = 32
MAX_DISTANCE = 128
WINDOW = 128
EPS = 1e-6
NEG_INF = -1e30
PAIRS = N_HEADS // 2
PAIRS_PER_KV = PAIRS // N_KV

Q_COL = 0
K_COL = Q_COL + D_MODEL
V_COL = K_COL + N_KV * HEAD_DIM
GA_COL = V_COL + N_KV * HEAD_DIM
U_COL = GA_COL + D_MODEL
VB_COL = U_COL + D_MODEL
GB_COL = VB_COL + D_MODEL
MGA_COL = GB_COL + D_MODEL
MGB_COL = MGA_COL + D_MODEL

N_U = NT
N_MB = N_U + 2 * KT
N_KVU = N_MB + 2 * KT
N_ATT = N_KVU + 2
N_YA = N_ATT + 3 * PAIRS
N_OUT = N_YA + KT
BIAS_ROW = 3 * P


def bucket_runs():
    dist = np.arange(WINDOW)
    exact = N_BUCKETS // 2
    large = exact + (np.log(np.maximum(dist, exact) / exact)
                     / np.log(MAX_DISTANCE / exact) * (N_BUCKETS - exact)).astype(np.int32)
    bucket = np.where(dist < exact, dist, np.minimum(large, N_BUCKETS - 1))
    return [(int(b), int(np.argmax(bucket == b)), int(np.sum(bucket <= b))) for b in np.unique(bucket)]


class Chain:

    def __init__(self, eng, sem):
        self.eng, self.sem, self.base, self.k = eng, sem, 0, 0

    def link(self, ins):
        self.k += 1
        ins.then_inc(self.sem, 1)
        self.eng.wait_ge(self.sem, self.base + self.k)

    def at(self, base):
        self.base, self.k = base, 0


def build(nc, x, rel_bias, pre_norm, post_norm, w_in, sinks, sgu_ln_g, sgu_ln_b,
          w_spatial, b_spatial, w_branch_a, w_branch_b, w_out, out):
    f32 = mybir.dt.float32
    f32r = mybir.dt.float32r
    bf16 = mybir.dt.bfloat16
    ACT = mybir.ActivationFunctionType
    ALU = mybir.AluOpType

    w_in_t = w_in[0].rearrange("(k p) c -> p k c", p=P)
    w_a_t = w_branch_a[0].rearrange("(k p) c -> p k c", p=P)
    w_b_t = w_branch_b[0].rearrange("(k p) c -> p k c", p=P)
    w_out_t = w_out[0].rearrange("(k p) c -> p k c", p=P)

    mix_d = nc.dram_tensor("mix_d", [KT, P, SEQ], f32)
    acc_d = nc.dram_tensor("acc_d", [KT, P, SEQ], f32)
    sig_d = nc.dram_tensor("sig_d", [KT, P, SEQ], f32)
    bias_d = nc.dram_tensor("bias_d", [N_HEADS, BIAS_ROW], f32)
    skew_d = nc.dram_tensor("skew_d", [N_HEADS, P, BIAS_ROW], f32)

    with ExitStack() as ctx:
        def sb(name, shape, dt=f32, scope=ctx):
            return scope.enter_context(nc.sbuf_tensor(name, shape, dt))

        def sem(name):
            return ctx.enter_context(nc.semaphore(name))

        ht_hi = sb("ht_hi", [P, KT * SEQ], f32r)
        ht_lo = sb("ht_lo", [P, KT * SEQ], f32r)
        g_hi = sb("g_hi", [P, KT * SEQ], f32r)
        g_lo = sb("g_lo", [P, KT * SEQ], f32r)
        raw = [sb(f"raw{b}", [P, 1024]) for b in range(2)]
        w_hi = [sb(f"w_hi{b}", [P, 1024], f32r) for b in range(2)]
        w_lo = [sb(f"w_lo{b}", [P, 1024], f32r) for b in range(2)]
        buf_t = sb("buf_t", [P, SEQ])
        buf_a = sb("buf_a", [P, SEQ])
        buf_b = sb("buf_b", [P, SEQ])
        junk = sb("junk", [P, SEQ], bf16)
        ident = sb("ident", [P, P])
        neg_half = sb("neg_half", [P, 1])
        ssq = sb("ssq", [P, 2])
        msq = sb("msq", [P, 2])
        rstd = sb("rstd", [P, 2])
        bn6 = sb("bn6", [P, 12])
        mean_var = sb("mean_var", [P, 2])
        var_eps = sb("var_eps", [P, 1])
        ln_rstd = sb("ln_rstd", [P, 1])
        sink_b = sb("sink_b", [P, N_HEADS])
        sink_p = sb("sink_p", [P, 2])
        row_max = sb("row_max", [P, 2 * NT])
        neg_max = sb("neg_max", [P, 2 * NT])
        sink_d = sb("sink_d", [P, 2 * NT])
        row_sum = sb("row_sum", [P, 2 * NT])
        sink_e = sb("sink_e", [P, 2 * NT])
        denom = sb("denom", [P, 2 * NT])
        inv_den = sb("inv_den", [P, 2 * NT])
        rel_t = sb("rel_t", [N_HEADS, N_BUCKETS])
        bias_row = sb("bias_row", [N_HEADS, BIAS_ROW])

        with ExitStack() as s0:
            x_b = [sb(f"x_b{b}", [P, D_MODEL], f32, s0) for b in range(2)]
            pre_b = sb("pre_b", [P, D_MODEL], f32, s0)
            lng_b = sb("lng_b", [P, D_MODEL], f32, s0)
            lnb_b = sb("lnb_b", [P, D_MODEL], f32, s0)
            bs_b = sb("bs_b", [P, KT * P], f32, s0)
            mix_b = [sb(f"mix_b{b}", [P, KT * P], f32, s0) for b in range(2)]
            vn_hi = sb("vn_hi", [P, D_MODEL], f32r, s0)
            vn_lo = sb("vn_lo", [P, D_MODEL], f32r, s0)
            ws_hi = sb("ws_hi", [P, KT * P], f32r, s0)
            ws_lo = sb("ws_lo", [P, KT * P], f32r, s0)
        with ExitStack() as s1:
            k_hi = sb("k_hi", [P, N_KV * SEQ], f32r, s1)
            k_lo = sb("k_lo", [P, N_KV * SEQ], f32r, s1)
            v_st = sb("v_st", [P, N_KV * NT * P], f32r, s1)
            q_st = [sb(f"q_st{h}", [P, SEQ], f32r, s1) for h in range(2)]
            pt_hi = sb("pt_hi", [P, 512], f32r, s1)
            pt_lo = sb("pt_lo", [P, 512], f32r, s1)
            prob = [sb(f"prob{b}", [P, 512], f32, s1) for b in range(3)]
            bias_t = sb("bias_t", [P, 512], f32, s1)
            o_tmp = [sb(f"o_tmp{b}", [P, 256], f32, s1) for b in range(2)]
        with ExitStack() as s2:
            wo_hi = sb("wo_hi", [P, KT * HALF], f32r, s2)
            wo_lo = sb("wo_lo", [P, KT * HALF], f32r, s2)
            x_r = [sb(f"x_r{b}", [P, D_MODEL], f32, s2) for b in range(2)]

        acc = [ctx.enter_context(nc.psum_tensor(f"acc{b}", [P, 1024], f32)) for b in range(2)]
        ps_t = ctx.enter_context(nc.psum_tensor("ps_t", [P, 1024], f32))
        ps_m = ctx.enter_context(nc.psum_tensor("ps_m", [P, 1024], f32))
        ps_s, ps_p = ps_t[:, 0:512], ps_t[:, 512:1024]

        raw_in = [sem(f"raw_in{b}") for b in range(2)]
        hi_done, lo_done = sem("hi_done"), sem("lo_done")
        unit_done = sem("unit_done")
        acc_free = [sem(f"acc_free{b}") for b in range(2)]
        x_in = [sem(f"x_in{b}") for b in range(2)]
        pre_in, ln_in, bs_in, wsp_in = sem("pre_in"), sem("ln_in"), sem("bs_in"), sem("wsp_in")
        rel_in, sink_in, bias_out, skew_out = sem("rel_in"), sem("sink_in"), sem("bias_out"), sem("skew_out")
        bias_made = sem("bias_made")
        const_ok, wsp_ok = sem("const_ok"), sem("wsp_ok")
        ssq_ok, msq_ok, rstd_ok, h_ok = sem("ssq_ok"), sem("msq_ok"), sem("rstd_ok"), sem("h_ok")
        tr_done = sem("tr_done")
        hs_hi, hs_lo, ht_ok = sem("hs_hi"), sem("hs_lo"), sem("ht_ok")
        wsh_ok, wsl_ok = sem("wsh_ok"), sem("wsl_ok")
        vg_ok, var_ok, lnr_ok, vn_ok = sem("vg_ok"), sem("var_ok"), sem("lnr_ok"), sem("vn_ok")
        vnh_ok, vnl_ok = sem("vnh_ok"), sem("vnl_ok")
        mix_done, mix_ok = sem("mix_done"), sem("mix_ok")
        mix_out = [sem(f"mix_out{b}") for b in range(2)]
        mix_in, gelu_ok, gate_t_ok, um_ok, prod_ok = sem("mix_in"), sem("gelu_ok"), sem("gate_t_ok"), sem("um_ok"), sem("prod_ok")
        ghi_ok, g_ready = sem("ghi_ok"), sem("g_ready")
        mtan_ok, acc_ok, spill_out = sem("mtan_ok"), sem("acc_ok"), sem("spill_out")
        kraw_ok, khi_ok, klo_ok = sem("kraw_ok"), sem("khi_ok"), sem("klo_ok")
        vraw_ok, vt_done, vhi_ok, vlo_ok = sem("vraw_ok"), sem("vt_done"), sem("vhi_ok"), sem("vlo_ok")
        bias_in = sem("bias_in")
        q_hi_ok, q_ok = sem("q_hi_ok"), sem("q_ok")
        scores_ok, scores_used, max_ok, exp_ok, inv_ok, prob_ok = (
            sem("scores_ok"), sem("scores_used"), sem("max_ok"), sem("exp_ok"), sem("inv_ok"), sem("prob_ok"))
        pt_done, pth_ok, ptl_ok, pv_done = sem("pt_done"), sem("pth_ok"), sem("ptl_ok"), sem("pv_done")
        otmp_ok, oadd_ok, gtan_ok, gate_ok, og_ok = (
            sem("otmp_ok"), sem("oadd_ok"), sem("gtan_ok"), sem("gate_ok"), sem("og_ok"))
        siga_ok = sem("siga_ok")
        sigr_in, accr_in, mrg_ok, mhi_ok = sem("sigr_in"), sem("accr_in"), sem("mrg_ok"), sem("mhi_ok")
        post_in, xr_in = sem("post_in"), [sem(f"xr_in{b}") for b in range(2)]
        mt_hi, mt_lo = sem("mt_hi"), sem("mt_lo")
        osq_ok, oms_ok, ors_ok, y_ok = sem("osq_ok"), sem("oms_ok"), sem("ors_ok"), sem("y_ok")
        y_out = [sem(f"y_out{b}") for b in range(2)]
        dve_own, pool_own, waited = sem("dve_own"), sem("pool_own"), sem("waited")

        block = ctx.enter_context(nc.Block())

        def stand_alone(eng):
            eng.sem_inc(waited, 1)

        def tile(buf, i, n=SEQ):
            return buf[:, bass.ds(i * n, n)]

        def col3(buf, i):
            return buf[:, :].rearrange("p (k s) -> p k s", k=KT)[:, :, bass.ds(i * P, P)]

        def k3(buf):
            return buf[:, :].rearrange("p (k s) -> p k s", k=KT)

        def half(c, i=0, s=0):
            return c // 2 + (s // 2) * i if s else c // 2

        @block.sync
        def _(sp):
            def load_raw(n, b, src, col):
                sp.wait_ge(hi_done, n - 1)
                stand_alone(sp)
                sp.wait_ge(lo_done, n - 1)
                stand_alone(sp)
                sp.dma_start(raw[b][:, :].rearrange("p (k c) -> p k c", c=P),
                             src[:, :, bass.ds(col, P)]).then_inc(raw_in[b], 16)

            def load_x(t, b):
                sp.dma_start(x_b[b][:, :], x[0, bass.ds(t * P, P), :]).then_inc(x_in[b], 16)

            def load_vb(k):
                if k >= 2:
                    sp.wait_ge(hi_done, k - 1)
                    sp.wait_ge(lo_done, k - 1)
                sp.dma_start(raw[k % 2][:, :], w_in_t[:, k, VB_COL:VB_COL + D_MODEL]).then_inc(raw_in[k % 2], 16)

            load_x(0, 0)
            load_vb(0)
            sp.dma_start(pre_b[:, :], pre_norm[0:1, :].to_broadcast([P, D_MODEL])).then_inc(pre_in, 16)
            load_vb(1)
            sp.dma_start(buf_b[:, :].rearrange("p (g s) -> p g s", g=KT),
                         w_spatial[0].rearrange("g t s -> t g s")).then_inc(wsp_in, 16)
            load_vb(2)
            load_x(1, 1)
            for k in range(3, KT):
                load_vb(k)
            sp.dma_start(lng_b[:, :], sgu_ln_g[0:1, :].to_broadcast([P, D_MODEL])).then_inc(ln_in, 16)
            sp.dma_start(lnb_b[:, :], sgu_ln_b[0:1, :].to_broadcast([P, D_MODEL])).then_inc(ln_in, 16)
            sp.dma_start(bs_b[:, :], b_spatial.rearrange("a g t -> a (g t)").to_broadcast([P, KT * P])).then_inc(bs_in, 16)
            sp.dma_start(sink_b[:, :], sinks[0:1, :].to_broadcast([P, N_HEADS])).then_inc(sink_in, 16)
            sp.dma_start(rel_t[:, :], rel_bias.rearrange("b h -> h b"), allow_slow_non_contiguous=True).then_inc(rel_in, 16)
            load_raw(N_U, 0, w_in_t, U_COL)
            load_raw(N_U + 1, 1, w_in_t, GB_COL)
            with sp.Fori(1, NT // 2) as i:
                for b in range(2):
                    sp.wait_ge(tr_done, 2 * i + b)
                    load_x(2 * i + b, b)

            def load_mix(g):
                sp.dma_start(buf_b[:, :], mix_d[bass.ds(g, 1), :, :].rearrange("a p s -> p (a s)")).then_inc(mix_in, 16)

            for b in range(2):
                sp.wait_ge(mix_out[b], 16 * (1 + NT // 2))
            load_mix(0)
            sp.wait_ge(bias_made, 1)
            sp.dma_start(bias_d[:, :], bias_row[:, :]).then_inc(bias_out, 16)
            sp.wait_ge(bias_out, 16)
            sp.dma_start(skew_d[:, :, :], bass.AP(bias_d, 0, [[BIAS_ROW, N_HEADS], [0, P], [1, BIAS_ROW]])).then_inc(skew_out, 16)
            with sp.Fori(1, KT) as g:
                load_raw(N_U + 2 * g, 0, w_in_t, U_COL + g * P)
                load_raw(N_U + 2 * g + 1, 1, w_in_t, GB_COL + g * P)
                sp.wait_ge(um_ok, g)
                load_mix(g)
            with sp.Fori(0, KT) as j:
                load_raw(N_MB + 2 * j, 0, w_in_t, MGB_COL + j * P)
                load_raw(N_MB + 2 * j + 1, 1, w_b_t, j * P)
            load_raw(N_KVU, 0, w_in_t, K_COL)
            load_raw(N_KVU + 1, 1, w_in_t, V_COL)
            sp.wait_ge(skew_out, 16)
            sp.wait_ge(mix_done, NT)
            with sp.Fori(0, PAIRS // 2) as i:
                for r in range(2):
                    p = 2 * i + r
                    n = N_ATT + 3 * r + 6 * i
                    load_raw(n, r, w_in_t, Q_COL + p * P)
                    load_raw(n + 1, 1 - r, w_in_t, GA_COL + p * P)
                    sp.wait_ge(scores_used, 8 * p + 1)
                    sp.dma_start(bias_t[:, :].rearrange("p (h j) -> p h j", h=2),
                                 bass.AP(skew_d, p * (2 * P * BIAS_ROW) + (P - 1),
                                         [[BIAS_ROW - 1, P], [P * BIAS_ROW, 2], [1, 2 * P]])).then_inc(bias_in, 16)
                    load_raw(n + 2, r, w_in_t, MGA_COL + p * P)
            with sp.Fori(0, KT // 2) as i:
                for b in range(2):
                    load_raw(N_YA + b + 2 * i, b, w_a_t, (2 * i + b) * P)
            for s in range(8):
                r, hf, kk = N_OUT + s, s // 4, s % 4
                sp.wait_ge(hi_done, r - 1)
                sp.wait_ge(lo_done, r - 1)
                sp.dma_start(raw[r % 2][:, :].rearrange("p (k c) -> p k c", k=2),
                             w_out_t[:, 2 * kk:2 * kk + 2, hf * HALF:(hf + 1) * HALF]).then_inc(raw_in[r % 2], 16)
            sp.wait_ge(acc_free[1], N_OUT // 2)
            sp.dma_start(buf_t[:, :], post_norm[0:1, :].to_broadcast([P, D_MODEL])).then_inc(post_in, 16)

            def load_res(t, b):
                sp.dma_start(x_r[b][:, :], x[0, bass.ds(t * P, P), :]).then_inc(xr_in[b], 16)

            def store(t, b):
                sp.wait_ge(y_ok, t + 1)
                sp.dma_start(out[0, bass.ds(t * P, P), :], (buf_a, buf_b)[b][:, :]).then_inc(y_out[b], 16)

            load_res(0, 0)
            load_res(1, 1)
            with sp.Fori(0, NT // 2 - 1) as i:
                for b in range(2):
                    store(2 * i + b, b)
                    load_res(2 * i + b + 2, b)
            store(NT - 2, 0)
            store(NT - 1, 1)
            for b in range(2):
                sp.wait_ge(y_out[b], 16 * NT // 2)

        @block.tensor
        def _(pe):
            def products(b, lh, ll, rh, rl):
                ops = []
                for k in range(KT):
                    for l, r, kind in ((lh, rh, 0), (lh, rl, 1), (ll, rh, 2)):
                        for hf in range(2):
                            ops.append((acc[b][:, hf * HALF:(hf + 1) * HALF], l[:, k * P:(k + 1) * P],
                                        r[:, k * SEQ + hf * HALF:k * SEQ + (hf + 1) * HALF],
                                        k == 0 and kind == 0, k == KT - 1 and kind == 2))
                return ops

            def run(ops):
                last = None
                for o, l, r, a, z in ops:
                    last = nc.tensor.matmul(o, l, r, start=a, stop=z, skip_group_check=True)
                return last

            def start_unit(n, hn, b):
                pe.wait_ge(lo_done, n + 1)
                pe.wait_ge(acc_free[b], hn)

            def unit(n, hn, b, rh, rl):
                start_unit(n, hn, b)
                run(products(b, w_hi[b], w_lo[b], rh, rl)).then_inc(unit_done, 1)

            def transpose_h(t, b):
                pe.wait_ge(h_ok, t + 1)
                for k in range(KT):
                    last = nc.tensor.transpose(ps_t[:, k * P:(k + 1) * P], x_b[b][:, k * P:(k + 1) * P], ident[:, :])
                last.then_inc(tr_done, 1)

            def mix(t):
                pe.wait_ge(vnl_ok, t + 1)
                for g in range(KT):
                    c = slice(g * P, (g + 1) * P)
                    nc.tensor.matmul(ps_m[:, c], vn_hi[:, c], ws_hi[:, c], start=True, stop=False, skip_group_check=True)
                    nc.tensor.matmul(ps_m[:, c], vn_hi[:, c], ws_lo[:, c], start=False, stop=False, skip_group_check=True)
                    last = nc.tensor.matmul(ps_m[:, c], vn_lo[:, c], ws_hi[:, c], start=False, stop=True, skip_group_check=True)
                last.then_inc(mix_done, 1)

            def vb_unit(t, b):
                pe.wait_ge(hs_lo, t + 1)
                run(products(b, w_hi[b], w_lo[b], g_hi, g_lo)).then_inc(unit_done, 1)

            pe.wait_ge(const_ok, 1)
            transpose_h(0, 0)
            pe.wait_ge(wsp_ok, 1)
            pe.wait_ge(hs_lo, 1)
            for g in range(KT):
                c = slice(g * P, (g + 1) * P)
                last = nc.tensor.transpose(ps_t[:, c], buf_b[:, c], ident[:, :])
            last.then_inc(tr_done, 1)
            ops = products(0, w_hi[0], w_lo[0], g_hi, g_lo)
            for k in range(KT):
                pe.wait_ge(lo_done, k + 1)
                last = run(ops[6 * k:6 * k + 6])
            last.then_inc(unit_done, 1)
            pe.wait_ge(wsl_ok, 1)
            transpose_h(1, 1)
            with pe.Fori(0, NT // 2 - 1) as i:
                for b in (1, 0):
                    t = 2 * i + 2 - b
                    vb_unit(t, b)
                    transpose_h(t + 1, 1 - b)
                    mix(t - 1)
            vb_unit(NT - 1, 1)
            mix(NT - 2)
            mix(NT - 1)
            pe.wait_ge(ht_ok, NT)
            with pe.Fori(0, KT) as g:
                for b in range(2):
                    unit(N_U + b + 2 * g, half(N_U, g, 2), b, ht_hi, ht_lo)
            with pe.Fori(0, KT) as j:
                unit(N_MB + 2 * j, half(N_MB, j, 2), 0, ht_hi, ht_lo)
                pe.wait_ge(g_ready, KT)
                unit(N_MB + 1 + 2 * j, half(N_MB, j, 2), 1, g_hi, g_lo)
            unit(N_KVU, half(N_KVU), 0, ht_hi, ht_lo)
            unit(N_KVU + 1, half(N_KVU), 1, ht_hi, ht_lo)
            pe.wait_ge(acc_free[1], half(N_KVU) + 1)
            pe.wait_ge(mix_ok, NT)
            for t in range(NT):
                last = nc.tensor.transpose(ps_m[:, t * P:(t + 1) * P], buf_b[:, t * P:(t + 1) * P], ident[:, :])
            last.then_inc(vt_done, 1)

            def pair(kv, p, i, c, r):
                q_rows = half(c, i, 6) + 1

                def scores(blk):
                    s = 8 * p + blk
                    if blk == 0:
                        pe.wait_ge(acc_free[r], q_rows)
                    pe.wait_ge(scores_used, s + 1)
                    lo = P if blk == 0 else 0
                    kc = kv * SEQ + (blk - 1) * P
                    for h in range(2):
                        for kbuf, a in ((k_hi, True), (k_lo, False)):
                            last = nc.tensor.matmul(ps_s[:, h * 256 + lo:(h + 1) * 256], q_st[h][:, blk * P:(blk + 1) * P],
                                                    kbuf[:, kc + lo:kc + 256], start=a, stop=not a, skip_group_check=True)
                    last.then_inc(scores_ok, 1)

                def transpose_p(blk):
                    s = 8 * p + blk
                    pe.wait_ge(prob_ok, s + 1)
                    if blk > 0:
                        pe.wait_ge(ptl_ok, s)
                    for h in range(2):
                        for kb in ((1,) if blk == 0 else (0, 1)):
                            c0 = (2 * h + kb) * P
                            last = nc.tensor.transpose(ps_p[:, c0:c0 + P], prob[blk % 3][:, c0:c0 + P], ident[:, :])
                    last.then_inc(pt_done, 1)

                def values(blk):
                    s = 8 * p + blk
                    pe.wait_ge(ptl_ok, s + 1)
                    if blk in (4, 6):
                        pe.wait_ge(oadd_ok, 4 * p + blk // 2 - 1)
                    for h in range(2):
                        o = ps_m[:, (blk // 2 % 2) * 512 + h * 256 + (blk % 2) * P:][:, 0:P]
                        kbs = (1,) if blk == 0 else (0, 1)
                        for kb in kbs:
                            v0 = (kv * NT + blk - 1 + kb) * P
                            c0 = (2 * h + kb) * P
                            for pt in (pt_hi, pt_lo):
                                last = nc.tensor.matmul(o, v_st[:, v0:v0 + P], pt[:, c0:c0 + P],
                                                        start=(kb == kbs[0] and pt is pt_hi),
                                                        stop=(kb == 1 and pt is pt_lo), skip_group_check=True)
                    if blk % 2:
                        last.then_inc(pv_done, 1)

                n0 = c + 6 * i
                unit(n0, half(c, i, 6), r, ht_hi, ht_lo)
                start_unit(n0 + 1, half(c + 1, i, 6), 1 - r)
                ops_a = products(1 - r, w_hi[1 - r], w_lo[1 - r], ht_hi, ht_lo)
                ops_m = products(r, w_hi[r], w_lo[r], ht_hi, ht_lo)
                ops = ops_a + ops_m
                at = [14 + (15 * k) // 2 for k in range(11)]
                for m in range(len(ops)):
                    if m in at:
                        k = at.index(m)
                        if k < 8:
                            scores(k)
                        if 3 <= k:
                            values(k - 3)
                        if 2 <= k < 10:
                            transpose_p(k - 2)
                    if m == len(ops_a):
                        start_unit(n0 + 2, half(c + 2, i, 6), r)
                    last = run(ops[m:m + 1])
                    if m == len(ops_a) - 1 or m == len(ops) - 1:
                        last.then_inc(unit_done, 1)

            pe.wait_ge(klo_ok, 1)
            for kv in range(N_KV):
                with pe.Fori(kv * PAIRS_PER_KV // 2, (kv + 1) * PAIRS_PER_KV // 2) as i:
                    for r in range(2):
                        pair(kv, 2 * i + r, i, N_ATT + 3 * r, r)
            pe.wait_ge(g_ready, 2 * KT)
            with pe.Fori(0, KT // 2) as i:
                for b in range(2):
                    unit(N_YA + b + 2 * i, half(N_YA, i, 2), b, g_hi, g_lo)

            def out_unit(t, i, b, first):
                pe.wait_ge(mt_hi, t + 1)
                pe.wait_ge(mt_lo, t + 1)
                pe.wait_ge(acc_free[b], half(N_OUT, i, 2) if not first else half(N_OUT))
                for hf in range(2):
                    rh, rl = ((wo_hi, wo_lo) if hf == 0 else (g_hi[:, 0:KT * HALF], g_hi[:, KT * HALF:2 * KT * HALF]))
                    for k in range(KT):
                        if first and k % 2 == 0:
                            pe.wait_ge(lo_done, N_OUT + 4 * hf + k // 2 + 1)
                        for l, r, kind in ((w_hi[b], rh, 0), (w_hi[b], rl, 1), (w_lo[b], rh, 2)):
                            last = nc.tensor.matmul(acc[b][:, hf * HALF:(hf + 1) * HALF], l[:, k * P:(k + 1) * P],
                                                    r[:, k * HALF:(k + 1) * HALF], start=(k == 0 and kind == 0),
                                                    stop=(k == KT - 1 and kind == 2), skip_group_check=True)
                last.then_inc(unit_done, 1)

            out_unit(0, 0, 0, True)
            out_unit(1, 0, 1, False)
            with pe.Fori(1, NT // 2) as i:
                for b in range(2):
                    out_unit(2 * i + b, i, b, False)

        @block.scalar
        def _(act):
            def split_hi(n, hn, b, dst=None):
                act.wait_ge(raw_in[b], 16 * (hn + 1))
                act.wait_ge(unit_done, n - 1)
                nc.scalar.activation(w_hi[b][:, :] if dst is None else dst, raw[b][:, :], ACT.Copy).then_inc(hi_done, 1)

            def vb_hi(k):
                act.wait_ge(raw_in[k % 2], 16 * (k // 2 + 1))
                nc.scalar.activation(tile(g_hi, k), raw[k % 2][:, :], ACT.Copy).then_inc(hi_done, 1)

            def square_x(t, ht, b):
                act.wait_ge(x_in[b], 16 * (ht + 1))
                nc.scalar.activation(junk[:, :], x_b[b][:, :], ACT.Square, accum_out=ssq[:, b:b + 1]).then_inc(ssq_ok, 1)

            def h_hi(t, n_tr, b):
                act.wait_ge(tr_done, n_tr)
                nc.scalar.activation(w_hi[b][:, :], ps_t[:, :], ACT.Copy).then_inc(hs_hi, 1)

            def gelu_v(t, b):
                act.wait_ge(unit_done, t + 1)
                nc.scalar.activation(buf_a[:, :], acc[b][:, :], ACT.Gelu).then_inc(acc_free[b], 1)

            def vn_split(t):
                act.wait_ge(vn_ok, t + 1)
                nc.scalar.activation(vn_hi[:, :], buf_a[:, :], ACT.Copy).then_inc(vnh_ok, 1)

            def spill_mix(t, b):
                act.wait_ge(mix_ok, t + 1)
                act.dma_start(mix_d[:, :, bass.ds(t * P, P)].rearrange("g p s -> p g s"),
                              mix_b[b][:, :].rearrange("p (g s) -> p g s", g=KT)).then_inc(mix_out[b], 16)

            for b in range(2):
                act.sem_inc(mix_out[b], 16)
            act.sem_inc(spill_out, 16)
            square_x(0, 0, 0)
            vb_hi(0)
            h_hi(0, 1, 0)
            vb_hi(1)
            act.wait_ge(tr_done, 2)
            nc.scalar.activation(ws_hi[:, :], ps_t[:, :], ACT.Copy).then_inc(wsh_ok, 1)
            vb_hi(2)
            square_x(1, 0, 1)
            for k in range(3, KT):
                vb_hi(k)
            h_hi(1, 3, 1)
            gelu_v(0, 0)
            vn_split(0)
            with act.Fori(0, NT // 2 - 1) as i:
                for b in (1, 0):
                    t = 2 * i + 2 - b
                    square_x(t + 1, i + 1, 1 - b)
                    act.wait_ge(ht_ok, t)
                    h_hi(t + 1, t + 3, 1 - b)
                    act.wait_ge(vnl_ok, t)
                    gelu_v(t, b)
                    act.wait_ge(mix_done, t)
                    vn_split(t)
                    spill_mix(t - 1, 1 - b)
            act.wait_ge(ht_ok, NT - 1)
            split_hi(N_U, half(N_U), 0)
            act.wait_ge(vnl_ok, NT - 1)
            gelu_v(NT - 1, 1)
            act.wait_ge(mix_done, NT - 1)
            vn_split(NT - 1)
            spill_mix(NT - 2, 0)
            act.wait_ge(ht_ok, NT)
            split_hi(N_U + 1, half(N_U + 1), 1)
            spill_mix(NT - 1, 1)
            act.wait_ge(vnl_ok, NT)

            with act.Fori(0, KT) as g:
                n = N_U + 2 * g
                act.wait_ge(unit_done, n + 1)
                nc.scalar.activation(buf_a[:, :], acc[0][:, :], ACT.Gelu).then_inc(acc_free[0], 1)
                split_hi(n + 2, half(N_U + 2, g, 2), 0)
                act.wait_ge(unit_done, n + 2)
                act.wait_ge(um_ok, g + 1)
                nc.scalar.activation(buf_t[:, :], acc[1][:, :], ACT.Tanh, scale=0.5).then_inc(gate_t_ok, 1)
                split_hi(n + 3, half(N_U + 3, g, 2), 1)
                act.wait_ge(prod_ok, g + 1)
                nc.scalar.activation(tile(g_hi, g), buf_t[:, :], ACT.Copy).then_inc(ghi_ok, 1)
            act.wait_ge(g_ready, KT)
            with act.Fori(0, KT) as j:
                n = N_MB + 2 * j
                act.wait_ge(unit_done, n + 1)
                act.wait_ge(acc_free[1], half(N_MB, j, 2))
                nc.scalar.activation(buf_t[:, :], acc[0][:, :], ACT.Tanh, scale=0.5).then_inc(acc_free[0], 1)
                split_hi(n + 2, half(N_MB + 2, j, 2), 0)
                split_hi(n + 3, half(N_MB + 3, j, 2), 1)
                act.wait_ge(acc_free[1], half(N_MB + 2, j, 2))
                act.dma_start(acc_d[bass.ds(j, 1), :, :].rearrange("a p s -> p (a s)"), buf_a[:, :]).then_inc(spill_out, 16)
            act.wait_ge(unit_done, N_KVU + 1)
            act.wait_ge(spill_out, 16 * (1 + KT))
            nc.scalar.activation(buf_a[:, :], acc[0][:, :], ACT.Copy).then_inc(acc_free[0], 1)
            split_hi(N_ATT, half(N_ATT), 0)
            act.wait_ge(acc_free[0], half(N_KVU) + 1)
            for kv in range(N_KV):
                rows = slice(kv * HEAD_DIM, (kv + 1) * HEAD_DIM)
                for hf in range(2):
                    last = nc.scalar.activation(k_hi[hf * HEAD_DIM:(hf + 1) * HEAD_DIM, kv * SEQ:(kv + 1) * SEQ],
                                                buf_a[rows, :], ACT.Copy)
            last.then_inc(khi_ok, 1)
            act.wait_ge(unit_done, N_KVU + 2)
            act.wait_ge(prod_ok, KT)
            nc.scalar.activation(buf_b[:, :], acc[1][:, :], ACT.Copy).then_inc(acc_free[1], 1)
            split_hi(N_ATT + 1, half(N_ATT + 1), 1)
            act.wait_ge(vt_done, 1)
            for kv in range(N_KV):
                last = nc.scalar.activation(
                    v_st[:, :].rearrange("p (v t x d) -> p v t x d", v=N_KV, t=NT, x=2)[:, kv, :, 0, :],
                    ps_m[:, :].rearrange("p (t v d) -> p t v d", t=NT, v=N_KV)[:, :, kv, :], ACT.Copy)
            last.then_inc(vhi_ok, 1)

            def pair(p, i, c, r):
                n0 = c + 6 * i
                act.wait_ge(unit_done, n0 + 1)
                nc.scalar.activation(q_st[0][0:64, :], acc[r][0:64, :], ACT.Copy)
                nc.scalar.activation(q_st[1][64:128, :], acc[r][64:128, :], ACT.Copy).then_inc(q_hi_ok, 1)
                split_hi(n0 + 2, half(c + 2, i, 6), r)
                for k in range(12):
                    if k < 8:
                        s = 8 * p + k
                        lo = P if k == 0 else 0
                        act.wait_ge(max_ok, s + 1)
                        for h in range(2):
                            w = prob[k % 3][:, h * 256 + lo:(h + 1) * 256]
                            nc.scalar.activation(w, w, ACT.Exp, bias=neg_max[:, 2 * k + h:2 * k + h + 1],
                                                 accum_out=row_sum[:, 2 * k + h:2 * k + h + 1])
                        nc.scalar.activation(sink_e[:, 2 * k:2 * k + 2], sink_d[:, 2 * k:2 * k + 2], ACT.Exp).then_inc(exp_ok, 1)
                    if 2 <= k < 10:
                        s = 8 * p + k - 2
                        act.wait_ge(pt_done, s + 1)
                        if k == 2:
                            last = nc.scalar.activation(pt_hi[:, :].rearrange("p (h c) -> p h c", h=2)[:, :, P:256],
                                                        ps_p.rearrange("p (h c) -> p h c", h=2)[:, :, P:256], ACT.Copy)
                        else:
                            last = nc.scalar.activation(pt_hi[:, :], ps_p, ACT.Copy)
                        last.then_inc(pth_ok, 1)
                    if k >= 5 and k % 2:
                        g = (k - 5) // 2
                        gg = 4 * p + g
                        act.wait_ge(pv_done, gg + 1)
                        if g >= 2:
                            act.wait_ge(oadd_ok, gg - 1)
                        o = ps_m[:, (g % 2) * 512:(g % 2 + 1) * 512]
                        nc.scalar.activation(o_tmp[g % 2][0:64, :], o[64:128, 0:256], ACT.Copy)
                        nc.scalar.activation(o_tmp[g % 2][64:128, :], o[0:64, 256:512], ACT.Copy).then_inc(otmp_ok, 1)
                    if k == 5:
                        act.wait_ge(unit_done, n0 + 2)
                        act.wait_ge(spill_out, 16 * (1 + KT) + 16 * p)
                        nc.scalar.activation(buf_t[:, :], acc[1 - r][:, :], ACT.Tanh, scale=0.5).then_inc(gtan_ok, 1)
                        split_hi(n0 + 3, half(c + 3, i, 6), 1 - r)
                act.wait_ge(unit_done, n0 + 3)
                act.wait_ge(acc_free[1 - r], half(c + 1, i, 6) + 1)
                nc.scalar.activation(buf_t[:, :], acc[r][:, :], ACT.Tanh, scale=0.5).then_inc(acc_free[r], 1)
                split_hi(n0 + 4, half(c + 4, i, 6), r)
                act.wait_ge(og_ok, p + 1)
                nc.scalar.activation(tile(g_hi, p), buf_b[:, :], ACT.Copy).then_inc(ghi_ok, 1)
                act.wait_ge(siga_ok, p + 1)
                act.dma_start(sig_d[bass.ds(p, 1), :, :].rearrange("a p s -> p (a s)"), buf_t[:, :]).then_inc(spill_out, 16)

            with act.Fori(0, PAIRS // 2) as i:
                for r in range(2):
                    pair(2 * i + r, i, N_ATT + 3 * r, r)

            def load_merge(j):
                act.dma_start(buf_t[:, :], sig_d[bass.ds(j, 1), :, :].rearrange("a p s -> p (a s)")).then_inc(sigr_in, 16)
                act.dma_start(buf_a[:, :], acc_d[bass.ds(j, 1), :, :].rearrange("a p s -> p (a s)")).then_inc(accr_in, 16)

            def merged_hi(j):
                act.wait_ge(mrg_ok, j + 1)
                nc.scalar.activation(tile(ht_hi, j), buf_b[:, :], ACT.Copy).then_inc(mhi_ok, 1)

            act.wait_ge(spill_out, 16 * (1 + KT + PAIRS))
            act.wait_ge(g_ready, 2 * KT)
            load_merge(0)
            with act.Fori(0, KT // 2 - 1) as i:
                for b in range(2):
                    j = 2 * i + b
                    split_hi(N_YA + b + 2 + 2 * i, half(N_YA + 2, i, 2), b)
                    merged_hi(j)
                    act.wait_ge(g_ready, 2 * KT + j + 1)
                    load_merge(j + 1)

            def split_out(s):
                r = N_OUT + s
                act.wait_ge(raw_in[r % 2], 16 * (r // 2 + 1))
                if s >= 4:
                    act.wait_ge(unit_done, N_OUT)
                nc.scalar.activation(tile(wo_hi if s < 4 else g_hi, s % 4), raw[r % 2][:, :], ACT.Copy).then_inc(hi_done, 1)

            split_out(0)
            split_out(1)
            merged_hi(KT - 2)
            act.wait_ge(g_ready, 3 * KT - 1)
            load_merge(KT - 1)
            split_out(2)
            split_out(3)
            merged_hi(KT - 1)

            def tile_hi(t, b):
                act.wait_ge(unit_done, N_OUT + t - 1)
                nc.scalar.activation(w_hi[b][:, :].rearrange("p (k s) -> p k s", k=KT),
                                     ht_hi[:, :].bitcast(f32).rearrange("p (k s) -> p k s", k=KT)[:, :, bass.ds(t * P, P)],
                                     ACT.Copy).then_inc(mt_hi, 1)

            def square_out(t, b):
                if isinstance(t, int):
                    act.wait_ge(osq_ok, t)
                else:
                    act.wait_ge(mt_hi, t + 2)
                act.wait_ge(unit_done, N_OUT + t + 1)
                nc.scalar.activation(junk[:, :], acc[b][:, :], ACT.Square, accum_out=ssq[:, b:b + 1]).then_inc(osq_ok, 1)

            act.wait_ge(mhi_ok, KT)
            tile_hi(0, 0)
            for s in range(4, 8):
                split_out(s)
            tile_hi(1, 1)
            with act.Fori(0, NT // 2 - 1) as i:
                for b in range(2):
                    square_out(2 * i + b, b)
                    tile_hi(2 * i + b + 2, b)
            square_out(NT - 2, 0)
            square_out(NT - 1, 1)

        @block.gpsimd
        def _(pool):
            def split_lo(n, b):
                pool.wait_ge(hi_done, n + 1)
                nc.gpsimd.tensor_tensor(w_lo[b][:, :], raw[b][:, :], w_hi[b][:, :].bitcast(f32), ALU.subtract).then_inc(lo_done, 1)

            def split_lo_to(n, b, dst, hi):
                pool.wait_ge(hi_done, n + 1)
                nc.gpsimd.tensor_tensor(dst, raw[b][:, :], hi.bitcast(f32), ALU.subtract).then_inc(lo_done, 1)

            def rsqrt_h(t, b):
                pool.wait_ge(msq_ok, t + 1)
                nc.gpsimd.tensor_tensor(rstd[:, b:b + 1], msq[:, b:b + 1], neg_half[:, :], ALU.pow).then_inc(rstd_ok, 1)

            def copy_h(t, b):
                pool.wait_ge(hs_lo, t + 1)
                stand_alone(pool)
                nc.gpsimd.tensor_copy(col3(ht_hi, t), k3(w_hi[b]).bitcast(f32))
                nc.gpsimd.tensor_copy(col3(ht_lo, t), k3(w_lo[b]).bitcast(f32)).then_inc(ht_ok, 1)

            def rsqrt_ln(t):
                pool.wait_ge(var_ok, t + 1)
                nc.gpsimd.tensor_tensor(ln_rstd[:, :], var_eps[:, :], neg_half[:, :], ALU.pow).then_inc(lnr_ok, 1)

            def vn_low(t):
                pool.wait_ge(vnh_ok, t + 1)
                nc.gpsimd.tensor_tensor(vn_lo[:, :], buf_a[:, :], vn_hi[:, :].bitcast(f32), ALU.subtract).then_inc(vnl_ok, 1)

            nc.gpsimd.memset(neg_half[:, :], -0.5).then_inc(pool_own, 1)
            nc.gpsimd.memset(ident[:, :], 0.0).then_inc(pool_own, 1)
            pool.wait_ge(pool_own, 2)
            nc.gpsimd.affine_select(out=ident[:, :], in_=ident[:, :], compare_op=ALU.not_equal, fill=1.0, base=0,
                                    pattern=[[-1, P]], channel_multiplier=1).then_inc(const_ok, 1)
            rsqrt_h(0, 0)
            split_lo_to(0, 0, tile(g_lo, 0), tile(g_hi, 0))
            pool.wait_ge(wsp_in, 16)
            nc.gpsimd.affine_select(out=buf_b[:, :].rearrange("p (g s) -> p g s", g=KT),
                                    in_=buf_b[:, :].rearrange("p (g s) -> p g s", g=KT), compare_op=ALU.is_ge, fill=0.0,
                                    base=0, pattern=[[0, KT], [-1, P]], channel_multiplier=1).then_inc(wsp_ok, 1)
            for k in range(1, KT):
                split_lo_to(k, k % 2, tile(g_lo, k), tile(g_hi, k))
                if k == 3:
                    rsqrt_h(1, 1)
            copy_h(0, 0)
            rsqrt_ln(0)
            copy_h(1, 1)
            vn_low(0)
            with pool.Fori(0, NT // 2 - 1) as i:
                for b in (1, 0):
                    t = 2 * i + 2 - b
                    rsqrt_h(t + 1, 1 - b)
                    rsqrt_ln(t)
                    copy_h(t + 1, 1 - b)
                    pool.wait_ge(mix_done, t)
                    vn_low(t)
            split_lo(N_U, 0)
            rsqrt_ln(NT - 1)
            pool.wait_ge(mix_done, NT - 1)
            vn_low(NT - 1)
            split_lo(N_U + 1, 1)
            pool.wait_ge(rel_in, 16)
            nc.gpsimd.memset(bias_row[:, :], NEG_INF / HEAD_DIM ** -0.5).then_inc(pool_own, 1)
            pool.wait_ge(pool_own, 3)
            for bucket, d0, d1 in bucket_runs():
                last = nc.gpsimd.tensor_scalar(bias_row[:, 2 * P - d1:2 * P - d0],
                                               rel_t[:, bucket:bucket + 1].to_broadcast([N_HEADS, d1 - d0]),
                                               1.0 / HEAD_DIM ** -0.5, 1.0, ALU.mult, ALU.mult)
            last.then_inc(bias_made, 1)
            with pool.Fori(N_U // 2, N_ATT // 2 - 1) as h:
                for b in range(2):
                    split_lo(2 * h + 2 + b, b)
            split_lo(N_ATT, 0)
            split_lo(N_ATT + 1, 1)

            def pair(p, i, c, r):
                n0 = c + 6 * i
                split_lo(n0 + 2, r)
                for k in range(8):
                    s = 8 * p + k
                    lo = P if k == 0 else 0
                    pool.wait_ge(inv_ok, s + 1)
                    stand_alone(pool)
                    for h in range(2):
                        w = prob[k % 3][:, h * 256 + lo:(h + 1) * 256]
                        last = nc.gpsimd.tensor_scalar(w, w, inv_den[:, 2 * k + h:2 * k + h + 1], 0.5, ALU.mult, ALU.mult)
                    last.then_inc(prob_ok, 1)
                    if k == 4:
                        split_lo(n0 + 3, 1 - r)
                pool.wait_ge(acc_free[r], half(c + 2, i, 6) + 1)
                stand_alone(pool)
                nc.gpsimd.tensor_scalar(buf_t[:, :], buf_t[:, :], 0.5, 0.5, ALU.mult, ALU.add).then_inc(siga_ok, 1)
                split_lo(n0 + 4, r)
                pool.wait_ge(oadd_ok, 4 * p + 4)
                nc.gpsimd.tensor_tensor(buf_b[:, :], buf_b[:, :], buf_a[:, :], ALU.mult).then_inc(og_ok, 1)
                pool.wait_ge(ghi_ok, KT + p + 1)
                nc.gpsimd.tensor_tensor(tile(g_lo, p), buf_b[:, :], tile(g_hi, p).bitcast(f32), ALU.subtract).then_inc(g_ready, 1)

            with pool.Fori(0, PAIRS // 2) as i:
                for r in range(2):
                    pair(2 * i + r, i, N_ATT + 3 * r, r)
            with pool.Fori(0, KT // 2 - 1) as i:
                for b in range(2):
                    split_lo(N_YA + 2 + b + 2 * i, b)

            def split_out(s):
                r = N_OUT + s
                if s < 4:
                    split_lo_to(r, r % 2, tile(wo_lo, s), tile(wo_hi, s))
                else:
                    split_lo_to(r, r % 2, tile(g_hi, s), tile(g_hi, s - 4))

            for s in range(4):
                split_out(s)

            def tile_lo(t, b):
                pool.wait_ge(unit_done, N_OUT + t - 1)
                stand_alone(pool)
                nc.gpsimd.tensor_copy(k3(w_lo[b]), ht_lo[:, :].bitcast(f32).rearrange(
                    "p (k s) -> p k s", k=KT)[:, :, bass.ds(t * P, P)]).then_inc(mt_lo, 1)

            def rsqrt_out(t, b):
                pool.wait_ge(oms_ok, t + 1)
                nc.gpsimd.tensor_tensor(rstd[:, b:b + 1], msq[:, b:b + 1], neg_half[:, :], ALU.pow).then_inc(ors_ok, 1)

            pool.wait_ge(g_ready, 3 * KT)
            tile_lo(0, 0)
            for s in range(4, 8):
                split_out(s)
            tile_lo(1, 1)
            with pool.Fori(0, NT // 2 - 1) as i:
                for b in range(2):
                    rsqrt_out(2 * i + b, b)
                    tile_lo(2 * i + b + 2, b)
            rsqrt_out(NT - 2, 0)
            rsqrt_out(NT - 1, 1)

        @block.vector
        def _(dve):
            own = Chain(dve, dve_own)

            def mean_sq(t, b):
                dve.wait_ge(ssq_ok, t + 1)
                nc.vector.tensor_scalar(msq[:, b:b + 1], ssq[:, b:b + 1], 1.0 / D_MODEL, EPS, ALU.mult, ALU.add).then_inc(msq_ok, 1)

            def norm_h(t, b):
                dve.wait_ge(rstd_ok, t + 1)
                nc.vector.scalar_tensor_tensor(out=x_b[b][:, :], in0=x_b[b][:, :], scalar=rstd[:, b:b + 1],
                                               in1=pre_b[:, :], op0=ALU.mult, op1=ALU.mult).then_inc(h_ok, 1)

            def h_lo(t, b):
                dve.wait_ge(hs_hi, t + 1)
                nc.vector.tensor_tensor(w_lo[b][:, :], ps_t[:, :], w_hi[b][:, :].bitcast(f32), ALU.subtract).then_inc(hs_lo, 1)

            def mix_read(t, ht, b):
                dve.wait_ge(mix_done, t + 1)
                dve.wait_ge(mix_out[b], 16 * (ht + 1))
                nc.vector.tensor_tensor(mix_b[b][:, :], ps_m[:, :], bs_b[:, :], ALU.add).then_inc(mix_ok, 1)

            def layer_norm(t, b):
                dve.wait_ge(acc_free[b], (t // 2 if isinstance(t, int) else t[1]) + 1)
                t = t if isinstance(t, int) else t[0]
                for hf in range(2):
                    last = nc.vector.bn_stats(bn6[:, 6 * hf:6 * hf + 6], buf_a[:, hf * HALF:(hf + 1) * HALF])
                own.link(last)
                stand_alone(dve)
                own.link(nc.vector.bn_aggr(mean_var[:, :], bn6[:, :].rearrange("p (a s) -> p a s", s=6)))
                nc.vector.tensor_scalar(var_eps[:, :], mean_var[:, 1:2], EPS, None, ALU.add).then_inc(var_ok, 1)
                dve.wait_ge(lnr_ok, t + 1)
                own.link(nc.vector.tensor_scalar(buf_a[:, :], buf_a[:, :], mean_var[:, 0:1], ln_rstd[:, 0:1],
                                                 ALU.subtract, ALU.mult))
                own.link(nc.vector.tensor_tensor(buf_a[:, :], buf_a[:, :], lng_b[:, :], ALU.mult))
                nc.vector.tensor_tensor(buf_a[:, :], buf_a[:, :], lnb_b[:, :], ALU.add).then_inc(vn_ok, 1)

            LN_LINKS = 4
            mean_sq(0, 0)
            dve.wait_ge(pre_in, 16)
            norm_h(0, 0)
            h_lo(0, 0)
            dve.wait_ge(wsh_ok, 1)
            nc.vector.tensor_tensor(ws_lo[:, :], ps_t[:, :], ws_hi[:, :].bitcast(f32), ALU.subtract).then_inc(wsl_ok, 1)
            mean_sq(1, 1)
            norm_h(1, 1)
            h_lo(1, 1)
            dve.wait_ge(ln_in, 32)
            dve.wait_ge(bs_in, 16)
            layer_norm(0, 0)
            with dve.Fori(0, NT // 2 - 1) as i:
                own.at(LN_LINKS + 2 * LN_LINKS * i)
                for b in (1, 0):
                    t = 2 * i + 2 - b
                    mean_sq(t + 1, 1 - b)
                    norm_h(t + 1, 1 - b)
                    h_lo(t + 1, 1 - b)
                    if b == 1:
                        mix_read(t - 1, i, 0)
                        layer_norm((t, i), 1)
                    else:
                        mix_read(t - 1, i, 1)
                        layer_norm((t, i + 1), 0)
            own.at(LN_LINKS * (NT - 1))
            mix_read(NT - 2, NT // 2 - 1, 0)
            layer_norm(NT - 1, 1)
            mix_read(NT - 1, NT // 2 - 1, 1)

            with dve.Fori(0, KT) as g:
                dve.wait_ge(acc_free[0], half(N_U + 2, g, 2))
                dve.wait_ge(mix_in, 16 * (g + 1))
                nc.vector.tensor_tensor(buf_a[:, :], buf_a[:, :], buf_b[:, :], ALU.mult).then_inc(um_ok, 1)
                dve.wait_ge(gate_t_ok, g + 1)
                nc.vector.scalar_tensor_tensor(out=buf_t[:, :], in0=buf_t[:, :], scalar=1.0, in1=acc[1][:, :],
                                               op0=ALU.add, op1=ALU.mult).then_inc(acc_free[1], 1)
                dve.wait_ge(um_ok, g + 1)
                dve.wait_ge(acc_free[1], half(N_U + 2, g, 2))
                nc.vector.scalar_tensor_tensor(out=buf_t[:, :], in0=buf_t[:, :], scalar=0.5, in1=buf_a[:, :],
                                               op0=ALU.mult, op1=ALU.mult).then_inc(prod_ok, 1)
                dve.wait_ge(prod_ok, g + 1)
                dve.wait_ge(ghi_ok, g + 1)
                nc.vector.tensor_tensor(tile(g_lo, g), buf_t[:, :], tile(g_hi, g).bitcast(f32), ALU.subtract).then_inc(g_ready, 1)
            base = own.base + own.k
            with dve.Fori(0, KT) as j:
                own.at(base + j)
                dve.wait_ge(acc_free[0], half(N_MB + 2, j, 2))
                own.link(nc.vector.tensor_scalar(buf_t[:, :], buf_t[:, :], 0.5, 0.5, ALU.mult, ALU.add))
                dve.wait_ge(unit_done, N_MB + 2 + 2 * j)
                dve.wait_ge(spill_out, 16 * (j + 1))
                nc.vector.tensor_tensor(buf_a[:, :], acc[1][:, :], buf_t[:, :], ALU.mult).then_inc(acc_free[1], 1)
            base = base + KT
            dve.wait_ge(khi_ok, 1)
            for kv in range(N_KV):
                rows = slice(kv * HEAD_DIM, (kv + 1) * HEAD_DIM)
                cols = slice(kv * SEQ, (kv + 1) * SEQ)
                for hf in range(2):
                    last = nc.vector.tensor_tensor(k_lo[hf * HEAD_DIM:(hf + 1) * HEAD_DIM, cols], buf_a[rows, :],
                                                   k_hi[rows, cols].bitcast(f32), ALU.subtract)
            last.then_inc(klo_ok, 1)
            dve.wait_ge(vhi_ok, 1)
            v5 = v_st[:, :].rearrange("p (v t x d) -> p v t x d", v=N_KV, t=NT, x=2)
            v5f = v_st[:, :].bitcast(f32).rearrange("p (v t x d) -> p v t x d", v=N_KV, t=NT, x=2)
            for kv in range(N_KV):
                last = nc.vector.tensor_tensor(
                    v5[:, kv, :, 1, :], ps_m[:, :].rearrange("p (t v d) -> p t v d", t=NT, v=N_KV)[:, :, kv, :],
                    v5f[:, kv, :, 0, :], ALU.subtract)
            last.then_inc(scores_used, 1)
            dve.wait_ge(sink_in, 16)

            def pair(p, i, c, r):
                dve.wait_ge(q_hi_ok, p + 1)
                nc.vector.tensor_tensor(q_st[0][64:128, :], acc[r][0:64, :], q_st[0][0:64, :].bitcast(f32), ALU.subtract)
                nc.vector.tensor_tensor(q_st[1][0:64, :], acc[r][64:128, :], q_st[1][64:128, :].bitcast(f32),
                                        ALU.subtract).then_inc(acc_free[r], 1)
                own.link(nc.vector.tensor_copy(sink_p[:, :], sink_b[:, bass.ds(2 * p, 2)]))
                dve.wait_ge(bias_in, 16 * (p + 1))
                for k in range(12):
                    if k < 8:
                        lo = P if k == 0 else 0
                        c2 = slice(2 * k, 2 * k + 2)
                        dve.wait_ge(scores_ok, 8 * p + k + 1)
                        stand_alone(dve)
                        for h in range(2):
                            cs = slice(h * 256 + lo, (h + 1) * 256)
                            last = nc.vector.tensor_tensor_reduce(
                                out=prob[k % 3][:, cs], in0=ps_s[:, cs], in1=bias_t[:, cs], scale=HEAD_DIM ** -0.5,
                                scalar=sink_p[:, h:h + 1], op0=ALU.add, op1=ALU.max,
                                accum_out=row_max[:, 2 * k + h:2 * k + h + 1])
                        last.then_inc(scores_used, 1)
                        dve.wait_ge(scores_used, 8 * p + k + 2)
                        nc.vector.tensor_scalar(neg_max[:, c2], row_max[:, c2], -1.0, None, ALU.mult)
                        nc.vector.tensor_tensor(sink_d[:, c2], sink_p[:, :], row_max[:, c2],
                                                ALU.subtract).then_inc(max_ok, 1)
                    if 1 <= k < 9:
                        m2 = slice(2 * k - 2, 2 * k)
                        dve.wait_ge(exp_ok, 8 * p + k)
                        own.link(nc.vector.tensor_tensor(denom[:, m2], row_sum[:, m2], sink_e[:, m2], ALU.add))
                        nc.vector.reciprocal(inv_den[:, m2], denom[:, m2]).then_inc(inv_ok, 1)
                    if 2 <= k < 10:
                        dve.wait_ge(pth_ok, 8 * p + k - 1)
                        if k == 2:
                            v = lambda t: t.rearrange("p (h c) -> p h c", h=2)[:, :, P:256]
                            last = nc.vector.tensor_tensor(v(pt_lo[:, :]), v(ps_p), v(pt_hi[:, :].bitcast(f32)), ALU.subtract)
                        else:
                            last = nc.vector.tensor_tensor(pt_lo[:, :], ps_p, pt_hi[:, :].bitcast(f32), ALU.subtract)
                        last.then_inc(ptl_ok, 1)
                    if k >= 5 and k % 2:
                        g = (k - 5) // 2
                        if g == 0:
                            dve.wait_ge(g_ready, KT + p)
                        dve.wait_ge(otmp_ok, 4 * p + g + 1)
                        o = ps_m[:, (g % 2) * 512:(g % 2 + 1) * 512]
                        cols = slice(g * 256, (g + 1) * 256)
                        nc.vector.tensor_tensor(buf_b[0:64, cols], o[0:64, 0:256], o_tmp[g % 2][0:64, :], ALU.add)
                        nc.vector.tensor_tensor(buf_b[64:128, cols], o[64:128, 256:512], o_tmp[g % 2][64:128, :],
                                                ALU.add).then_inc(oadd_ok, 1)
                    if k == 5:
                        dve.wait_ge(gtan_ok, p + 1)
                        nc.vector.scalar_tensor_tensor(out=buf_a[:, :], in0=buf_t[:, :], scalar=1.0, in1=acc[1 - r][:, :],
                                                       op0=ALU.add, op1=ALU.mult).then_inc(acc_free[1 - r], 1)

            with dve.Fori(0, PAIRS // 2) as i:
                own.at(base + 2 * (NT + 1) * i)
                for r in range(2):
                    pair(2 * i + r, i, N_ATT + 3 * r, r)
            dve.wait_ge(g_ready, 2 * KT)
            with dve.Fori(0, KT // 2) as i:
                for b in range(2):
                    j = 2 * i + b
                    dve.wait_ge(unit_done, N_YA + 1 + b + 2 * i)
                    dve.wait_ge(sigr_in, 16 * (j + 1))
                    nc.vector.tensor_tensor(buf_b[:, :], acc[b][:, :], buf_t[:, :], ALU.mult).then_inc(acc_free[b], 1)
                    dve.wait_ge(acc_free[b], half(N_YA + 2, i, 2))
                    dve.wait_ge(accr_in, 16 * (j + 1))
                    nc.vector.tensor_tensor(buf_b[:, :], buf_b[:, :], buf_a[:, :], ALU.add).then_inc(mrg_ok, 1)
                    dve.wait_ge(mhi_ok, j + 1)
                    nc.vector.tensor_tensor(tile(ht_lo, j), buf_b[:, :], tile(ht_hi, j).bitcast(f32), ALU.subtract).then_inc(g_ready, 1)

            dve.wait_ge(post_in, 16)

            def out_tile(t, b, ht, first):
                y = (buf_a, buf_b)[b]
                dve.wait_ge(osq_ok, t + 1)
                nc.vector.tensor_scalar(msq[:, b:b + 1], ssq[:, b:b + 1], 1.0 / D_MODEL, EPS, ALU.mult, ALU.add).then_inc(oms_ok, 1)
                if not first:
                    dve.wait_ge(y_out[b], 16 * ht)
                dve.wait_ge(ors_ok, t + 1)
                nc.vector.scalar_tensor_tensor(out=y[:, :], in0=acc[b][:, :], scalar=rstd[:, b:b + 1], in1=buf_t[:, :],
                                               op0=ALU.mult, op1=ALU.mult).then_inc(acc_free[b], 1)
                dve.wait_ge(acc_free[b], N_OUT // 2 + 1 + ht)
                dve.wait_ge(xr_in[b], 16 * (ht + 1))
                nc.vector.tensor_tensor(y[:, :], y[:, :], x_r[b][:, :], ALU.add).then_inc(y_ok, 1)

            out_tile(0, 0, 0, True)
            out_tile(1, 1, 0, True)
            with dve.Fori(1, NT // 2) as i:
                for b in range(2):
                    out_tile(2 * i + b, b, i, False)


INPUTS = ("x", "rel_bias", "pre_norm", "post_norm", "w_in", "sinks", "sgu_ln_g", "sgu_ln_b", "w_spatial",
          "b_spatial", "w_branch_a", "w_branch_b", "w_out")


def kernel(**inputs):
    import concourse.bacc as bacc
    from concourse.bass_utils import run_bass_kernel_spmd

    nc = bacc.Bacc("TRN2", target_bir_lowering=False, num_devices=1, dynamic_dma_scratch_size=1024)
    arrays, args = {}, []
    for name in INPUTS:
        a = np.ascontiguousarray(inputs[name])
        arrays["in_" + name] = a
        args.append(nc.dram_tensor("in_" + name, a.shape, mybir.dt.from_np(a.dtype), kind="ExternalInput").ap())
    args.append(nc.dram_tensor("out", inputs["x"].shape, mybir.dt.float32, kind="ExternalOutput").ap())
    build(nc, *args)
    r = run_bass_kernel_spmd(nc, [arrays], core_ids=[0])
    return r.results[0]["out"]
```

```python
import numpy as np
import concourse.bass as bass
from concourse import mybir
from contextlib import ExitStack

P = 128
D_MODEL = 1024
SEQ = 1024
HEAD_DIM = 64
N_HEADS = D_MODEL // HEAD_DIM
N_KV = 2
KT = D_MODEL // P
NT = SEQ // P
HALF = 512
N_BUCKETS = 32
MAX_DISTANCE = 128
WINDOW = 128
EPS = 1e-6
NEG_INF = -1e30
PAIRS = N_HEADS // 2
PAIRS_PER_KV = PAIRS // N_KV

Q_COL = 0
K_COL = Q_COL + D_MODEL
V_COL = K_COL + N_KV * HEAD_DIM
GA_COL = V_COL + N_KV * HEAD_DIM
U_COL = GA_COL + D_MODEL
VB_COL = U_COL + D_MODEL
GB_COL = VB_COL + D_MODEL
MGA_COL = GB_COL + D_MODEL
MGB_COL = MGA_COL + D_MODEL

N_U = NT
N_MB = N_U + 2 * KT
N_KVU = N_MB + 2 * KT
N_ATT = N_KVU + 2
N_YA = N_ATT + 3 * PAIRS
N_OUT = N_YA + KT
BIAS_ROW = 3 * P


def bucket_runs():
    dist = np.arange(WINDOW)
    exact = N_BUCKETS // 2
    large = exact + (np.log(np.maximum(dist, exact) / exact)
                     / np.log(MAX_DISTANCE / exact) * (N_BUCKETS - exact)).astype(np.int32)
    bucket = np.where(dist < exact, dist, np.minimum(large, N_BUCKETS - 1))
    return [(int(b), int(np.argmax(bucket == b)), int(np.sum(bucket <= b))) for b in np.unique(bucket)]


class Chain:

    def __init__(self, eng, sem):
        self.eng, self.sem, self.base, self.k = eng, sem, 0, 0

    def link(self, ins):
        self.k += 1
        ins.then_inc(self.sem, 1)
        self.eng.wait_ge(self.sem, self.base + self.k)

    def at(self, base):
        self.base, self.k = base, 0


def build(nc, x, rel_bias, pre_norm, post_norm, w_in, sinks, sgu_ln_g, sgu_ln_b,
          w_spatial, b_spatial, w_branch_a, w_branch_b, w_out, out):
    f32 = mybir.dt.float32
    f32r = mybir.dt.float32r
    bf16 = mybir.dt.bfloat16
    ACT = mybir.ActivationFunctionType
    ALU = mybir.AluOpType

    w_in_t = w_in[0].rearrange("(k p) c -> p k c", p=P)
    w_a_t = w_branch_a[0].rearrange("(k p) c -> p k c", p=P)
    w_b_t = w_branch_b[0].rearrange("(k p) c -> p k c", p=P)
    w_out_t = w_out[0].rearrange("(k p) c -> p k c", p=P)

    mix_d = nc.dram_tensor("mix_d", [KT, P, SEQ], f32)
    acc_d = nc.dram_tensor("acc_d", [KT, P, SEQ], f32)
    sig_d = nc.dram_tensor("sig_d", [KT, P, SEQ], f32)
    bias_d = nc.dram_tensor("bias_d", [N_HEADS, BIAS_ROW], f32)
    skew_d = nc.dram_tensor("skew_d", [N_HEADS, P, BIAS_ROW], f32)

    with ExitStack() as ctx:
        def sb(name, shape, dt=f32, scope=ctx):
            return scope.enter_context(nc.sbuf_tensor(name, shape, dt))

        def sem(name):
            return ctx.enter_context(nc.semaphore(name))

        ht_hi = sb("ht_hi", [P, KT * SEQ], f32r)
        ht_lo = sb("ht_lo", [P, KT * SEQ], f32r)
        g_hi = sb("g_hi", [P, KT * SEQ], f32r)
        g_lo = sb("g_lo", [P, KT * SEQ], f32r)
        raw = [sb(f"raw{b}", [P, 1024]) for b in range(2)]
        w_hi = [sb(f"w_hi{b}", [P, 1024], f32r) for b in range(2)]
        w_lo = [sb(f"w_lo{b}", [P, 1024], f32r) for b in range(2)]
        buf_t = sb("buf_t", [P, SEQ])
        buf_a = sb("buf_a", [P, SEQ])
        buf_b = sb("buf_b", [P, SEQ])
        junk = sb("junk", [P, SEQ], bf16)
        ident = sb("ident", [P, P])
        neg_half = sb("neg_half", [P, 1])
        ssq = sb("ssq", [P, 2])
        msq = sb("msq", [P, 2])
        rstd = sb("rstd", [P, 2])
        bn6 = sb("bn6", [P, 12])
        mean_var = sb("mean_var", [P, 2])
        var_eps = sb("var_eps", [P, 1])
        ln_rstd = sb("ln_rstd", [P, 1])
        sink_b = sb("sink_b", [P, N_HEADS])
        sink_p = sb("sink_p", [P, 2])
        row_max = sb("row_max", [P, 2 * NT])
        neg_max = sb("neg_max", [P, 2 * NT])
        sink_d = sb("sink_d", [P, 2 * NT])
        row_sum = sb("row_sum", [P, 2 * NT])
        sink_e = sb("sink_e", [P, 2 * NT])
        denom = sb("denom", [P, 2 * NT])
        inv_den = sb("inv_den", [P, 2 * NT])
        rel_t = sb("rel_t", [N_HEADS, N_BUCKETS])
        bias_row = sb("bias_row", [N_HEADS, BIAS_ROW])

        with ExitStack() as s0:
            x_b = [sb(f"x_b{b}", [P, D_MODEL], f32, s0) for b in range(2)]
            pre_b = sb("pre_b", [P, D_MODEL], f32, s0)
            lng_b = sb("lng_b", [P, D_MODEL], f32, s0)
            lnb_b = sb("lnb_b", [P, D_MODEL], f32, s0)
            bs_b = sb("bs_b", [P, KT * P], f32, s0)
            mix_b = [sb(f"mix_b{b}", [P, KT * P], f32, s0) for b in range(2)]
            vn_hi = sb("vn_hi", [P, D_MODEL], f32r, s0)
            vn_lo = sb("vn_lo", [P, D_MODEL], f32r, s0)
            ws_hi = sb("ws_hi", [P, KT * P], f32r, s0)
            ws_lo = sb("ws_lo", [P, KT * P], f32r, s0)
        with ExitStack() as s1:
            k_hi = sb("k_hi", [P, N_KV * SEQ], f32r, s1)
            k_lo = sb("k_lo", [P, N_KV * SEQ], f32r, s1)
            v_st = sb("v_st", [P, N_KV * NT * P], f32r, s1)
            q_st = [sb(f"q_st{h}", [P, SEQ], f32r, s1) for h in range(2)]
            pt_hi = sb("pt_hi", [P, 512], f32r, s1)
            pt_lo = sb("pt_lo", [P, 512], f32r, s1)
            prob = [sb(f"prob{b}", [P, 512], f32, s1) for b in range(3)]
            bias_t = sb("bias_t", [P, 512], f32, s1)
            o_tmp = [sb(f"o_tmp{b}", [P, 256], f32, s1) for b in range(2)]
        with ExitStack() as s2:
            wo_hi = sb("wo_hi", [P, KT * HALF], f32r, s2)
            wo_lo = sb("wo_lo", [P, KT * HALF], f32r, s2)
            x_r = [sb(f"x_r{b}", [P, D_MODEL], f32, s2) for b in range(2)]

        acc = [ctx.enter_context(nc.psum_tensor(f"acc{b}", [P, 1024], f32)) for b in range(2)]
        ps_t = ctx.enter_context(nc.psum_tensor("ps_t", [P, 1024], f32))
        ps_m = ctx.enter_context(nc.psum_tensor("ps_m", [P, 1024], f32))
        ps_s, ps_p = ps_t[:, 0:512], ps_t[:, 512:1024]

        raw_in = [sem(f"raw_in{b}") for b in range(2)]
        hi_done, lo_done = sem("hi_done"), sem("lo_done")
        unit_done = sem("unit_done")
        acc_free = [sem(f"acc_free{b}") for b in range(2)]
        x_in = [sem(f"x_in{b}") for b in range(2)]
        pre_in, ln_in, bs_in, wsp_in = sem("pre_in"), sem("ln_in"), sem("bs_in"), sem("wsp_in")
        rel_in, sink_in, bias_out, skew_out = sem("rel_in"), sem("sink_in"), sem("bias_out"), sem("skew_out")
        bias_made = sem("bias_made")
        const_ok, wsp_ok = sem("const_ok"), sem("wsp_ok")
        ssq_ok, msq_ok, rstd_ok, h_ok = sem("ssq_ok"), sem("msq_ok"), sem("rstd_ok"), sem("h_ok")
        tr_done = sem("tr_done")
        hs_hi, hs_lo = sem("hs_hi"), sem("hs_lo")
        ht_in = [sem(f"ht_in{b}") for b in range(2)]
        vb_in = [sem(f"vb_in{b}") for b in range(4)]
        wsh_ok, wsl_ok = sem("wsh_ok"), sem("wsl_ok")
        vg_ok, var_ok, lnr_ok, vn_ok = sem("vg_ok"), sem("var_ok"), sem("lnr_ok"), sem("vn_ok")
        vnh_ok, vnl_ok = sem("vnh_ok"), sem("vnl_ok")
        mix_done, mix_ok = sem("mix_done"), sem("mix_ok")
        mix_out = [sem(f"mix_out{b}") for b in range(2)]
        mix_in, gelu_ok, gate_t_ok, um_ok, prod_ok = sem("mix_in"), sem("gelu_ok"), sem("gate_t_ok"), sem("um_ok"), sem("prod_ok")
        ghi_ok, g_ready = sem("ghi_ok"), sem("g_ready")
        mtan_ok, acc_ok, spill_out = sem("mtan_ok"), sem("acc_ok"), sem("spill_out")
        kraw_ok, khi_ok, klo_ok = sem("kraw_ok"), sem("khi_ok"), sem("klo_ok")
        vraw_ok, vt_done, vhi_ok, vlo_ok = sem("vraw_ok"), sem("vt_done"), sem("vhi_ok"), sem("vlo_ok")
        bias_in = sem("bias_in")
        q_hi_ok, q_ok = sem("q_hi_ok"), sem("q_ok")
        scores_ok, scores_used, max_ok, exp_ok, inv_ok, prob_ok = (
            sem("scores_ok"), sem("scores_used"), sem("max_ok"), sem("exp_ok"), sem("inv_ok"), sem("prob_ok"))
        pt_done, pth_ok, ptl_ok, pv_done = sem("pt_done"), sem("pth_ok"), sem("ptl_ok"), sem("pv_done")
        otmp_ok, oadd_ok, gtan_ok, gate_ok, og_ok = (
            sem("otmp_ok"), sem("oadd_ok"), sem("gtan_ok"), sem("gate_ok"), sem("og_ok"))
        siga_ok = sem("siga_ok")
        sigr_in, accr_in, mrg_ok, mhi_ok = sem("sigr_in"), sem("accr_in"), sem("mrg_ok"), sem("mhi_ok")
        post_in, xr_in = sem("post_in"), [sem(f"xr_in{b}") for b in range(2)]
        mt_hi, mt_lo = sem("mt_hi"), sem("mt_lo")
        osq_ok, oms_ok, ors_ok, y_ok = sem("osq_ok"), sem("oms_ok"), sem("ors_ok"), sem("y_ok")
        y_out = [sem(f"y_out{b}") for b in range(2)]
        dve_own, pool_own, waited = sem("dve_own"), sem("pool_own"), sem("waited")

        block = ctx.enter_context(nc.Block())

        def stand_alone(eng):
            eng.sem_inc(waited, 1)

        def tile(buf, i, n=SEQ):
            return buf[:, bass.ds(i * n, n)]

        def col3(buf, i):
            return buf[:, :].rearrange("p (k s) -> p k s", k=KT)[:, :, bass.ds(i * P, P)]

        def k3(buf):
            return buf[:, :].rearrange("p (k s) -> p k s", k=KT)

        land = (raw[0], raw[1], buf_t, buf_a)

        def half(c, i=0, s=0):
            return c // 2 + (s // 2) * i if s else c // 2

        @block.sync
        def _(sp):
            def load_raw(n, b, src, col):
                sp.wait_ge(hi_done, n - 1)
                stand_alone(sp)
                sp.wait_ge(lo_done, n - 1)
                stand_alone(sp)
                sp.dma_start(raw[b][:, :].rearrange("p (k c) -> p k c", c=P),
                             src[:, :, bass.ds(col, P)]).then_inc(raw_in[b], 16)

            def load_x(t, b):
                sp.dma_start(x_b[b][:, :], x[0, bass.ds(t * P, P), :]).then_inc(x_in[b], 16)

            def load_vb(k):
                if k >= 4:
                    sp.wait_ge(hi_done, k - 3)
                    sp.wait_ge(lo_done, k - 3)
                sp.dma_start(land[k % 4][:, :], w_in_t[:, k, VB_COL:VB_COL + D_MODEL]).then_inc(vb_in[k % 4], 16)

            def copy_h(t, b):
                sp.wait_ge(hs_lo, t + 1)
                stand_alone(sp)
                for src, dst in ((w_hi[b], ht_hi), (w_lo[b], ht_lo)):
                    sp.dma_start(col3(dst, t).bitcast(f32), k3(src).bitcast(f32)).then_inc(ht_in[b], 16)

            load_x(0, 0)
            load_vb(0)
            sp.dma_start(pre_b[:, :], pre_norm[0:1, :].to_broadcast([P, D_MODEL])).then_inc(pre_in, 16)
            load_vb(1)
            sp.dma_start(buf_b[:, :].rearrange("p (g s) -> p g s", g=KT),
                         w_spatial[0].rearrange("g t s -> t g s")).then_inc(wsp_in, 16)
            load_vb(2)
            load_vb(3)
            load_x(1, 1)
            for k in range(4, KT):
                load_vb(k)
            sp.dma_start(lng_b[:, :], sgu_ln_g[0:1, :].to_broadcast([P, D_MODEL])).then_inc(ln_in, 16)
            sp.dma_start(lnb_b[:, :], sgu_ln_b[0:1, :].to_broadcast([P, D_MODEL])).then_inc(ln_in, 16)
            sp.dma_start(bs_b[:, :], b_spatial.rearrange("a g t -> a (g t)").to_broadcast([P, KT * P])).then_inc(bs_in, 16)
            sp.dma_start(sink_b[:, :], sinks[0:1, :].to_broadcast([P, N_HEADS])).then_inc(sink_in, 16)
            sp.dma_start(rel_t[:, :], rel_bias.rearrange("b h -> h b"), allow_slow_non_contiguous=True).then_inc(rel_in, 16)

            def spill_mix(t, b):
                sp.wait_ge(mix_ok, t + 1)
                stand_alone(sp)
                sp.dma_start(mix_d[:, :, bass.ds(t * P, P)].rearrange("g p s -> p g s"),
                             mix_b[b][:, :].rearrange("p (g s) -> p g s", g=KT)).then_inc(mix_out[b], 16)

            def next_x(t, b):
                sp.wait_ge(tr_done, t)
                load_x(t, b)
                copy_h(t - 2, b)

            next_x(2, 0)
            next_x(3, 1)
            load_raw(N_U, 0, w_in_t, U_COL)
            load_raw(N_U + 1, 1, w_in_t, GB_COL)
            with sp.Fori(2, NT // 2) as i:
                for b in range(2):
                    next_x(2 * i + b, b)
                    spill_mix(2 * i + b - 4, b)
            for t in range(NT - 2, NT):
                copy_h(t, t % 2)
                spill_mix(t - 2, t % 2)
            spill_mix(NT - 2, 0)
            load_raw(N_U + 2, 0, w_in_t, U_COL + P)
            load_raw(N_U + 3, 1, w_in_t, GB_COL + P)
            spill_mix(NT - 1, 1)

            def load_mix(g):
                sp.dma_start(buf_b[:, :], mix_d[bass.ds(g, 1), :, :].rearrange("a p s -> p (a s)")).then_inc(mix_in, 16)

            for b in range(2):
                sp.wait_ge(mix_out[b], 16 * (1 + NT // 2))
            load_mix(0)
            sp.wait_ge(bias_made, 1)
            sp.dma_start(bias_d[:, :], bias_row[:, :]).then_inc(bias_out, 16)
            sp.wait_ge(bias_out, 16)
            sp.dma_start(skew_d[:, :, :], bass.AP(bias_d, 0, [[BIAS_ROW, N_HEADS], [0, P], [1, BIAS_ROW]])).then_inc(skew_out, 16)
            sp.wait_ge(um_ok, 1)
            load_mix(1)
            with sp.Fori(2, KT) as g:
                load_raw(N_U + 2 * g, 0, w_in_t, U_COL + g * P)
                load_raw(N_U + 2 * g + 1, 1, w_in_t, GB_COL + g * P)
                sp.wait_ge(um_ok, g)
                load_mix(g)
            with sp.Fori(0, KT) as j:
                load_raw(N_MB + 2 * j, 0, w_in_t, MGB_COL + j * P)
                load_raw(N_MB + 2 * j + 1, 1, w_b_t, j * P)
            load_raw(N_KVU, 0, w_in_t, K_COL)
            load_raw(N_KVU + 1, 1, w_in_t, V_COL)
            sp.wait_ge(skew_out, 16)
            sp.wait_ge(mix_done, NT)
            load_raw(N_ATT, 0, w_in_t, Q_COL)

            def load_pair(p, i, r, last):
                    n = N_ATT + 3 * r + 6 * i
                    load_raw(n + 1, 1 - r, w_in_t, GA_COL + p * P)
                    load_raw(n + 2, r, w_in_t, MGA_COL + p * P)
                    sp.wait_ge(scores_used, 8 * p + 1)
                    sp.dma_start(bias_t[:, :].rearrange("p (h j) -> p h j", h=2),
                                 bass.AP(skew_d, p * (2 * P * BIAS_ROW) + (P - 1),
                                         [[BIAS_ROW - 1, P], [P * BIAS_ROW, 2], [1, 2 * P]])).then_inc(bias_in, 16)
                    if not last:
                        load_raw(n + 3, 1 - r, w_in_t, Q_COL + (p + 1) * P)

            with sp.Fori(0, PAIRS // 2 - 1) as i:
                for r in range(2):
                    load_pair(2 * i + r, i, r, False)
            for r in range(2):
                load_pair(PAIRS - 2 + r, PAIRS // 2 - 1, r, r == 1)
            with sp.Fori(0, KT // 2) as i:
                for b in range(2):
                    load_raw(N_YA + b + 2 * i, b, w_a_t, (2 * i + b) * P)
            for s in range(8):
                r, hf, kk = N_OUT + s, s // 4, s % 4
                sp.wait_ge(hi_done, r - 1)
                sp.wait_ge(lo_done, r - 1)
                sp.dma_start(raw[r % 2][:, :].rearrange("p (k c) -> p k c", k=2),
                             w_out_t[:, 2 * kk:2 * kk + 2, hf * HALF:(hf + 1) * HALF]).then_inc(raw_in[r % 2], 16)
            sp.wait_ge(acc_free[1], N_OUT // 2)
            sp.dma_start(buf_t[:, :], post_norm[0:1, :].to_broadcast([P, D_MODEL])).then_inc(post_in, 16)

            def load_res(t, b):
                sp.dma_start(x_r[b][:, :], x[0, bass.ds(t * P, P), :]).then_inc(xr_in[b], 16)

            def store(t, b):
                sp.wait_ge(y_ok, t + 1)
                sp.dma_start(out[0, bass.ds(t * P, P), :], (buf_a, buf_b)[b][:, :]).then_inc(y_out[b], 16)

            load_res(0, 0)
            load_res(1, 1)
            with sp.Fori(0, NT // 2 - 1) as i:
                for b in range(2):
                    store(2 * i + b, b)
                    load_res(2 * i + b + 2, b)
            store(NT - 2, 0)
            store(NT - 1, 1)
            for b in range(2):
                sp.wait_ge(y_out[b], 16 * NT // 2)

        @block.tensor
        def _(pe):
            def products(b, lh, ll, rh, rl):
                ops = []
                for k in range(KT):
                    for l, r, kind in ((lh, rh, 0), (lh, rl, 1), (ll, rh, 2)):
                        for hf in range(2):
                            ops.append((acc[b][:, hf * HALF:(hf + 1) * HALF], l[:, k * P:(k + 1) * P],
                                        r[:, k * SEQ + hf * HALF:k * SEQ + (hf + 1) * HALF],
                                        k == 0 and kind == 0, k == KT - 1 and kind == 2))
                return ops

            def run(ops):
                last = None
                for o, l, r, a, z in ops:
                    last = nc.tensor.matmul(o, l, r, start=a, stop=z, skip_group_check=True)
                return last

            def start_unit(n, hn, b):
                pe.wait_ge(lo_done, n + 1)
                pe.wait_ge(acc_free[b], hn)

            def unit(n, hn, b, rh, rl):
                start_unit(n, hn, b)
                run(products(b, w_hi[b], w_lo[b], rh, rl)).then_inc(unit_done, 1)

            def transpose_h(t, b):
                pe.wait_ge(h_ok, t + 1)
                for k in range(KT):
                    last = nc.tensor.transpose(ps_t[:, k * P:(k + 1) * P], x_b[b][:, k * P:(k + 1) * P], ident[:, :])
                last.then_inc(tr_done, 1)

            def mix(t):
                pe.wait_ge(vnl_ok, t + 1)
                for g in range(KT):
                    c = slice(g * P, (g + 1) * P)
                    nc.tensor.matmul(ps_m[:, c], vn_hi[:, c], ws_hi[:, c], start=True, stop=False, skip_group_check=True)
                    nc.tensor.matmul(ps_m[:, c], vn_hi[:, c], ws_lo[:, c], start=False, stop=False, skip_group_check=True)
                    last = nc.tensor.matmul(ps_m[:, c], vn_lo[:, c], ws_hi[:, c], start=False, stop=True, skip_group_check=True)
                last.then_inc(mix_done, 1)

            def vb_unit(t, b, more=True):
                pe.wait_ge(hs_lo, t + 1)
                ops = products(b, w_hi[b], w_lo[b], g_hi, g_lo)
                if more:
                    run(ops[:20])
                    transpose_h(t + 1, 1 - b)
                    ops = ops[20:]
                run(ops).then_inc(unit_done, 1)

            pe.wait_ge(const_ok, 1)
            transpose_h(0, 0)
            pe.wait_ge(wsp_ok, 1)
            pe.wait_ge(hs_lo, 1)
            for g in range(KT):
                c = slice(g * P, (g + 1) * P)
                last = nc.tensor.transpose(ps_t[:, c], buf_b[:, c], ident[:, :])
            last.then_inc(tr_done, 1)
            ops = products(0, w_hi[0], w_lo[0], g_hi, g_lo)
            for k in range(KT):
                pe.wait_ge(lo_done, k + 1)
                last = run(ops[6 * k:6 * k + 6])
                if k == KT - 2:
                    pe.wait_ge(wsl_ok, 1)
                    transpose_h(1, 1)
            last.then_inc(unit_done, 1)
            with pe.Fori(0, NT // 2 - 1) as i:
                for b in (1, 0):
                    t = 2 * i + 2 - b
                    vb_unit(t, b)
                    mix(t - 1)
            vb_unit(NT - 1, 1, more=False)
            mix(NT - 2)
            for b in range(2):
                pe.wait_ge(ht_in[b], 16 * NT)
            unit(N_U, half(N_U), 0, ht_hi, ht_lo)
            mix(NT - 1)
            unit(N_U + 1, half(N_U), 1, ht_hi, ht_lo)
            with pe.Fori(1, KT) as g:
                for b in range(2):
                    unit(N_U + b + 2 * g, half(N_U, g, 2), b, ht_hi, ht_lo)
            with pe.Fori(0, KT) as j:
                unit(N_MB + 2 * j, half(N_MB, j, 2), 0, ht_hi, ht_lo)
                pe.wait_ge(g_ready, KT)
                unit(N_MB + 1 + 2 * j, half(N_MB, j, 2), 1, g_hi, g_lo)
            unit(N_KVU, half(N_KVU), 0, ht_hi, ht_lo)
            unit(N_KVU + 1, half(N_KVU), 1, ht_hi, ht_lo)
            unit(N_ATT, half(N_ATT), 0, ht_hi, ht_lo)
            pe.wait_ge(acc_free[1], half(N_KVU) + 1)
            pe.wait_ge(mix_ok, NT)
            for t in range(NT):
                last = nc.tensor.transpose(ps_m[:, t * P:(t + 1) * P], buf_b[:, t * P:(t + 1) * P], ident[:, :])
            last.then_inc(vt_done, 1)

            def pair(kv, p, i, c, r, final=False):
                q_rows = half(c, i, 6) + 1

                def scores(blk):
                    s = 8 * p + blk
                    if blk == 0:
                        pe.wait_ge(acc_free[r], q_rows)
                    pe.wait_ge(scores_used, s + 1)
                    lo = P if blk == 0 else 0
                    kc = kv * SEQ + (blk - 1) * P
                    for h in range(2):
                        for kbuf, a in ((k_hi, True), (k_lo, False)):
                            last = nc.tensor.matmul(ps_s[:, h * 256 + lo:(h + 1) * 256], q_st[h][:, blk * P:(blk + 1) * P],
                                                    kbuf[:, kc + lo:kc + 256], start=a, stop=not a, skip_group_check=True)
                    last.then_inc(scores_ok, 1)

                def transpose_p(blk):
                    s = 8 * p + blk
                    pe.wait_ge(prob_ok, s + 1)
                    if blk > 0:
                        pe.wait_ge(ptl_ok, s)
                    for h in range(2):
                        for kb in ((1,) if blk == 0 else (0, 1)):
                            c0 = (2 * h + kb) * P
                            last = nc.tensor.transpose(ps_p[:, c0:c0 + P], prob[blk % 3][:, c0:c0 + P], ident[:, :])
                    last.then_inc(pt_done, 1)

                def values(blk):
                    s = 8 * p + blk
                    pe.wait_ge(ptl_ok, s + 1)
                    if blk in (4, 6):
                        pe.wait_ge(oadd_ok, 4 * p + blk // 2 - 1)
                    heads = lambda t, c0: t.rearrange("p (h c) -> p h c", h=2)[:, :, c0:c0 + P]
                    o = heads(ps_m[:, (blk // 2 % 2) * 512:(blk // 2 % 2 + 1) * 512], (blk % 2) * P)
                    kbs = (1,) if blk == 0 else (0, 1)
                    for kb in kbs:
                        v0 = (kv * NT + blk - 1 + kb) * P
                        for pt in (pt_hi, pt_lo):
                            last = nc.tensor.matmul(o, v_st[:, v0:v0 + P], heads(pt[:, :], kb * P),
                                                    start=(kb == kbs[0] and pt is pt_hi),
                                                    stop=(kb == 1 and pt is pt_lo), skip_group_check=True)
                    if blk % 2:
                        last.then_inc(pv_done, 1)

                n0 = c + 6 * i

                def start_ya(j):
                    start_unit(N_YA + j, half(N_YA), j)
                    if j == 0:
                        pe.wait_ge(g_ready, 2 * KT - 1)

                ops_a = products(1 - r, w_hi[1 - r], w_lo[1 - r], ht_hi, ht_lo)
                ops_m = products(r, w_hi[r], w_lo[r], ht_hi, ht_lo)
                beside = [(lambda: start_unit(n0 + 1, half(c + 1, i, 6), 1 - r), ops_a, True),
                          (lambda: start_unit(n0 + 2, half(c + 2, i, 6), r), ops_m, True)]
                if final:
                    ya = [products(j, w_hi[j], w_lo[j], g_hi, g_lo) for j in range(2)]
                    beside += [(lambda: start_ya(0), ya[0][:-6], False), (lambda: start_ya(1), ya[1][:-6], False)]
                else:
                    beside.append((lambda: start_unit(n0 + 3, half(c + 3, i, 6), 1 - r), ops_a, True))
                at = [18 + 12 * k for k in range(11)]
                m = 0
                for start, ops, ends in beside:
                    start()
                    for n, op in enumerate(ops):
                        if m in at:
                            k = at.index(m)
                            if 3 <= k:
                                values(k - 3)
                            if 2 <= k < 10:
                                transpose_p(k - 2)
                            if k < 8:
                                scores(k)
                        last = run([op])
                        m += 1
                    if ends:
                        last.then_inc(unit_done, 1)
                if final:
                    pe.wait_ge(g_ready, 2 * KT)
                    for j in range(2):
                        run(ya[j][-6:]).then_inc(unit_done, 1)

            pe.wait_ge(klo_ok, 1)
            with pe.Fori(0, PAIRS_PER_KV // 2) as i:
                for r in range(2):
                    pair(0, 2 * i + r, i, N_ATT + 3 * r, r)
            with pe.Fori(PAIRS_PER_KV // 2, PAIRS // 2 - 1) as i:
                for r in range(2):
                    pair(1, 2 * i + r, i, N_ATT + 3 * r, r)
            for r in range(2):
                pair(1, PAIRS - 2 + r, PAIRS // 2 - 1, N_ATT + 3 * r, r, final=(r == 1))
            with pe.Fori(1, KT // 2) as i:
                for b in range(2):
                    unit(N_YA + b + 2 * i, half(N_YA, i, 2), b, g_hi, g_lo)

            def out_half(t, b, hf, first=False):
                rh, rl = ((wo_hi, wo_lo) if hf == 0 else (g_hi[:, 0:KT * HALF], g_hi[:, KT * HALF:2 * KT * HALF]))
                for k in range(KT):
                    if first and k % 2 == 0:
                        pe.wait_ge(lo_done, N_OUT + 4 * hf + k // 2 + 1)
                    if first and hf == 0 and k == KT - 1:
                        pe.wait_ge(mt_hi, 2)
                        pe.wait_ge(mt_lo, 2)
                    for l, r, kind in ((w_hi[b], rh, 0), (w_hi[b], rl, 1), (w_lo[b], rh, 2)):
                        last = nc.tensor.matmul(acc[b][:, hf * HALF:(hf + 1) * HALF], l[:, k * P:(k + 1) * P],
                                                r[:, k * HALF:(k + 1) * HALF], start=(k == 0 and kind == 0),
                                                stop=(k == KT - 1 and kind == 2), skip_group_check=True)
                return last

            def out_start(t, i, b):
                pe.wait_ge(mt_hi, t + 2)
                pe.wait_ge(mt_lo, t + 2)
                pe.wait_ge(acc_free[b], half(N_OUT, i, 2))

            pe.wait_ge(mt_hi, 1)
            pe.wait_ge(mt_lo, 1)
            pe.wait_ge(acc_free[0], half(N_OUT))
            out_half(0, 0, 0, True)
            out_start(1, 0, 1)
            out_half(1, 1, 0)
            out_half(0, 0, 1, True).then_inc(unit_done, 1)
            out_half(1, 1, 1).then_inc(unit_done, 1)
            with pe.Fori(1, NT // 2) as i:
                for b in range(2):
                    out_start(2 * i + b, i, b)
                    out_half(2 * i + b, b, 0)
                    out_half(2 * i + b, b, 1).then_inc(unit_done, 1)

        @block.scalar
        def _(act):
            def split_hi(n, hn, b, dst=None):
                act.wait_ge(raw_in[b], 16 * (hn + 1 - N_U // 2))
                act.wait_ge(unit_done, n - 1)
                nc.scalar.activation(w_hi[b][:, :] if dst is None else dst, raw[b][:, :], ACT.Copy).then_inc(hi_done, 1)

            def vb_hi(k):
                act.wait_ge(vb_in[k % 4], 16 * (k // 4 + 1))
                nc.scalar.activation(tile(g_hi, k), land[k % 4][:, :], ACT.Copy).then_inc(hi_done, 1)

            def square_x(t, ht, b):
                act.wait_ge(x_in[b], 16 * (ht + 1))
                nc.scalar.activation(junk[:, :], x_b[b][:, :], ACT.Square, accum_out=ssq[:, b:b + 1]).then_inc(ssq_ok, 1)

            def h_hi(t, n_tr, b):
                act.wait_ge(tr_done, n_tr)
                nc.scalar.activation(w_hi[b][:, :], ps_t[:, :], ACT.Copy).then_inc(hs_hi, 1)

            def gelu_v(t, b):
                act.wait_ge(unit_done, t + 1)
                nc.scalar.activation(buf_a[:, :], acc[b][:, :], ACT.Gelu).then_inc(acc_free[b], 1)

            def vn_split(t):
                act.wait_ge(vn_ok, t + 1)
                nc.scalar.activation(vn_hi[:, :], buf_a[:, :], ACT.Copy).then_inc(vnh_ok, 1)

            for b in range(2):
                act.sem_inc(mix_out[b], 16)
            act.sem_inc(spill_out, 16)
            square_x(0, 0, 0)
            vb_hi(0)
            h_hi(0, 1, 0)
            vb_hi(1)
            act.wait_ge(tr_done, 2)
            nc.scalar.activation(ws_hi[:, :], ps_t[:, :], ACT.Copy).then_inc(wsh_ok, 1)
            vb_hi(2)
            vb_hi(3)
            square_x(1, 0, 1)
            for k in range(4, KT):
                vb_hi(k)
            h_hi(1, 3, 1)
            act.wait_ge(lo_done, KT)
            gelu_v(0, 0)
            with act.Fori(0, NT // 2 - 1) as i:
                for b in (1, 0):
                    t = 2 * i + 2 - b
                    square_x(t + 1, i + 1, 1 - b)
                    act.wait_ge(ht_in[1 - b], 32 * (i + 1))
                    h_hi(t + 1, t + 3, 1 - b)
                    vn_split(t - 1)
                    act.wait_ge(vnl_ok, t)
                    gelu_v(t, b)
            act.wait_ge(mix_done, NT - 2)
            vn_split(NT - 2)
            act.wait_ge(ht_in[0], 16 * NT)
            split_hi(N_U, half(N_U), 0)
            act.wait_ge(vnl_ok, NT - 1)
            gelu_v(NT - 1, 1)
            act.wait_ge(ht_in[1], 16 * NT)
            split_hi(N_U + 1, half(N_U + 1), 1)
            act.wait_ge(mix_done, NT - 1)
            vn_split(NT - 1)
            act.wait_ge(vnl_ok, NT)

            with act.Fori(0, KT) as g:
                n = N_U + 2 * g
                act.wait_ge(unit_done, n + 1)
                nc.scalar.activation(buf_a[:, :], acc[0][:, :], ACT.Gelu).then_inc(acc_free[0], 1)
                split_hi(n + 2, half(N_U + 2, g, 2), 0)
                act.wait_ge(unit_done, n + 2)
                act.wait_ge(um_ok, g + 1)
                nc.scalar.activation(buf_t[:, :], acc[1][:, :], ACT.Tanh, scale=0.5).then_inc(gate_t_ok, 1)
                split_hi(n + 3, half(N_U + 3, g, 2), 1)
                act.wait_ge(prod_ok, g + 1)
                nc.scalar.activation(tile(g_hi, g), buf_t[:, :], ACT.Copy).then_inc(ghi_ok, 1)
            act.wait_ge(g_ready, KT)
            with act.Fori(0, KT) as j:
                n = N_MB + 2 * j
                act.wait_ge(unit_done, n + 1)
                act.wait_ge(acc_free[1], half(N_MB, j, 2))
                nc.scalar.activation(buf_t[:, :], acc[0][:, :], ACT.Tanh, scale=0.5).then_inc(acc_free[0], 1)
                split_hi(n + 2, half(N_MB + 2, j, 2), 0)
                split_hi(n + 3, half(N_MB + 3, j, 2), 1)
                act.wait_ge(acc_free[1], half(N_MB + 2, j, 2))
                act.dma_start(acc_d[bass.ds(j, 1), :, :].rearrange("a p s -> p (a s)"), buf_a[:, :]).then_inc(spill_out, 16)
            act.wait_ge(unit_done, N_KVU + 1)
            act.wait_ge(spill_out, 16 * (1 + KT))
            nc.scalar.activation(buf_a[:, :], acc[0][:, :], ACT.Copy).then_inc(acc_free[0], 1)
            split_hi(N_ATT, half(N_ATT), 0)
            act.wait_ge(acc_free[0], half(N_KVU) + 1)
            for kv in range(N_KV):
                rows = slice(kv * HEAD_DIM, (kv + 1) * HEAD_DIM)
                for hf in range(2):
                    last = nc.scalar.activation(k_hi[hf * HEAD_DIM:(hf + 1) * HEAD_DIM, kv * SEQ:(kv + 1) * SEQ],
                                                buf_a[rows, :], ACT.Copy)
            last.then_inc(khi_ok, 1)
            act.wait_ge(unit_done, N_KVU + 2)
            nc.scalar.activation(buf_b[:, :], acc[1][:, :], ACT.Copy).then_inc(acc_free[1], 1)
            split_hi(N_ATT + 1, half(N_ATT + 1), 1)

            def q_split(p, n0, hn, r):
                act.wait_ge(unit_done, n0 + 1)
                nc.scalar.activation(q_st[0][0:64, :], acc[r][0:64, :], ACT.Copy).then_inc(q_hi_ok, 1)
                nc.scalar.activation(q_st[1][64:128, :], acc[r][64:128, :], ACT.Copy).then_inc(q_hi_ok, 1)
                split_hi(n0 + 2, hn, r)

            q_split(0, N_ATT, half(N_ATT + 2), 0)
            act.wait_ge(vt_done, 1)
            for kv in range(N_KV):
                last = nc.scalar.activation(
                    v_st[:, :].rearrange("p (v t x d) -> p v t x d", v=N_KV, t=NT, x=2)[:, kv, :, 0, :],
                    ps_m[:, :].rearrange("p (t v d) -> p t v d", t=NT, v=N_KV)[:, :, kv, :], ACT.Copy)
            last.then_inc(vhi_ok, 1)

            def pair(p, i, c, r, final=False):
                n0 = c + 6 * i
                for k in range(12):
                    if k >= 5 and k % 2:
                        g = (k - 5) // 2
                        gg = 4 * p + g
                        act.wait_ge(pv_done, gg + 1)
                        if g >= 2:
                            act.wait_ge(oadd_ok, gg - 1)
                        o = ps_m[:, (g % 2) * 512:(g % 2 + 1) * 512]
                        nc.scalar.activation(o_tmp[g % 2][0:64, :], o[64:128, 0:256], ACT.Copy)
                        nc.scalar.activation(o_tmp[g % 2][64:128, :], o[0:64, 256:512], ACT.Copy).then_inc(otmp_ok, 1)
                    if k == 3:
                        act.wait_ge(unit_done, n0 + 2)
                        act.wait_ge(spill_out, 16 * (1 + KT) + 16 * p)
                        nc.scalar.activation(buf_t[:, :], acc[1 - r][:, :], ACT.Tanh, scale=0.5).then_inc(gtan_ok, 1)
                    if k == 7:
                        act.wait_ge(unit_done, n0 + 3)
                        act.wait_ge(acc_free[1 - r], half(c + 1, i, 6) + 1)
                        nc.scalar.activation(buf_t[:, :], acc[r][:, :], ACT.Tanh, scale=0.5).then_inc(acc_free[r], 1)
                    if 2 <= k < 10:
                        s = 8 * p + k - 2
                        act.wait_ge(pt_done, s + 1)
                        if k == 2:
                            last = nc.scalar.activation(pt_hi[:, :].rearrange("p (h c) -> p h c", h=2)[:, :, P:256],
                                                        ps_p.rearrange("p (h c) -> p h c", h=2)[:, :, P:256], ACT.Copy)
                        else:
                            last = nc.scalar.activation(pt_hi[:, :], ps_p, ACT.Copy)
                        last.then_inc(pth_ok, 1)
                    if k < 8:
                        s = 8 * p + k
                        lo = P if k == 0 else 0
                        act.wait_ge(max_ok, s + 1)
                        for h in range(2):
                            w = prob[k % 3][:, h * 256 + lo:(h + 1) * 256]
                            nc.scalar.activation(w, w, ACT.Exp, bias=neg_max[:, 2 * k + h:2 * k + h + 1],
                                                 accum_out=row_sum[:, 2 * k + h:2 * k + h + 1])
                        nc.scalar.activation(sink_e[:, 2 * k:2 * k + 2], sink_d[:, 2 * k:2 * k + 2], ACT.Exp).then_inc(exp_ok, 1)
                    if k == 3:
                        split_hi(n0 + 3, half(c + 3, i, 6), 1 - r)
                    if k == 7:
                        split_hi(n0 + 4, half(c + 4, i, 6), r)
                if not final:
                    q_split(p + 1, n0 + 3, half(c + 5, i, 6), 1 - r)
                act.wait_ge(og_ok, p + 1)
                nc.scalar.activation(tile(g_hi, p), buf_b[:, :], ACT.Copy).then_inc(ghi_ok, 1)
                act.wait_ge(siga_ok, p + 1)
                act.dma_start(sig_d[bass.ds(p, 1), :, :].rearrange("a p s -> p (a s)"), buf_t[:, :]).then_inc(spill_out, 16)

            with act.Fori(0, PAIRS // 2 - 1) as i:
                for r in range(2):
                    pair(2 * i + r, i, N_ATT + 3 * r, r)
            for r in range(2):
                pair(PAIRS - 2 + r, PAIRS // 2 - 1, N_ATT + 3 * r, r, final=(r == 1))

            def load_merge(j):
                act.dma_start(buf_t[:, :], sig_d[bass.ds(j, 1), :, :].rearrange("a p s -> p (a s)")).then_inc(sigr_in, 16)
                act.dma_start(buf_a[:, :], acc_d[bass.ds(j, 1), :, :].rearrange("a p s -> p (a s)")).then_inc(accr_in, 16)

            def merged_hi(j):
                act.wait_ge(mrg_ok, j + 1)
                nc.scalar.activation(tile(ht_hi, j), buf_b[:, :], ACT.Copy).then_inc(mhi_ok, 1)

            act.wait_ge(spill_out, 16 * (1 + KT + PAIRS))
            act.wait_ge(g_ready, 2 * KT)
            load_merge(0)
            with act.Fori(0, KT // 2 - 1) as i:
                for b in range(2):
                    j = 2 * i + b
                    split_hi(N_YA + b + 2 + 2 * i, half(N_YA + 2, i, 2), b)
                    merged_hi(j)
                    act.wait_ge(g_ready, 2 * KT + j + 1)
                    load_merge(j + 1)

            def split_out(s):
                r = N_OUT + s
                act.wait_ge(raw_in[r % 2], 16 * (r // 2 + 1 - N_U // 2))
                if s >= 4:
                    act.wait_ge(unit_done, N_OUT)
                nc.scalar.activation(tile(wo_hi if s < 4 else g_hi, s % 4), raw[r % 2][:, :], ACT.Copy).then_inc(hi_done, 1)

            def tile_hi(t, b, k0=0, k1=KT):
                act.wait_ge(unit_done, N_OUT + t - 1)
                nc.scalar.activation(w_hi[b][:, k0 * P:k1 * P].rearrange("p (k s) -> p k s", k=k1 - k0),
                                     ht_hi[:, :].bitcast(f32).rearrange("p (k s) -> p k s", k=KT)[:, k0:k1, bass.ds(t * P, P)],
                                     ACT.Copy).then_inc(mt_hi, 1)

            split_out(0)
            split_out(1)
            merged_hi(KT - 2)
            act.wait_ge(g_ready, 3 * KT - 1)
            load_merge(KT - 1)
            split_out(2)
            split_out(3)
            act.wait_ge(mhi_ok, KT - 1)
            tile_hi(0, 0, 0, KT - 1)
            merged_hi(KT - 1)

            def square_out(t, b):
                if isinstance(t, int):
                    act.wait_ge(osq_ok, t)
                else:
                    act.wait_ge(mt_hi, t + 3)
                act.wait_ge(unit_done, N_OUT + t + 1)
                nc.scalar.activation(junk[:, :], acc[b][:, :], ACT.Square, accum_out=ssq[:, b:b + 1]).then_inc(osq_ok, 1)

            act.wait_ge(mhi_ok, KT)
            tile_hi(0, 0, KT - 1, KT)
            tile_hi(1, 1)
            for s in range(4, 8):
                split_out(s)
            with act.Fori(0, NT // 2 - 1) as i:
                for b in range(2):
                    square_out(2 * i + b, b)
                    tile_hi(2 * i + b + 2, b)
            square_out(NT - 2, 0)
            square_out(NT - 1, 1)

        @block.gpsimd
        def _(pool):
            def split_lo(n, b):
                pool.wait_ge(hi_done, n + 1)
                nc.gpsimd.tensor_tensor(w_lo[b][:, :], raw[b][:, :], w_hi[b][:, :].bitcast(f32), ALU.subtract).then_inc(lo_done, 1)

            def split_lo_to(n, b, dst, hi):
                pool.wait_ge(hi_done, n + 1)
                nc.gpsimd.tensor_tensor(dst, raw[b][:, :], hi.bitcast(f32), ALU.subtract).then_inc(lo_done, 1)

            def rsqrt_h(t, b):
                pool.wait_ge(msq_ok, t + 1)
                nc.gpsimd.tensor_tensor(rstd[:, b:b + 1], msq[:, b:b + 1], neg_half[:, :], ALU.pow).then_inc(rstd_ok, 1)

            def rsqrt_ln(t):
                pool.wait_ge(var_ok, t + 1)
                nc.gpsimd.tensor_tensor(ln_rstd[:, :], var_eps[:, :], neg_half[:, :], ALU.pow).then_inc(lnr_ok, 1)

            def vn_low(t):
                pool.wait_ge(vnh_ok, t + 1)
                nc.gpsimd.tensor_tensor(vn_lo[:, :], buf_a[:, :], vn_hi[:, :].bitcast(f32), ALU.subtract).then_inc(vnl_ok, 1)

            nc.gpsimd.memset(neg_half[:, :], -0.5).then_inc(pool_own, 1)
            nc.gpsimd.memset(ident[:, :], 0.0).then_inc(pool_own, 1)
            pool.wait_ge(pool_own, 2)
            nc.gpsimd.affine_select(out=ident[:, :], in_=ident[:, :], compare_op=ALU.not_equal, fill=1.0, base=0,
                                    pattern=[[-1, P]], channel_multiplier=1).then_inc(const_ok, 1)
            rsqrt_h(0, 0)
            pool.wait_ge(wsp_in, 16)
            nc.gpsimd.affine_select(out=buf_b[:, :].rearrange("p (g s) -> p g s", g=KT),
                                    in_=buf_b[:, :].rearrange("p (g s) -> p g s", g=KT), compare_op=ALU.is_ge, fill=0.0,
                                    base=0, pattern=[[0, KT], [-1, P]], channel_multiplier=1).then_inc(wsp_ok, 1)
            rsqrt_h(1, 1)
            with pool.Fori(0, NT // 2 - 1) as i:
                for b in (1, 0):
                    t = 2 * i + 2 - b
                    rsqrt_h(t + 1, 1 - b)
                    rsqrt_ln(t - 1)
                    vn_low(t - 1)
            rsqrt_ln(NT - 2)
            vn_low(NT - 2)
            split_lo(N_U, 0)
            rsqrt_ln(NT - 1)
            split_lo(N_U + 1, 1)
            vn_low(NT - 1)
            pool.wait_ge(rel_in, 16)
            nc.gpsimd.memset(bias_row[:, :], NEG_INF / HEAD_DIM ** -0.5).then_inc(pool_own, 1)
            pool.wait_ge(pool_own, 3)
            for bucket, d0, d1 in bucket_runs():
                last = nc.gpsimd.tensor_scalar(bias_row[:, 2 * P - d1:2 * P - d0],
                                               rel_t[:, bucket:bucket + 1].to_broadcast([N_HEADS, d1 - d0]),
                                               1.0 / HEAD_DIM ** -0.5, 1.0, ALU.mult, ALU.mult)
            last.then_inc(bias_made, 1)
            with pool.Fori(N_U // 2, N_ATT // 2 - 1) as h:
                for b in range(2):
                    split_lo(2 * h + 2 + b, b)
            split_lo(N_ATT, 0)
            split_lo(N_ATT + 1, 1)

            split_lo(N_ATT + 2, 0)

            def pair(p, i, c, r, final=False):
                n0 = c + 6 * i
                for k in range(8):
                    s = 8 * p + k
                    lo = P if k == 0 else 0
                    pool.wait_ge(inv_ok, s + 1)
                    stand_alone(pool)
                    for h in range(2):
                        w = prob[k % 3][:, h * 256 + lo:(h + 1) * 256]
                        last = nc.gpsimd.tensor_scalar(w, w, inv_den[:, 2 * k + h:2 * k + h + 1], 0.5, ALU.mult, ALU.mult)
                    last.then_inc(prob_ok, 1)
                    if k == 3:
                        split_lo(n0 + 3, 1 - r)
                    if k == 7:
                        pool.wait_ge(acc_free[r], half(c + 2, i, 6) + 1)
                        stand_alone(pool)
                        nc.gpsimd.tensor_scalar(buf_t[:, :], buf_t[:, :], 0.5, 0.5, ALU.mult, ALU.add).then_inc(siga_ok, 1)
                        split_lo(n0 + 4, r)
                pool.wait_ge(oadd_ok, 4 * p + 4)
                nc.gpsimd.tensor_tensor(buf_b[:, :], buf_b[:, :], buf_a[:, :], ALU.mult).then_inc(og_ok, 1)
                pool.wait_ge(ghi_ok, KT + p + 1)
                nc.gpsimd.tensor_tensor(tile(g_lo, p), buf_b[:, :], tile(g_hi, p).bitcast(f32), ALU.subtract).then_inc(g_ready, 1)
                if not final:
                    split_lo(n0 + 5, 1 - r)

            with pool.Fori(0, PAIRS // 2 - 1) as i:
                for r in range(2):
                    pair(2 * i + r, i, N_ATT + 3 * r, r)
            for r in range(2):
                pair(PAIRS - 2 + r, PAIRS // 2 - 1, N_ATT + 3 * r, r, final=(r == 1))
            with pool.Fori(0, KT // 2 - 1) as i:
                for b in range(2):
                    split_lo(N_YA + 2 + b + 2 * i, b)

            def split_out(s):
                r = N_OUT + s
                if s < 4:
                    split_lo_to(r, r % 2, tile(wo_lo, s), tile(wo_hi, s))
                else:
                    split_lo_to(r, r % 2, tile(g_hi, s), tile(g_hi, s - 4))

            for s in range(4):
                split_out(s)

            def rsqrt_out(t, b):
                pool.wait_ge(oms_ok, t + 1)
                nc.gpsimd.tensor_tensor(rstd[:, b:b + 1], msq[:, b:b + 1], neg_half[:, :], ALU.pow).then_inc(ors_ok, 1)

            for s in range(4, 8):
                split_out(s)
            with pool.Fori(0, NT // 2) as i:
                for b in range(2):
                    rsqrt_out(2 * i + b, b)

        @block.vector
        def _(dve):
            own = Chain(dve, dve_own)

            def mean_sq(t, b):
                dve.wait_ge(ssq_ok, t + 1)
                nc.vector.tensor_scalar(msq[:, b:b + 1], ssq[:, b:b + 1], 1.0 / D_MODEL, EPS, ALU.mult, ALU.add).then_inc(msq_ok, 1)

            def norm_h(t, b):
                dve.wait_ge(rstd_ok, t + 1)
                nc.vector.scalar_tensor_tensor(out=x_b[b][:, :], in0=x_b[b][:, :], scalar=rstd[:, b:b + 1],
                                               in1=pre_b[:, :], op0=ALU.mult, op1=ALU.mult).then_inc(h_ok, 1)

            def h_lo(t, b):
                dve.wait_ge(hs_hi, t + 1)
                nc.vector.tensor_tensor(w_lo[b][:, :], ps_t[:, :], w_hi[b][:, :].bitcast(f32), ALU.subtract).then_inc(hs_lo, 1)

            def mix_read(t, ht, b):
                dve.wait_ge(mix_done, t + 1)
                dve.wait_ge(mix_out[b], 16 * (ht + 1))
                nc.vector.tensor_tensor(mix_b[b][:, :], ps_m[:, :], bs_b[:, :], ALU.add).then_inc(mix_ok, 1)

            def layer_norm(t, ht, b):
                dve.wait_ge(acc_free[b], ht + 1)
                for hf in range(2):
                    last = nc.vector.bn_stats(bn6[:, 6 * hf:6 * hf + 6], buf_a[:, hf * HALF:(hf + 1) * HALF])
                own.link(last)
                stand_alone(dve)
                own.link(nc.vector.bn_aggr(mean_var[:, :], bn6[:, :].rearrange("p (a s) -> p a s", s=6)))
                nc.vector.tensor_scalar(var_eps[:, :], mean_var[:, 1:2], EPS, None, ALU.add).then_inc(var_ok, 1)
                dve.wait_ge(lnr_ok, t + 1)
                own.link(nc.vector.tensor_scalar(buf_a[:, :], buf_a[:, :], mean_var[:, 0:1], ln_rstd[:, 0:1],
                                                 ALU.subtract, ALU.mult))
                own.link(nc.vector.tensor_tensor(buf_a[:, :], buf_a[:, :], lng_b[:, :], ALU.mult))
                nc.vector.tensor_tensor(buf_a[:, :], buf_a[:, :], lnb_b[:, :], ALU.add).then_inc(vn_ok, 1)

            LN_LINKS = 4
            def vb_lo(k):
                dve.wait_ge(hi_done, k + 1)
                nc.vector.tensor_tensor(tile(g_lo, k), land[k % 4][:, :], tile(g_hi, k).bitcast(f32), ALU.subtract).then_inc(lo_done, 1)

            mean_sq(0, 0)
            dve.wait_ge(pre_in, 16)
            norm_h(0, 0)
            vb_lo(0)
            h_lo(0, 0)
            vb_lo(1)
            dve.wait_ge(wsh_ok, 1)
            nc.vector.tensor_tensor(ws_lo[:, :], ps_t[:, :], ws_hi[:, :].bitcast(f32), ALU.subtract).then_inc(wsl_ok, 1)
            vb_lo(2)
            vb_lo(3)
            mean_sq(1, 1)
            norm_h(1, 1)
            for k in range(4, KT):
                vb_lo(k)
            h_lo(1, 1)
            dve.wait_ge(ln_in, 32)
            dve.wait_ge(bs_in, 16)
            with dve.Fori(0, NT // 2 - 1) as i:
                own.at(2 * LN_LINKS * i)
                for b in (1, 0):
                    t = 2 * i + 2 - b
                    mean_sq(t + 1, 1 - b)
                    norm_h(t + 1, 1 - b)
                    layer_norm(t - 1, i, 1 - b)
                    h_lo(t + 1, 1 - b)
                    mix_read(t - 1, i, 1 - b)
            own.at(LN_LINKS * (NT - 2))
            layer_norm(NT - 2, NT // 2 - 1, 0)
            mix_read(NT - 2, NT // 2 - 1, 0)
            layer_norm(NT - 1, NT // 2 - 1, 1)
            mix_read(NT - 1, NT // 2 - 1, 1)

            with dve.Fori(0, KT) as g:
                dve.wait_ge(acc_free[0], half(N_U + 2, g, 2))
                dve.wait_ge(mix_in, 16 * (g + 1))
                nc.vector.tensor_tensor(buf_a[:, :], buf_a[:, :], buf_b[:, :], ALU.mult).then_inc(um_ok, 1)
                dve.wait_ge(gate_t_ok, g + 1)
                nc.vector.scalar_tensor_tensor(out=buf_t[:, :], in0=buf_t[:, :], scalar=1.0, in1=acc[1][:, :],
                                               op0=ALU.add, op1=ALU.mult).then_inc(acc_free[1], 1)
                dve.wait_ge(um_ok, g + 1)
                dve.wait_ge(acc_free[1], half(N_U + 2, g, 2))
                nc.vector.scalar_tensor_tensor(out=buf_t[:, :], in0=buf_t[:, :], scalar=0.5, in1=buf_a[:, :],
                                               op0=ALU.mult, op1=ALU.mult).then_inc(prod_ok, 1)
                dve.wait_ge(prod_ok, g + 1)
                dve.wait_ge(ghi_ok, g + 1)
                nc.vector.tensor_tensor(tile(g_lo, g), buf_t[:, :], tile(g_hi, g).bitcast(f32), ALU.subtract).then_inc(g_ready, 1)
            base = own.base + own.k
            with dve.Fori(0, KT) as j:
                own.at(base + j)
                dve.wait_ge(acc_free[0], half(N_MB + 2, j, 2))
                own.link(nc.vector.tensor_scalar(buf_t[:, :], buf_t[:, :], 0.5, 0.5, ALU.mult, ALU.add))
                dve.wait_ge(unit_done, N_MB + 2 + 2 * j)
                dve.wait_ge(spill_out, 16 * (j + 1))
                nc.vector.tensor_tensor(buf_a[:, :], acc[1][:, :], buf_t[:, :], ALU.mult).then_inc(acc_free[1], 1)
            base = base + KT
            dve.wait_ge(khi_ok, 1)
            for kv in range(N_KV):
                rows = slice(kv * HEAD_DIM, (kv + 1) * HEAD_DIM)
                cols = slice(kv * SEQ, (kv + 1) * SEQ)
                for hf in range(2):
                    last = nc.vector.tensor_tensor(k_lo[hf * HEAD_DIM:(hf + 1) * HEAD_DIM, cols], buf_a[rows, :],
                                                   k_hi[rows, cols].bitcast(f32), ALU.subtract)
            last.then_inc(klo_ok, 1)
            dve.wait_ge(vhi_ok, 1)
            v5 = v_st[:, :].rearrange("p (v t x d) -> p v t x d", v=N_KV, t=NT, x=2)
            v5f = v_st[:, :].bitcast(f32).rearrange("p (v t x d) -> p v t x d", v=N_KV, t=NT, x=2)
            for kv in range(N_KV):
                last = nc.vector.tensor_tensor(
                    v5[:, kv, :, 1, :], ps_m[:, :].rearrange("p (t v d) -> p t v d", t=NT, v=N_KV)[:, :, kv, :],
                    v5f[:, kv, :, 0, :], ALU.subtract)
            last.then_inc(scores_used, 1)
            dve.wait_ge(sink_in, 16)

            def q_lo(p, r):
                dve.wait_ge(q_hi_ok, 2 * p + 1)
                nc.vector.tensor_tensor(q_st[0][64:128, :], acc[r][0:64, :], q_st[0][0:64, :].bitcast(f32), ALU.subtract)
                dve.wait_ge(q_hi_ok, 2 * p + 2)
                nc.vector.tensor_tensor(q_st[1][0:64, :], acc[r][64:128, :], q_st[1][64:128, :].bitcast(f32),
                                        ALU.subtract).then_inc(acc_free[r], 1)

            q_lo(0, 0)

            def pair(p, i, c, r, final=False):
                own.link(nc.vector.tensor_copy(sink_p[:, :], sink_b[:, bass.ds(2 * p, 2)]))
                dve.wait_ge(bias_in, 16 * (p + 1))
                for k in range(12):
                    if k >= 5 and k % 2:
                        g = (k - 5) // 2
                        if g == 0:
                            dve.wait_ge(g_ready, KT + p)
                        dve.wait_ge(otmp_ok, 4 * p + g + 1)
                        o = ps_m[:, (g % 2) * 512:(g % 2 + 1) * 512]
                        cols = slice(g * 256, (g + 1) * 256)
                        nc.vector.tensor_tensor(buf_b[0:64, cols], o[0:64, 0:256], o_tmp[g % 2][0:64, :], ALU.add)
                        nc.vector.tensor_tensor(buf_b[64:128, cols], o[64:128, 256:512], o_tmp[g % 2][64:128, :],
                                                ALU.add).then_inc(oadd_ok, 1)
                    if k < 8:
                        lo = P if k == 0 else 0
                        c2 = slice(2 * k, 2 * k + 2)
                        dve.wait_ge(scores_ok, 8 * p + k + 1)
                        stand_alone(dve)
                        for h in range(2):
                            cs = slice(h * 256 + lo, (h + 1) * 256)
                            last = nc.vector.tensor_tensor_reduce(
                                out=prob[k % 3][:, cs], in0=ps_s[:, cs], in1=bias_t[:, cs], scale=HEAD_DIM ** -0.5,
                                scalar=sink_p[:, h:h + 1], op0=ALU.add, op1=ALU.max,
                                accum_out=row_max[:, 2 * k + h:2 * k + h + 1])
                        last.then_inc(scores_used, 1)
                        dve.wait_ge(scores_used, 8 * p + k + 2)
                        nc.vector.tensor_scalar(neg_max[:, c2], row_max[:, c2], -1.0, None, ALU.mult)
                        nc.vector.tensor_tensor(sink_d[:, c2], sink_p[:, :], row_max[:, c2],
                                                ALU.subtract).then_inc(max_ok, 1)
                    if 1 <= k < 9:
                        m2 = slice(2 * k - 2, 2 * k)
                        dve.wait_ge(exp_ok, 8 * p + k)
                        own.link(nc.vector.tensor_tensor(denom[:, m2], row_sum[:, m2], sink_e[:, m2], ALU.add))
                        nc.vector.reciprocal(inv_den[:, m2], denom[:, m2]).then_inc(inv_ok, 1)
                    if 2 <= k < 10:
                        dve.wait_ge(pth_ok, 8 * p + k - 1)
                        if k == 2:
                            v = lambda t: t.rearrange("p (h c) -> p h c", h=2)[:, :, P:256]
                            last = nc.vector.tensor_tensor(v(pt_lo[:, :]), v(ps_p), v(pt_hi[:, :].bitcast(f32)), ALU.subtract)
                        else:
                            last = nc.vector.tensor_tensor(pt_lo[:, :], ps_p, pt_hi[:, :].bitcast(f32), ALU.subtract)
                        last.then_inc(ptl_ok, 1)
                    if k == 3:
                        dve.wait_ge(g_ready, KT + p)
                        dve.wait_ge(gtan_ok, p + 1)
                        nc.vector.scalar_tensor_tensor(out=buf_a[:, :], in0=buf_t[:, :], scalar=1.0, in1=acc[1 - r][:, :],
                                                       op0=ALU.add, op1=ALU.mult).then_inc(acc_free[1 - r], 1)
                if not final:
                    q_lo(p + 1, 1 - r)

            with dve.Fori(0, PAIRS // 2 - 1) as i:
                own.at(base + 2 * (NT + 1) * i)
                for r in range(2):
                    pair(2 * i + r, i, N_ATT + 3 * r, r)
            own.at(base + 2 * (NT + 1) * (PAIRS // 2 - 1))
            for r in range(2):
                pair(PAIRS - 2 + r, PAIRS // 2 - 1, N_ATT + 3 * r, r, final=(r == 1))
            def tile_lo(t, b, k0=0, k1=KT):
                dve.wait_ge(unit_done, N_OUT + t - 1)
                nc.vector.tensor_copy(w_lo[b][:, k0 * P:k1 * P].rearrange("p (k s) -> p k s", k=k1 - k0),
                                      ht_lo[:, :].bitcast(f32).rearrange("p (k s) -> p k s", k=KT)[:, k0:k1, bass.ds(t * P, P)]
                                      ).then_inc(mt_lo, 1)

            def merge(j, i, b):
                    dve.wait_ge(unit_done, N_YA + 1 + b + 2 * i)
                    dve.wait_ge(sigr_in, 16 * (j + 1))
                    nc.vector.tensor_tensor(buf_b[:, :], acc[b][:, :], buf_t[:, :], ALU.mult).then_inc(acc_free[b], 1)
                    dve.wait_ge(acc_free[b], half(N_YA + 2, i, 2))
                    dve.wait_ge(accr_in, 16 * (j + 1))
                    nc.vector.tensor_tensor(buf_b[:, :], buf_b[:, :], buf_a[:, :], ALU.add).then_inc(mrg_ok, 1)
                    dve.wait_ge(mhi_ok, j + 1)
                    nc.vector.tensor_tensor(tile(ht_lo, j), buf_b[:, :], tile(ht_hi, j).bitcast(f32), ALU.subtract).then_inc(g_ready, 1)

            dve.wait_ge(g_ready, 2 * KT)
            with dve.Fori(0, KT // 2 - 1) as i:
                for b in range(2):
                    merge(2 * i + b, i, b)
            merge(KT - 2, KT // 2 - 1, 0)
            dve.wait_ge(g_ready, 3 * KT - 1)
            tile_lo(0, 0, 0, KT - 1)
            merge(KT - 1, KT // 2 - 1, 1)
            dve.wait_ge(g_ready, 3 * KT)
            tile_lo(0, 0, KT - 1, KT)
            tile_lo(1, 1)

            dve.wait_ge(post_in, 16)

            def out_tile(t, b, ht, first):
                y = (buf_a, buf_b)[b]
                dve.wait_ge(osq_ok, t + 1)
                nc.vector.tensor_scalar(msq[:, b:b + 1], ssq[:, b:b + 1], 1.0 / D_MODEL, EPS, ALU.mult, ALU.add).then_inc(oms_ok, 1)
                if not first:
                    dve.wait_ge(y_out[b], 16 * ht)
                dve.wait_ge(ors_ok, t + 1)
                nc.vector.scalar_tensor_tensor(out=y[:, :], in0=acc[b][:, :], scalar=rstd[:, b:b + 1], in1=buf_t[:, :],
                                               op0=ALU.mult, op1=ALU.mult).then_inc(acc_free[b], 1)
                dve.wait_ge(acc_free[b], N_OUT // 2 + 1 + ht)
                dve.wait_ge(xr_in[b], 16 * (ht + 1))
                nc.vector.tensor_tensor(y[:, :], y[:, :], x_r[b][:, :], ALU.add).then_inc(y_ok, 1)

            out_tile(0, 0, 0, True)
            tile_lo(2, 0)
            out_tile(1, 1, 0, True)
            tile_lo(3, 1)
            with dve.Fori(1, NT // 2 - 1) as i:
                for b in range(2):
                    out_tile(2 * i + b, b, i, False)
                    tile_lo(2 * i + b + 2, b)
            for b in range(2):
                out_tile(NT - 2 + b, b, NT // 2 - 1, False)


INPUTS = ("x", "rel_bias", "pre_norm", "post_norm", "w_in", "sinks", "sgu_ln_g", "sgu_ln_b", "w_spatial",
          "b_spatial", "w_branch_a", "w_branch_b", "w_out")


def kernel(**inputs):
    import concourse.bacc as bacc
    from concourse.bass_utils import run_bass_kernel_spmd

    nc = bacc.Bacc("TRN2", target_bir_lowering=False, num_devices=1, dynamic_dma_scratch_size=1024)
    arrays, args = {}, []
    for name in INPUTS:
        a = np.ascontiguousarray(inputs[name])
        arrays["in_" + name] = a
        args.append(nc.dram_tensor("in_" + name, a.shape, mybir.dt.from_np(a.dtype), kind="ExternalInput").ap())
    args.append(nc.dram_tensor("out", inputs["x"].shape, mybir.dt.float32, kind="ExternalOutput").ap())
    build(nc, *args)
    r = run_bass_kernel_spmd(nc, [arrays], core_ids=[0])
    return r.results[0]["out"]
```

```python
import numpy as np
import concourse.bass as bass
from concourse import mybir
from contextlib import ExitStack

P = 128
D_MODEL = 1024
SEQ = 1024
HEAD_DIM = 64
N_HEADS = D_MODEL // HEAD_DIM
N_KV = 2
KT = D_MODEL // P
NT = SEQ // P
HALF = 512
N_BUCKETS = 32
MAX_DISTANCE = 128
WINDOW = 128
EPS = 1e-6
NEG_INF = -1e30
PAIRS = N_HEADS // 2
PAIRS_PER_KV = PAIRS // N_KV

Q_COL = 0
K_COL = Q_COL + D_MODEL
V_COL = K_COL + N_KV * HEAD_DIM
GA_COL = V_COL + N_KV * HEAD_DIM
U_COL = GA_COL + D_MODEL
VB_COL = U_COL + D_MODEL
GB_COL = VB_COL + D_MODEL
MGA_COL = GB_COL + D_MODEL
MGB_COL = MGA_COL + D_MODEL

N_U = NT
N_MB = N_U + 2 * KT
N_KVU = N_MB + 2 * KT
N_ATT = N_KVU + 2
N_YA = N_ATT + 3 * PAIRS
N_OUT = N_YA + KT
BIAS_ROW = 3 * P
WARM_UP = 24
UNIT = 6 * KT
FIRST_SLOT, SLOT_STEP, SLOTS = 19, 11, NT + 4


def bucket_runs():
    dist = np.arange(WINDOW)
    exact = N_BUCKETS // 2
    large = exact + (np.log(np.maximum(dist, exact) / exact)
                     / np.log(MAX_DISTANCE / exact) * (N_BUCKETS - exact)).astype(np.int32)
    bucket = np.where(dist < exact, dist, np.minimum(large, N_BUCKETS - 1))
    return [(int(b), int(np.argmax(bucket == b)), int(np.sum(bucket <= b))) for b in np.unique(bucket)]


class Chain:

    def __init__(self, eng, sem):
        self.eng, self.sem, self.base, self.k = eng, sem, 0, 0

    def link(self, ins):
        self.k += 1
        ins.then_inc(self.sem, 1)
        self.eng.wait_ge(self.sem, self.base + self.k)

    def at(self, base):
        self.base, self.k = base, 0


def build(nc, x, rel_bias, pre_norm, post_norm, w_in, sinks, sgu_ln_g, sgu_ln_b,
          w_spatial, b_spatial, w_branch_a, w_branch_b, w_out, out):
    f32 = mybir.dt.float32
    f32r = mybir.dt.float32r
    bf16 = mybir.dt.bfloat16
    ACT = mybir.ActivationFunctionType
    ALU = mybir.AluOpType

    w_in_t = w_in[0].rearrange("(k p) c -> p k c", p=P)
    w_a_t = w_branch_a[0].rearrange("(k p) c -> p k c", p=P)
    w_b_t = w_branch_b[0].rearrange("(k p) c -> p k c", p=P)
    w_out_t = w_out[0].rearrange("(k p) c -> p k c", p=P)

    mix_d = nc.dram_tensor("mix_d", [KT, P, SEQ], f32)
    acc_d = nc.dram_tensor("acc_d", [KT, P, SEQ], f32)
    sig_d = nc.dram_tensor("sig_d", [KT, P, SEQ], f32)
    bias_d = nc.dram_tensor("bias_d", [N_HEADS, BIAS_ROW], f32)
    skew_d = nc.dram_tensor("skew_d", [N_HEADS, P, BIAS_ROW], f32)

    with ExitStack() as ctx:
        def sb(name, shape, dt=f32, scope=ctx):
            return scope.enter_context(nc.sbuf_tensor(name, shape, dt))

        def sem(name):
            return ctx.enter_context(nc.semaphore(name))

        ht_hi = sb("ht_hi", [P, KT * SEQ], f32r)
        ht_lo = sb("ht_lo", [P, KT * SEQ], f32r)
        g_hi = sb("g_hi", [P, KT * SEQ], f32r)
        g_lo = sb("g_lo", [P, KT * SEQ], f32r)
        raw = [sb(f"raw{b}", [P, 1024]) for b in range(2)]
        w_hi = [sb(f"w_hi{b}", [P, 1024], f32r) for b in range(2)]
        w_lo = [sb(f"w_lo{b}", [P, 1024], f32r) for b in range(2)]
        buf_t = sb("buf_t", [P, SEQ])
        buf_a = sb("buf_a", [P, SEQ])
        buf_b = sb("buf_b", [P, SEQ])
        junk = sb("junk", [P, SEQ], bf16)
        ident = sb("ident", [P, P])
        before = sb("before", [P, 256])
        neg_half = sb("neg_half", [P, 1])
        ssq = sb("ssq", [P, 2])
        ssq_h = sb("ssq_h", [P, 2])
        msq = sb("msq", [P, 2])
        rstd = sb("rstd", [P, 2])
        bn6 = sb("bn6", [P, 12])
        mean_var = sb("mean_var", [P, 2])
        var_eps = sb("var_eps", [P, 1])
        ln_rstd = sb("ln_rstd", [P, 1])
        sink_b = sb("sink_b", [P, N_HEADS])
        sink_p = sb("sink_p", [P, 2])
        row_max = sb("row_max", [P, 2 * NT])
        neg_max = sb("neg_max", [P, 2 * NT])
        sink_d = sb("sink_d", [P, 2 * NT])
        row_sum = sb("row_sum", [P, 2 * NT])
        sink_e = sb("sink_e", [P, 2 * NT])
        denom = sb("denom", [P, 2 * NT])
        inv_den = sb("inv_den", [P, 2 * NT])
        rel_t = sb("rel_t", [N_HEADS, N_BUCKETS])
        bias_row = sb("bias_row", [N_HEADS, BIAS_ROW])

        with ExitStack() as s0:
            x_b = [sb(f"x_b{b}", [P, D_MODEL], f32, s0) for b in range(2)]
            pre_b = sb("pre_b", [P, D_MODEL], f32, s0)
            lng_b = sb("lng_b", [P, D_MODEL], f32, s0)
            lnb_b = sb("lnb_b", [P, D_MODEL], f32, s0)
            bs_b = sb("bs_b", [P, KT * P], f32, s0)
            mix_b = [sb(f"mix_b{b}", [P, KT * P], f32, s0) for b in range(2)]
            vn_hi = sb("vn_hi", [P, D_MODEL], f32r, s0)
            vn_lo = sb("vn_lo", [P, D_MODEL], f32r, s0)
            ws_st = sb("ws_st", [P, KT * 2 * P], f32r, s0)
        with ExitStack() as s1:
            k_hi = sb("k_hi", [P, N_KV * SEQ], f32r, s1)
            k_lo = sb("k_lo", [P, N_KV * SEQ], f32r, s1)
            v_st = sb("v_st", [P, N_KV * NT * P], f32r, s1)
            q_st = [sb(f"q_st{h}", [P, SEQ], f32r, s1) for h in range(2)]
            prob = [sb(f"prob{b}", [P, 256], f32, s1) for b in range(3)]
            pt_packed = sb("pt_packed", [P, 512], f32r, s1)
            pt = [sb(f"pt{b}", [P, 1024], f32r, s1) for b in range(2)]
            bias_t = sb("bias_t", [P, 512], f32, s1)
            bias_p = sb("bias_p", [P, 256], f32, s1)
            o_tmp = [sb(f"o_tmp{b}", [P, 256], f32, s1) for b in range(2)]
        with ExitStack() as s2:
            wo_hi = sb("wo_hi", [P, KT * HALF], f32r, s2)
            wo_lo = sb("wo_lo", [P, KT * HALF], f32r, s2)
            x_r = [sb(f"x_r{b}", [P, D_MODEL], f32, s2) for b in range(2)]

        acc = [ctx.enter_context(nc.psum_tensor(f"acc{b}", [P, 1024], f32)) for b in range(2)]
        ps_t = ctx.enter_context(nc.psum_tensor("ps_t", [P, 1024], f32))
        ps_m = ctx.enter_context(nc.psum_tensor("ps_m", [P, 1024], f32))
        ps_s, ps_p = ps_t[:, 0:512], ps_t[:, 512:768]

        raw_in = [sem(f"raw_in{b}") for b in range(2)]
        hi_done, lo_done = sem("hi_done"), sem("lo_done")
        unit_done = sem("unit_done")
        acc_free = [sem(f"acc_free{b}") for b in range(2)]
        x_in = [sem(f"x_in{b}") for b in range(2)]
        pre_in, ln_in, bs_in, wsp_in = sem("pre_in"), sem("ln_in"), sem("bs_in"), sem("wsp_in")
        rel_in, sink_in, bias_out, skew_out = sem("rel_in"), sem("sink_in"), sem("bias_out"), sem("skew_out")
        bias_made = sem("bias_made")
        const_ok, wsp_ok = sem("const_ok"), sem("wsp_ok")
        ssq_ok, msq_ok, rstd_ok, h_ok = sem("ssq_ok"), sem("msq_ok"), sem("rstd_ok"), sem("h_ok")
        tr_done = sem("tr_done")
        hs_hi, hs_lo = sem("hs_hi"), sem("hs_lo")
        ht_in = [sem(f"ht_in{b}") for b in range(2)]
        vb_in = [sem(f"vb_in{b}") for b in range(4)]
        vb_lo_dve, vb_lo_pool = sem("vb_lo_dve"), sem("vb_lo_pool")
        wsh_ok, wsl_ok = sem("wsh_ok"), sem("wsl_ok")
        var_ok, lnr_ok, vn_ok = sem("var_ok"), sem("lnr_ok"), sem("vn_ok")
        vnh_ok, vnl_ok = sem("vnh_ok"), sem("vnl_ok")
        mix_done, mix_lo_out, mix_ok, mix_biased = sem("mix_done"), sem("mix_lo_out"), sem("mix_ok"), sem("mix_biased")
        mix_out = [sem(f"mix_out{b}") for b in range(2)]
        mix_in, gate_t_ok, um_ok, prod_ok = sem("mix_in"), sem("gate_t_ok"), sem("um_ok"), sem("prod_ok")
        ghi_ok, g_ready = sem("ghi_ok"), sem("g_ready")
        spill_out = sem("spill_out")
        khi_ok, klo_ok, vt_done, vhi_ok = sem("khi_ok"), sem("klo_ok"), sem("vt_done"), sem("vhi_ok")
        bias_in, before_ok = sem("bias_in"), sem("before_ok")
        q_hi_ok = sem("q_hi_ok")
        scores_ok, scores_used, max_ok, exp_ok, inv_ok, prob_ok = (
            sem("scores_ok"), sem("scores_used"), sem("max_ok"), sem("exp_ok"), sem("inv_ok"), sem("prob_ok"))
        pt_done, pth_ok, ptl_ok, pt_ok, pv_done = (
            sem("pt_done"), sem("pth_ok"), sem("ptl_ok"), sem("pt_ok"), sem("pv_done"))
        otmp_ok, oadd_ok, gtan_ok, og_ok = (
            sem("otmp_ok"), sem("oadd_ok"), sem("gtan_ok"), sem("og_ok"))
        siga_ok = sem("siga_ok")
        sigr_in, accr_in, mrg_ok, mhi_ok = sem("sigr_in"), sem("accr_in"), sem("mrg_ok"), sem("mhi_ok")
        post_in, xr_in = sem("post_in"), [sem(f"xr_in{b}") for b in range(2)]
        mt_hi, mt_lo = sem("mt_hi"), sem("mt_lo")
        osq_ok, oms_ok, ors_ok, y_ok = sem("osq_ok"), sem("oms_ok"), sem("ors_ok"), sem("y_ok")
        y_out = [sem(f"y_out{b}") for b in range(2)]
        wo_in = [sem(f"wo_in{b}") for b in range(2)]
        wo_lo_dve, half_done, yw_ok, ssum_ok = sem("wo_lo_dve"), sem("half_done"), sem("yw_ok"), sem("ssum_ok")
        dve_own, pool_own, waited = sem("dve_own"), sem("pool_own"), sem("waited")

        block = ctx.enter_context(nc.Block())

        def stand_alone(eng):
            eng.sem_inc(waited, 1)

        def tile(buf, i, n=SEQ):
            return buf[:, bass.ds(i * n, n)]

        def col3(buf, i):
            return buf[:, :].rearrange("p (k s) -> p k s", k=KT)[:, :, bass.ds(i * P, P)]

        def k3(buf):
            return buf[:, :].rearrange("p (k s) -> p k s", k=KT)

        v_buf = (buf_a, buf_t)
        ws4 = ws_st[:, :].rearrange("p (g x t) -> p g x t", g=KT, x=2)

        land = (raw[0], raw[1], buf_t, buf_a)
        vb_by_pool = (4,)
        vb_by_dve = tuple(k for k in range(KT) if k not in vb_by_pool)

        def wo_land(s):
            return raw[s % 2] if s < 6 else x_r[s % 2]

        def wait_wo(eng, s):
            if s in (5, 7):
                eng.wait_ge(wo_lo_dve, 1 if s == 5 else 2)
            else:
                eng.wait_ge(lo_done, N_OUT + (s if s < 5 else 5) + 1)

        def wait_vb_lo(eng, k):
            if k in vb_by_pool:
                eng.wait_ge(vb_lo_pool, vb_by_pool.index(k) + 1)
            else:
                eng.wait_ge(vb_lo_dve, vb_by_dve.index(k) + 1)

        def half(c, i=0, s=0):
            return c // 2 + (s // 2) * i if s else c // 2

        @block.sync
        def _(sp):
            def load_raw(n, b, src, col):
                sp.wait_ge(hi_done, n - 1)
                stand_alone(sp)
                sp.wait_ge(lo_done, n - 1)
                stand_alone(sp)
                sp.dma_start(raw[b][:, :].rearrange("p (k c) -> p k c", c=P),
                             src[:, :, bass.ds(col, P)]).then_inc(raw_in[b], 16)

            def load_x(t, b):
                sp.dma_start(x_b[b][:, :], x[0, bass.ds(t * P, P), :]).then_inc(x_in[b], 16)

            def load_vb(k):
                if k >= 4:
                    wait_vb_lo(sp, k - 4)
                sp.dma_start(land[k % 4][:, :], w_in_t[:, k, VB_COL:VB_COL + D_MODEL]).then_inc(vb_in[k % 4], 16)

            def copy_h(t, b):
                sp.wait_ge(hs_lo, t + 1)
                stand_alone(sp)
                for src, dst in ((w_hi[b], ht_hi), (w_lo[b], ht_lo)):
                    sp.dma_start(col3(dst, t).bitcast(f32), k3(src).bitcast(f32)).then_inc(ht_in[b], 16)

            load_x(0, 0)
            sp.dma_start(pre_b[:, :], pre_norm[0:1, :].to_broadcast([P, D_MODEL])).then_inc(pre_in, 16)
            load_vb(0)
            sp.dma_start(buf_b[:, :].rearrange("p (g s) -> p g s", g=KT),
                         w_spatial[0].rearrange("g t s -> t g s")).then_inc(wsp_in, 16)
            load_vb(1)
            load_vb(2)
            load_vb(3)
            load_x(1, 1)
            for k in range(4, KT):
                load_vb(k)
            sp.dma_start(lng_b[:, :], sgu_ln_g[0:1, :].to_broadcast([P, D_MODEL])).then_inc(ln_in, 16)
            sp.dma_start(lnb_b[:, :], sgu_ln_b[0:1, :].to_broadcast([P, D_MODEL])).then_inc(ln_in, 16)
            sp.dma_start(bs_b[:, :], b_spatial.rearrange("a g t -> a (g t)").to_broadcast([P, KT * P])).then_inc(bs_in, 16)
            sp.dma_start(sink_b[:, :], sinks[0:1, :].to_broadcast([P, N_HEADS])).then_inc(sink_in, 16)
            sp.dma_start(rel_t[:, :], rel_bias.rearrange("b h -> h b"), allow_slow_non_contiguous=True).then_inc(rel_in, 16)

            def spill_mix(t, b):
                sp.wait_ge(mix_biased, t + 1)
                stand_alone(sp)
                sp.dma_start(mix_d[:, :, bass.ds(t * P, P)].rearrange("g p s -> p g s"),
                             mix_b[b][:, :].rearrange("p (g s) -> p g s", g=KT)).then_inc(mix_out[b], 16)

            def next_x(t, b):
                sp.wait_ge(tr_done, t)
                load_x(t, b)
                copy_h(t - 2, b)

            next_x(2, 0)
            next_x(3, 1)
            wait_vb_lo(sp, 4)
            wait_vb_lo(sp, 5)
            load_raw(N_U, 0, w_in_t, U_COL)
            load_raw(N_U + 1, 1, w_in_t, GB_COL)
            with sp.Fori(2, NT // 2) as i:
                for b in range(2):
                    next_x(2 * i + b, b)
                    spill_mix(2 * i + b - 4, b)
            for t in range(NT - 2, NT):
                copy_h(t, t % 2)
                spill_mix(t - 2, t % 2)
            load_raw(N_U + 2, 0, w_in_t, U_COL + P)
            load_raw(N_U + 3, 1, w_in_t, GB_COL + P)
            spill_mix(NT - 2, 0)
            spill_mix(NT - 1, 1)

            def load_mix(g):
                sp.dma_start(buf_b[:, :], mix_d[bass.ds(g, 1), :, :].rearrange("a p s -> p (a s)")).then_inc(mix_in, 16)

            for b in range(2):
                sp.wait_ge(mix_out[b], 16 * (1 + NT // 2))
            load_mix(0)
            sp.wait_ge(um_ok, 1)
            load_mix(1)
            with sp.Fori(2, KT) as g:
                load_raw(N_U + 2 * g, 0, w_in_t, U_COL + g * P)
                load_raw(N_U + 2 * g + 1, 1, w_in_t, GB_COL + g * P)
                sp.wait_ge(um_ok, g)
                load_mix(g)
            sp.wait_ge(bias_made, 1)
            sp.dma_start(bias_d[:, :], bias_row[:, :]).then_inc(bias_out, 16)
            sp.wait_ge(bias_out, 16)
            sp.dma_start(skew_d[:, :, :], bass.AP(bias_d, 0, [[BIAS_ROW, N_HEADS], [0, P], [1, BIAS_ROW]])).then_inc(skew_out, 16)
            with sp.Fori(0, KT) as j:
                load_raw(N_MB + 2 * j, 0, w_in_t, MGB_COL + j * P)
                load_raw(N_MB + 2 * j + 1, 1, w_b_t, j * P)
            load_raw(N_KVU, 0, w_in_t, K_COL)
            load_raw(N_KVU + 1, 1, w_in_t, V_COL)
            sp.wait_ge(skew_out, 16)
            sp.wait_ge(mix_done, NT)
            load_raw(N_ATT, 0, w_in_t, Q_COL)

            def load_pair(p, i, r, last):
                    n = N_ATT + 3 * r + 6 * i
                    load_raw(n + 1, 1 - r, w_in_t, GA_COL + p * P)
                    load_raw(n + 2, r, w_in_t, MGA_COL + p * P)
                    sp.wait_ge(scores_used, 8 * p + 1)
                    sp.dma_start(bias_t[:, :].rearrange("p (h j) -> p h j", h=2),
                                 bass.AP(skew_d, p * (2 * P * BIAS_ROW) + (P - 1),
                                         [[BIAS_ROW - 1, P], [P * BIAS_ROW, 2], [1, 2 * P]])).then_inc(bias_in, 16)
                    if not last:
                        load_raw(n + 3, 1 - r, w_in_t, Q_COL + (p + 1) * P)

            with sp.Fori(0, PAIRS // 2 - 1) as i:
                for r in range(2):
                    load_pair(2 * i + r, i, r, False)
            for r in range(2):
                load_pair(PAIRS - 2 + r, PAIRS // 2 - 1, r, r == 1)
            with sp.Fori(0, KT // 2) as i:
                for b in range(2):
                    load_raw(N_YA + b + 2 * i, b, w_a_t, (2 * i + b) * P)
            def load_wo(s, signal):
                hf, kk = s // 4, s % 4
                sp.dma_start(wo_land(s)[:, :].rearrange("p (k c) -> p k c", k=2),
                             w_out_t[:, 2 * kk:2 * kk + 2, hf * HALF:(hf + 1) * HALF]).then_inc(signal, 16)

            for s in range(6):
                r = N_OUT + s
                sp.wait_ge(hi_done, r - 1)
                if s < 2:
                    sp.wait_ge(lo_done, r - 1)
                else:
                    wait_wo(sp, s - 2)
                load_wo(s, raw_in[r % 2])
                if s == 1:
                    sp.wait_ge(g_ready, 2 * KT)
                    for b in range(2):
                        load_wo(6 + b, wo_in[b])
            sp.wait_ge(acc_free[1], N_OUT // 2)
            sp.dma_start(buf_t[:, :], post_norm[0:1, :].to_broadcast([P, D_MODEL])).then_inc(post_in, 16)

            def load_res(t, b):
                sp.dma_start(x_r[b][:, :], x[0, bass.ds(t * P, P), :]).then_inc(xr_in[b], 16)

            def store(t, b):
                sp.wait_ge(y_ok, t + 1)
                sp.dma_start(out[0, bass.ds(t * P, P), :], (buf_a, buf_b)[b][:, :]).then_inc(y_out[b], 16)

            def store_last():
                for hf in range(2):
                    sp.wait_ge(y_ok, NT + hf)
                    cols = slice(hf * HALF, (hf + 1) * HALF)
                    sp.dma_start(out[0, SEQ - P:SEQ, cols], buf_b[:, cols]).then_inc(y_out[1], 16)

            for b in range(2):
                wait_wo(sp, 6 + b)
                load_res(b, b)
            with sp.Fori(0, NT // 2 - 1) as i:
                for b in range(2):
                    store(2 * i + b, b)
                    load_res(2 * i + b + 2, b)
            store(NT - 2, 0)
            store_last()
            sp.wait_ge(y_out[0], 16 * NT // 2)
            sp.wait_ge(y_out[1], 16 * (NT // 2 + 1))

        @block.tensor
        def _(pe):
            def products(b, lh, ll, rh, rl):
                ops = []
                for k in range(KT):
                    for l, r, kind in ((lh, rh, 0), (lh, rl, 1), (ll, rh, 2)):
                        for hf in range(2):
                            ops.append((acc[b][:, hf * HALF:(hf + 1) * HALF], l[:, k * P:(k + 1) * P],
                                        r[:, k * SEQ + hf * HALF:k * SEQ + (hf + 1) * HALF],
                                        k == 0 and kind == 0, k == KT - 1 and kind == 2))
                return ops

            def run(ops):
                last = None
                for o, l, r, a, z in ops:
                    last = nc.tensor.matmul(o, l, r, start=a, stop=z, skip_group_check=True)
                return last

            def start_unit(n, hn, b):
                pe.wait_ge(lo_done, n + 1)
                pe.wait_ge(acc_free[b], hn)

            def unit(n, hn, b, rh, rl):
                start_unit(n, hn, b)
                run(products(b, w_hi[b], w_lo[b], rh, rl)).then_inc(unit_done, 1)

            def transpose_h(t, b):
                pe.wait_ge(h_ok, t + 1)
                for k in range(KT):
                    last = nc.tensor.transpose(ps_t[:, k * P:(k + 1) * P], x_b[b][:, k * P:(k + 1) * P], ident[:, :])
                last.then_inc(tr_done, 1)

            def mix(t, after_first=True):
                pe.wait_ge(vnl_ok, t + 1)
                if after_first:
                    pe.wait_ge(mix_ok, t)
                for g in range(KT):
                    c = slice(g * P, (g + 1) * P)
                    o = (ps_m, ps_t)[g // 4][:, g % 4 * 2 * P:(g % 4 + 1) * 2 * P]
                    nc.tensor.matmul(o, vn_hi[:, c], ws_st[:, g * 2 * P:(g + 1) * 2 * P], start=True, stop=False,
                                     skip_group_check=True)
                    last = nc.tensor.matmul(o[:, 0:P], vn_lo[:, c], ws_st[:, g * 2 * P:g * 2 * P + P], start=False, stop=True,
                                            skip_group_check=True)
                last.then_inc(mix_done, 1)

            def vb_unit(t, b, mixes=True, more=True, first_mix=False):
                pe.wait_ge(hs_lo, t + 1)
                ops = products(b, w_hi[b], w_lo[b], g_hi, g_lo)
                run(ops[:12])
                if mixes:
                    mix(t - 2, not first_mix)
                cut = 26 if mixes else 38
                run(ops[12:cut])
                if more:
                    if mixes:
                        pe.wait_ge(mix_ok, t - 1)
                    transpose_h(t + 1, 1 - b)
                run(ops[cut:]).then_inc(unit_done, 1)

            def unit_with_mix(n, b, t):
                start_unit(n, half(n), b)
                ops = products(b, w_hi[b], w_lo[b], ht_hi, ht_lo)
                run(ops[:12])
                mix(t)
                run(ops[12:]).then_inc(unit_done, 1)

            pe.wait_ge(const_ok, 1)
            for _ in range(WARM_UP):
                nc.tensor.transpose(acc[0][:, 0:P], ident[:, :], ident[:, :])
            transpose_h(0, 0)
            pe.wait_ge(wsp_ok, 1)
            for g in range(KT):
                c = slice(g * P, (g + 1) * P)
                last = nc.tensor.transpose(ps_m[:, c], buf_b[:, c], ident[:, :])
            last.then_inc(tr_done, 1)
            pe.wait_ge(hs_lo, 1)
            ops = products(0, w_hi[0], w_lo[0], g_hi, g_lo)
            for k in range(KT):
                wait_vb_lo(pe, k)
                last = run(ops[6 * k:6 * k + 6])
                if k == 3:
                    transpose_h(1, 1)
            last.then_inc(unit_done, 1)
            vb_unit(1, 1, mixes=False)
            pe.wait_ge(wsl_ok, 1)
            vb_unit(2, 0, first_mix=True)
            with pe.Fori(1, NT // 2 - 1) as i:
                for b in (1, 0):
                    vb_unit(2 * i + 2 - b, b)
            vb_unit(NT - 1, 1, more=False)
            for b in range(2):
                pe.wait_ge(ht_in[b], 16 * NT)
            unit_with_mix(N_U, 0, NT - 2)
            unit_with_mix(N_U + 1, 1, NT - 1)
            with pe.Fori(1, KT) as g:
                for b in range(2):
                    unit(N_U + b + 2 * g, half(N_U, g, 2), b, ht_hi, ht_lo)
            with pe.Fori(0, KT) as j:
                unit(N_MB + 2 * j, half(N_MB, j, 2), 0, ht_hi, ht_lo)
                pe.wait_ge(g_ready, KT)
                unit(N_MB + 1 + 2 * j, half(N_MB, j, 2), 1, g_hi, g_lo)
            unit(N_KVU, half(N_KVU), 0, ht_hi, ht_lo)
            unit(N_KVU + 1, half(N_KVU), 1, ht_hi, ht_lo)
            start_unit(N_ATT, half(N_ATT), 0)
            ops = products(0, w_hi[0], w_lo[0], ht_hi, ht_lo)
            run(ops[:12])
            pe.wait_ge(acc_free[1], half(N_KVU) + 1)
            pe.wait_ge(mix_ok, NT)
            for t in range(NT):
                last = nc.tensor.transpose(ps_m[:, t * P:(t + 1) * P], buf_b[:, t * P:(t + 1) * P], ident[:, :])
            last.then_inc(vt_done, 1)
            run(ops[12:]).then_inc(unit_done, 1)

            def pair(kv, p, i, c, r, final=False):
                q_rows = half(c, i, 6) + 1

                def scores(blk):
                    s = 8 * p + blk
                    if blk == 0:
                        pe.wait_ge(acc_free[r], q_rows)
                    pe.wait_ge(scores_used, s + 1)
                    lo = P if blk == 0 else 0
                    kc = kv * SEQ + (blk - 1) * P
                    for h in range(2):
                        for kbuf, a in ((k_hi, True), (k_lo, False)):
                            last = nc.tensor.matmul(ps_s[:, h * 256 + lo:(h + 1) * 256], q_st[h][:, blk * P:(blk + 1) * P],
                                                    kbuf[:, kc + lo:kc + 256], start=a, stop=not a, skip_group_check=True)
                    last.then_inc(scores_ok, 1)

                def transpose_p(blk):
                    s = 8 * p + blk
                    pe.wait_ge(prob_ok, s + 1)
                    if blk > 0:
                        pe.wait_ge(ptl_ok, s)
                    for h in range(2):
                        c = slice(h * P, (h + 1) * P)
                        last = nc.tensor.transpose(ps_p[:, c], prob[blk % 3][:, c], ident[:, :])
                    last.then_inc(pt_done, 1)

                def values(blk):
                    pe.wait_ge(pt_ok, 8 * p + blk + 1)
                    if blk in (4, 6):
                        pe.wait_ge(oadd_ok, 4 * p + blk // 2 - 1)
                    o = ps_m[:, (blk // 2 % 2) * 512:(blk // 2 % 2 + 1) * 512].rearrange(
                        "p (h c) -> p h c", h=2)[:, :, (blk % 2) * P:(blk % 2 + 1) * P]
                    kbs = (1,) if blk == 0 else (0, 1)
                    for kb in kbs:
                        v0 = (kv * NT + blk - 1 + kb) * P
                        for x in range(2):
                            c0 = (2 * kb + x) * 256
                            last = nc.tensor.matmul(o, v_st[:, v0:v0 + P],
                                                    pt[blk % 2][:, c0:c0 + 256].rearrange("p (h c) -> p h c", h=2),
                                                    start=(kb == kbs[0] and x == 0), stop=(kb == 1 and x == 1),
                                                    skip_group_check=True)
                    if blk % 2:
                        last.then_inc(pv_done, 1)

                def slot(k):
                    if 4 <= k:
                        values(k - 4)
                    if 2 <= k < 10:
                        transpose_p(k - 2)
                    if k < 8:
                        scores(k)

                def beside(ops, m0):
                    for m, op in enumerate(ops, m0):
                        if m >= FIRST_SLOT and (m - FIRST_SLOT) % SLOT_STEP == 0 and m < FIRST_SLOT + SLOTS * SLOT_STEP:
                            slot((m - FIRST_SLOT) // SLOT_STEP)
                        last = run([op])
                    return last

                n0 = c + 6 * i
                ops_a = products(1 - r, w_hi[1 - r], w_lo[1 - r], ht_hi, ht_lo)
                ops_m = products(r, w_hi[r], w_lo[r], ht_hi, ht_lo)
                start_unit(n0 + 1, half(c + 1, i, 6), 1 - r)
                beside(ops_a, 0).then_inc(unit_done, 1)
                start_unit(n0 + 2, half(c + 2, i, 6), r)
                beside(ops_m, UNIT).then_inc(unit_done, 1)
                if not final:
                    start_unit(n0 + 3, half(c + 3, i, 6), 1 - r)
                    beside(ops_a, 2 * UNIT).then_inc(unit_done, 1)
                else:
                    ya = [products(j, w_hi[j], w_lo[j], g_hi, g_lo) for j in range(2)]
                    start_unit(N_YA, half(N_YA), 0)
                    pe.wait_ge(g_ready, 2 * KT - 1)
                    beside(ya[0][:-6], 2 * UNIT)
                    start_unit(N_YA + 1, half(N_YA), 1)
                    beside(ya[1][:32], 3 * UNIT - 6)
                    pe.wait_ge(g_ready, 2 * KT)
                    run(ya[0][-6:]).then_inc(unit_done, 1)
                    run(ya[1][32:]).then_inc(unit_done, 1)

            pe.wait_ge(klo_ok, 1)
            with pe.Fori(0, PAIRS_PER_KV // 2) as i:
                for r in range(2):
                    pair(0, 2 * i + r, i, N_ATT + 3 * r, r)
            with pe.Fori(PAIRS_PER_KV // 2, PAIRS // 2 - 1) as i:
                for r in range(2):
                    pair(1, 2 * i + r, i, N_ATT + 3 * r, r)
            for r in range(2):
                pair(1, PAIRS - 2 + r, PAIRS // 2 - 1, N_ATT + 3 * r, r, final=(r == 1))
            with pe.Fori(1, KT // 2) as i:
                for b in range(2):
                    unit(N_YA + b + 2 * i, half(N_YA, i, 2), b, g_hi, g_lo)

            def out_half(t, b, hf, ks=range(KT), first=False):
                rh, rl = ((wo_hi, wo_lo) if hf == 0 else (g_hi[:, 0:KT * HALF], g_hi[:, KT * HALF:2 * KT * HALF]))
                for k in ks:
                    if first and k % 2 == 0:
                        wait_wo(pe, 4 * hf + k // 2)
                    for l, r, kind in ((w_hi[b], rh, 0), (w_hi[b], rl, 1), (w_lo[b], rh, 2)):
                        last = nc.tensor.matmul(acc[b][:, hf * HALF:(hf + 1) * HALF], l[:, k * P:(k + 1) * P],
                                                r[:, k * HALF:(k + 1) * HALF], start=(k == 0 and kind == 0),
                                                stop=(k == KT - 1 and kind == 2), skip_group_check=True)
                return last

            def out_start(n_copies, ht, b):
                pe.wait_ge(mt_hi, n_copies)
                pe.wait_ge(mt_lo, n_copies)
                pe.wait_ge(acc_free[b], half(N_OUT, ht, 2))

            out_start(1, 0, 0)
            out_half(0, 0, 0, range(KT - 1), first=True)
            out_start(2, 0, 1)
            out_half(1, 1, 0, range(KT - 1))
            for b in range(2):
                pe.wait_ge(mt_hi, 3 + b)
                pe.wait_ge(mt_lo, 3 + b)
                out_half(b, b, 0, (KT - 1,))
            out_half(0, 0, 1, first=True).then_inc(unit_done, 1)
            out_half(1, 1, 1).then_inc(unit_done, 1)
            with pe.Fori(1, NT // 2 - 1) as i:
                for b in range(2):
                    out_start(2 * i + b + 3, i, b)
                    out_half(2 * i + b, b, 0)
                    out_half(2 * i + b, b, 1).then_inc(unit_done, 1)
            for b in range(2):
                t = NT - 2 + b
                out_start(t + 3, NT // 2 - 1, b)
                last = out_half(t, b, 0)
                if b:
                    last.then_inc(half_done, 1)
                out_half(t, b, 1).then_inc(unit_done, 1)

        @block.scalar
        def _(act):
            def split_hi(n, hn, b, dst=None):
                act.wait_ge(raw_in[b], 16 * (hn + 1 - N_U // 2))
                act.wait_ge(unit_done, n - 1)
                nc.scalar.activation(w_hi[b][:, :] if dst is None else dst, raw[b][:, :], ACT.Copy).then_inc(hi_done, 1)

            def vb_hi(k):
                act.wait_ge(vb_in[k % 4], 16 * (k // 4 + 1))
                nc.scalar.activation(tile(g_hi, k), land[k % 4][:, :], ACT.Copy).then_inc(hi_done, 1)

            def square_x(t, ht, b):
                act.wait_ge(x_in[b], 16 * (ht + 1))
                nc.scalar.activation(junk[:, :], x_b[b][:, :], ACT.Square, accum_out=ssq[:, b:b + 1]).then_inc(ssq_ok, 1)

            def h_hi(t, n_tr, b):
                act.wait_ge(tr_done, n_tr)
                nc.scalar.activation(w_hi[b][:, :], ps_t[:, :], ACT.Copy).then_inc(hs_hi, 1)

            def gelu_v(t, b):
                act.wait_ge(unit_done, t + 1)
                nc.scalar.activation(v_buf[b][:, :], acc[b][:, :], ACT.Gelu).then_inc(acc_free[b], 1)

            def mix_copy(t, ht, b):
                act.wait_ge(mix_done, t + 1)
                act.wait_ge(mix_out[b], 16 * (ht + 1))
                for q, ps in enumerate((ps_m, ps_t)):
                    last = nc.scalar.activation(mix_b[b][:, q * HALF:(q + 1) * HALF].rearrange("p (g t) -> p g t", g=4),
                                                ps[:, :].rearrange("p (g x t) -> p g x t", g=4, x=2)[:, :, 1, :], ACT.Copy)
                last.then_inc(mix_lo_out, 1)

            def vn_split(t, b):
                act.wait_ge(vn_ok, t + 1)
                nc.scalar.activation(vn_hi[:, :], v_buf[b][:, :], ACT.Copy).then_inc(vnh_ok, 1)

            for b in range(2):
                act.sem_inc(mix_out[b], 16)
            act.sem_inc(spill_out, 16)
            act.sem_inc(lo_done, N_U)
            square_x(0, 0, 0)
            vb_hi(0)
            h_hi(0, 1, 0)
            vb_hi(1)
            vb_hi(2)
            vb_hi(3)
            square_x(1, 0, 1)
            for k in range(4, KT):
                vb_hi(k)
            h_hi(1, 3, 1)
            nc.scalar.activation(ws4[:, :, 0, :], ps_m[:, :].rearrange("p (g t) -> p g t", g=KT), ACT.Copy).then_inc(wsh_ok, 1)
            wait_vb_lo(act, KT - 1)
            wait_vb_lo(act, KT - 2)
            gelu_v(0, 0)
            def step(t, ht, b, mixes=True):
                square_x(t + 1, ht + 1, 1 - b)
                if mixes:
                    mix_copy(t - 2, ht - b, b)
                act.wait_ge(ht_in[1 - b], 32 * (ht + 1))
                h_hi(t + 1, t + 3, 1 - b)
                vn_split(t - 1, 1 - b)
                if mixes:
                    act.wait_ge(vnl_ok, t - 1)
                gelu_v(t, b)

            step(1, 0, 1, mixes=False)
            step(2, 0, 0)
            with act.Fori(1, NT // 2 - 1) as i:
                for b in (1, 0):
                    step(2 * i + 2 - b, i, b)
            mix_copy(NT - 3, NT // 2 - 2, 1)
            act.wait_ge(ht_in[0], 16 * NT)
            split_hi(N_U, half(N_U), 0)
            vn_split(NT - 2, 0)
            act.wait_ge(vnl_ok, NT - 2)
            gelu_v(NT - 1, 1)
            act.wait_ge(ht_in[1], 16 * NT)
            split_hi(N_U + 1, half(N_U + 1), 1)
            mix_copy(NT - 2, NT // 2 - 1, 0)
            vn_split(NT - 1, 1)
            act.wait_ge(vnl_ok, NT)
            mix_copy(NT - 1, NT // 2 - 1, 1)

            with act.Fori(0, KT) as g:
                n = N_U + 2 * g
                act.wait_ge(unit_done, n + 1)
                nc.scalar.activation(buf_a[:, :], acc[0][:, :], ACT.Gelu).then_inc(acc_free[0], 1)
                split_hi(n + 2, half(N_U + 2, g, 2), 0)
                act.wait_ge(unit_done, n + 2)
                act.wait_ge(um_ok, g + 1)
                nc.scalar.activation(buf_t[:, :], acc[1][:, :], ACT.Tanh, scale=0.5).then_inc(gate_t_ok, 1)
                split_hi(n + 3, half(N_U + 3, g, 2), 1)
                act.wait_ge(prod_ok, g + 1)
                nc.scalar.activation(tile(g_hi, g), buf_t[:, :], ACT.Copy).then_inc(ghi_ok, 1)
            act.wait_ge(g_ready, KT)
            with act.Fori(0, KT) as j:
                n = N_MB + 2 * j
                act.wait_ge(unit_done, n + 1)
                act.wait_ge(acc_free[1], half(N_MB, j, 2))
                nc.scalar.activation(buf_t[:, :], acc[0][:, :], ACT.Tanh, scale=0.5).then_inc(acc_free[0], 1)
                split_hi(n + 2, half(N_MB + 2, j, 2), 0)
                split_hi(n + 3, half(N_MB + 3, j, 2), 1)
                act.wait_ge(acc_free[1], half(N_MB + 2, j, 2))
                act.dma_start(acc_d[bass.ds(j, 1), :, :].rearrange("a p s -> p (a s)"), buf_a[:, :]).then_inc(spill_out, 16)
            act.wait_ge(unit_done, N_KVU + 1)
            act.wait_ge(spill_out, 16 * (1 + KT))
            nc.scalar.activation(buf_a[:, :], acc[0][:, :], ACT.Copy).then_inc(acc_free[0], 1)
            split_hi(N_ATT, half(N_ATT), 0)
            act.wait_ge(acc_free[0], half(N_KVU) + 1)
            for kv in range(N_KV):
                rows = slice(kv * HEAD_DIM, (kv + 1) * HEAD_DIM)
                for hf in range(2):
                    last = nc.scalar.activation(k_hi[hf * HEAD_DIM:(hf + 1) * HEAD_DIM, kv * SEQ:(kv + 1) * SEQ],
                                                buf_a[rows, :], ACT.Copy)
            last.then_inc(khi_ok, 1)
            act.wait_ge(unit_done, N_KVU + 2)
            nc.scalar.activation(buf_b[:, :], acc[1][:, :], ACT.Copy).then_inc(acc_free[1], 1)
            split_hi(N_ATT + 1, half(N_ATT + 1), 1)

            def q_split(p, n0, hn, r):
                act.wait_ge(unit_done, n0 + 1)
                nc.scalar.activation(q_st[0][0:64, :], acc[r][0:64, :], ACT.Copy).then_inc(q_hi_ok, 1)
                nc.scalar.activation(q_st[1][64:128, :], acc[r][64:128, :], ACT.Copy).then_inc(q_hi_ok, 1)
                split_hi(n0 + 2, hn, r)

            act.wait_ge(vt_done, 1)
            for kv in range(N_KV):
                last = nc.scalar.activation(
                    v_st[:, :].rearrange("p (v t x d) -> p v t x d", v=N_KV, t=NT, x=2)[:, kv, :, 0, :],
                    ps_m[:, :].rearrange("p (t v d) -> p t v d", t=NT, v=N_KV)[:, :, kv, :], ACT.Copy)
            last.then_inc(vhi_ok, 1)
            q_split(0, N_ATT, half(N_ATT + 2), 0)

            def split_hi_half(n, hn, b, hf):
                if hf == 0:
                    act.wait_ge(raw_in[b], 16 * (hn + 1 - N_U // 2))
                    act.wait_ge(unit_done, n - 1)
                hs = slice(hf * HALF, (hf + 1) * HALF)
                last = nc.scalar.activation(w_hi[b][:, hs], raw[b][:, hs], ACT.Copy)
                if hf == 1:
                    last.then_inc(hi_done, 1)

            def pair(p, i, c, r, final=False):
                n0 = c + 6 * i
                for k in range(13):
                    if k == 3:
                        act.wait_ge(unit_done, n0 + 2)
                        act.wait_ge(spill_out, 16 * (1 + KT) + 16 * p)
                        nc.scalar.activation(buf_t[:, :], acc[1 - r][:, :], ACT.Tanh, scale=0.5).then_inc(gtan_ok, 1)
                    if k == 8:
                        act.wait_ge(unit_done, n0 + 3)
                        act.wait_ge(acc_free[1 - r], half(c + 1, i, 6) + 1)
                        nc.scalar.activation(buf_t[:, :], acc[r][:, :], ACT.Tanh, scale=0.5).then_inc(acc_free[r], 1)
                    if 2 <= k < 10:
                        s = 8 * p + k - 2
                        act.wait_ge(pt_done, s + 1)
                        if k > 2:
                            act.wait_ge(pt_ok, s)
                        nc.scalar.activation(pt_packed[:, 0:256], ps_p, ACT.Copy).then_inc(pth_ok, 1)
                    if k >= 6 and k % 2 == 0:
                        g = (k - 6) // 2
                        gg = 4 * p + g
                        act.wait_ge(pv_done, gg + 1)
                        if g >= 2:
                            act.wait_ge(oadd_ok, gg - 1)
                        o = ps_m[:, (g % 2) * 512:(g % 2 + 1) * 512]
                        nc.scalar.activation(o_tmp[g % 2][0:64, :], o[64:128, 0:256], ACT.Copy)
                        nc.scalar.activation(o_tmp[g % 2][64:128, :], o[0:64, 256:512], ACT.Copy).then_inc(otmp_ok, 1)
                    if k < 8:
                        s = 8 * p + k
                        act.wait_ge(max_ok, s + 1)
                        for h in range(2):
                            w = prob[k % 3][:, h * P:(h + 1) * P]
                            nc.scalar.activation(w, w, ACT.Exp, bias=neg_max[:, 2 * k + h:2 * k + h + 1],
                                                 accum_out=row_sum[:, 2 * k + h:2 * k + h + 1])
                        nc.scalar.activation(sink_e[:, 2 * k:2 * k + 2], sink_d[:, 2 * k:2 * k + 2], ACT.Exp).then_inc(exp_ok, 1)
                    if k in (3, 4):
                        split_hi_half(n0 + 3, half(c + 3, i, 6), 1 - r, k - 3)
                    if k == 8:
                        split_hi(n0 + 4, half(c + 4, i, 6), r)
                if not final:
                    q_split(p + 1, n0 + 3, half(c + 5, i, 6), 1 - r)
                act.wait_ge(og_ok, p + 1)
                nc.scalar.activation(tile(g_hi, p), buf_b[:, :], ACT.Copy).then_inc(ghi_ok, 1)
                act.wait_ge(siga_ok, p + 1)
                act.dma_start(sig_d[bass.ds(p, 1), :, :].rearrange("a p s -> p (a s)"), buf_t[:, :]).then_inc(spill_out, 16)

            with act.Fori(0, PAIRS // 2 - 1) as i:
                for r in range(2):
                    pair(2 * i + r, i, N_ATT + 3 * r, r)
            for r in range(2):
                pair(PAIRS - 2 + r, PAIRS // 2 - 1, N_ATT + 3 * r, r, final=(r == 1))

            def load_merge(j):
                act.dma_start(buf_t[:, :], sig_d[bass.ds(j, 1), :, :].rearrange("a p s -> p (a s)")).then_inc(sigr_in, 16)
                act.dma_start(buf_a[:, :], acc_d[bass.ds(j, 1), :, :].rearrange("a p s -> p (a s)")).then_inc(accr_in, 16)

            def merged_hi(j):
                act.wait_ge(mrg_ok, j + 1)
                nc.scalar.activation(tile(ht_hi, j), buf_b[:, :], ACT.Copy).then_inc(mhi_ok, 1)

            act.wait_ge(spill_out, 16 * (1 + KT + PAIRS))
            act.wait_ge(g_ready, 2 * KT)
            load_merge(0)
            with act.Fori(0, KT // 2 - 1) as i:
                for b in range(2):
                    j = 2 * i + b
                    split_hi(N_YA + b + 2 + 2 * i, half(N_YA + 2, i, 2), b)
                    merged_hi(j)
                    act.wait_ge(g_ready, 2 * KT + j + 1)
                    load_merge(j + 1)

            def split_out(s):
                r = N_OUT + s
                if s < 6:
                    act.wait_ge(raw_in[r % 2], 16 * (r // 2 + 1 - N_U // 2))
                else:
                    act.wait_ge(wo_in[s - 6], 16)
                if s >= 4:
                    act.wait_ge(unit_done, N_OUT)
                nc.scalar.activation(tile(wo_hi if s < 4 else g_hi, s % 4), wo_land(s)[:, :], ACT.Copy).then_inc(hi_done, 1)

            def tile_hi(t, b, k0=0, k1=KT):
                act.wait_ge(unit_done, N_OUT + t - 1)
                nc.scalar.activation(w_hi[b][:, k0 * P:k1 * P].rearrange("p (k s) -> p k s", k=k1 - k0),
                                     ht_hi[:, :].bitcast(f32).rearrange("p (k s) -> p k s", k=KT)[:, k0:k1, bass.ds(t * P, P)],
                                     ACT.Copy).then_inc(mt_hi, 1)

            split_out(0)
            split_out(1)
            merged_hi(KT - 2)
            act.wait_ge(g_ready, 3 * KT - 1)
            load_merge(KT - 1)
            split_out(2)
            split_out(3)
            act.wait_ge(mhi_ok, KT - 1)
            tile_hi(0, 0, 0, KT - 1)
            tile_hi(1, 1, 0, KT - 1)
            merged_hi(KT - 1)

            def square_out(t, b, cols=slice(0, D_MODEL), acc_to=None):
                nc.scalar.activation(junk[:, cols], acc[b][:, cols], ACT.Square,
                                     accum_out=ssq[:, b:b + 1] if acc_to is None else acc_to).then_inc(osq_ok, 1)

            act.wait_ge(mhi_ok, KT)
            tile_hi(0, 0, KT - 1, KT)
            tile_hi(1, 1, KT - 1, KT)
            for s in range(4, 8):
                split_out(s)
            with act.Fori(0, NT // 2 - 1) as i:
                for b in range(2):
                    t = 2 * i + b
                    act.wait_ge(mt_hi, t + 4)
                    act.wait_ge(unit_done, N_OUT + t + 1)
                    square_out(t, b)
                    tile_hi(t + 2, b)
            act.wait_ge(osq_ok, NT - 2)
            act.wait_ge(unit_done, N_OUT + NT - 1)
            square_out(NT - 2, 0)
            for hf in range(2):
                act.wait_ge(osq_ok, NT - 1 + hf)
                if hf == 0:
                    act.wait_ge(half_done, 1)
                else:
                    act.wait_ge(unit_done, N_OUT + NT)
                square_out(NT - 1, 1, slice(hf * HALF, (hf + 1) * HALF), ssq_h[:, hf:hf + 1])

        @block.gpsimd
        def _(pool):
            def split_lo(n, b):
                pool.wait_ge(hi_done, n + 1)
                nc.gpsimd.tensor_tensor(w_lo[b][:, :], raw[b][:, :], w_hi[b][:, :].bitcast(f32), ALU.subtract).then_inc(lo_done, 1)

            def split_lo_to(n, src, dst, hi):
                pool.wait_ge(hi_done, n + 1)
                nc.gpsimd.tensor_tensor(dst, src[:, :], hi.bitcast(f32), ALU.subtract).then_inc(lo_done, 1)

            def rsqrt_h(t, b):
                pool.wait_ge(msq_ok, t + 1)
                nc.gpsimd.tensor_tensor(rstd[:, b:b + 1], msq[:, b:b + 1], neg_half[:, :], ALU.pow).then_inc(rstd_ok, 1)

            def rsqrt_ln(t):
                pool.wait_ge(var_ok, t + 1)
                nc.gpsimd.tensor_tensor(ln_rstd[:, :], var_eps[:, :], neg_half[:, :], ALU.pow).then_inc(lnr_ok, 1)

            def mix_bias(t, b):
                pool.wait_ge(mix_ok, t + 1)
                nc.gpsimd.tensor_tensor(mix_b[b][:, :], mix_b[b][:, :], bs_b[:, :], ALU.add).then_inc(mix_biased, 1)

            def vn_low(t, b):
                pool.wait_ge(vnh_ok, t + 1)
                nc.gpsimd.tensor_tensor(vn_lo[:, :], v_buf[b][:, :], vn_hi[:, :].bitcast(f32), ALU.subtract).then_inc(vnl_ok, 1)

            nc.gpsimd.memset(neg_half[:, :], -0.5).then_inc(pool_own, 1)
            nc.gpsimd.memset(ident[:, :], 0.0).then_inc(pool_own, 1)
            pool.wait_ge(pool_own, 2)
            nc.gpsimd.affine_select(out=ident[:, :], in_=ident[:, :], compare_op=ALU.not_equal, fill=1.0, base=0,
                                    pattern=[[-1, P]], channel_multiplier=1).then_inc(const_ok, 1)
            rsqrt_h(0, 0)
            pool.wait_ge(wsp_in, 16)
            nc.gpsimd.affine_select(out=buf_b[:, :].rearrange("p (g s) -> p g s", g=KT),
                                    in_=buf_b[:, :].rearrange("p (g s) -> p g s", g=KT), compare_op=ALU.is_ge, fill=0.0,
                                    base=0, pattern=[[0, KT], [-1, P]], channel_multiplier=1).then_inc(wsp_ok, 1)
            def vb_lo(k):
                pool.wait_ge(hi_done, k + 1)
                nc.gpsimd.tensor_tensor(tile(g_lo, k), land[k % 4][:, :], tile(g_hi, k).bitcast(f32), ALU.subtract).then_inc(vb_lo_pool, 1)

            rsqrt_h(1, 1)
            vb_lo(vb_by_pool[0])
            pool.wait_ge(bs_in, 16)

            def step(t, b, mixes=True):
                rsqrt_ln(t - 1)
                rsqrt_h(t + 1, 1 - b)
                if mixes:
                    mix_bias(t - 2, b)
                vn_low(t - 1, 1 - b)

            step(1, 1, mixes=False)
            step(2, 0)
            with pool.Fori(1, NT // 2 - 1) as i:
                for b in (1, 0):
                    step(2 * i + 2 - b, b)
            rsqrt_ln(NT - 2)
            split_lo(N_U, 0)
            vn_low(NT - 2, 0)
            mix_bias(NT - 3, 1)
            rsqrt_ln(NT - 1)
            split_lo(N_U + 1, 1)
            vn_low(NT - 1, 1)
            mix_bias(NT - 2, 0)
            mix_bias(NT - 1, 1)
            for b in range(2):
                split_lo(N_U + 2 + b, b)
            nc.gpsimd.memset(before[:, :], 1.0).then_inc(pool_own, 1)
            pool.wait_ge(pool_own, 3)
            nc.gpsimd.affine_select(out=before[:, :].rearrange("p (h j) -> p h j", h=2),
                                    in_=before[:, :].rearrange("p (h j) -> p h j", h=2), compare_op=ALU.is_ge, fill=0.0,
                                    base=-1, pattern=[[0, 2], [1, P]], channel_multiplier=-1).then_inc(before_ok, 1)
            pool.wait_ge(rel_in, 16)
            nc.gpsimd.memset(bias_row[:, :], NEG_INF / HEAD_DIM ** -0.5).then_inc(pool_own, 1)
            pool.wait_ge(pool_own, 4)
            for bucket, d0, d1 in bucket_runs():
                last = nc.gpsimd.tensor_scalar(bias_row[:, 2 * P - d1:2 * P - d0],
                                               rel_t[:, bucket:bucket + 1].to_broadcast([N_HEADS, d1 - d0]),
                                               1.0 / HEAD_DIM ** -0.5, 1.0, ALU.mult, ALU.mult)
            last.then_inc(bias_made, 1)
            with pool.Fori(N_U // 2 + 1, N_ATT // 2 - 1) as h:
                for b in range(2):
                    split_lo(2 * h + 2 + b, b)
            split_lo(N_ATT, 0)
            split_lo(N_ATT + 1, 1)


            def pair(p, i, c, r, final=False):
                n0 = c + 6 * i
                for k in range(1, 10):
                    if k < 9:
                        pool.wait_ge(inv_ok, 8 * p + k)
                        stand_alone(pool)
                        for h in range(2):
                            w = prob[(k - 1) % 3][:, h * P:(h + 1) * P]
                            last = nc.gpsimd.tensor_scalar(w, w, inv_den[:, 2 * k - 2 + h:2 * k - 1 + h], 0.5, ALU.mult, ALU.mult)
                        last.then_inc(prob_ok, 1)
                    if k >= 2:
                        blk = k - 2
                        pool.wait_ge(ptl_ok, 8 * p + blk + 1)
                        stand_alone(pool)
                        for kb, first, step in ((0, -1, -1), (1, 0, 1)):
                            if kb == 0 and blk == 0:
                                continue
                            last = nc.gpsimd.affine_select(
                                out=pt[blk % 2][:, kb * 512:(kb + 1) * 512].rearrange("p (y q) -> p y q", y=4),
                                in_=pt_packed[:, :].rearrange("p (y q) -> p y q", y=4), compare_op=ALU.is_ge, fill=0.0,
                                base=first, pattern=[[0, 4], [step, P]], channel_multiplier=-step)
                        last.then_inc(pt_ok, 1)
                    if k == 1:
                        split_lo(n0 + 2, r)
                    if k == 5:
                        split_lo(n0 + 3, 1 - r)
                    if k == 8:
                        split_lo(n0 + 4, r)
                    if k == 9:
                        pool.wait_ge(acc_free[r], half(c + 2, i, 6) + 1)
                        stand_alone(pool)
                        nc.gpsimd.tensor_scalar(buf_t[:, :], buf_t[:, :], 0.5, 0.5, ALU.mult, ALU.add).then_inc(siga_ok, 1)
                if not final:
                    pool.wait_ge(oadd_ok, 4 * p + 4)
                    nc.gpsimd.tensor_tensor(buf_b[:, :], buf_b[:, :], buf_a[:, :], ALU.mult).then_inc(og_ok, 1)
                    pool.wait_ge(ghi_ok, KT + p + 1)
                    nc.gpsimd.tensor_tensor(tile(g_lo, p), buf_b[:, :], tile(g_hi, p).bitcast(f32), ALU.subtract).then_inc(g_ready, 1)

            with pool.Fori(0, PAIRS // 2 - 1) as i:
                for r in range(2):
                    pair(2 * i + r, i, N_ATT + 3 * r, r)
            for r in range(2):
                pair(PAIRS - 2 + r, PAIRS // 2 - 1, N_ATT + 3 * r, r, final=(r == 1))
            with pool.Fori(0, KT // 2 - 1) as i:
                for b in range(2):
                    split_lo(N_YA + 2 + b + 2 * i, b)

            def split_out(s):
                r = N_OUT + s
                if s < 4:
                    split_lo_to(r, wo_land(s), tile(wo_lo, s), tile(wo_hi, s))
                else:
                    split_lo_to(r, wo_land(s), tile(g_hi, s), tile(g_hi, s - 4))

            for s in range(4):
                split_out(s)

            def rsqrt_out(t, b):
                pool.wait_ge(oms_ok, t + 1)
                nc.gpsimd.tensor_tensor(rstd[:, b:b + 1], msq[:, b:b + 1], neg_half[:, :], ALU.pow).then_inc(ors_ok, 1)

            for s in (4, 6):
                split_out(s)
            with pool.Fori(0, NT // 2) as i:
                for b in range(2):
                    rsqrt_out(2 * i + b, b)

        @block.vector
        def _(dve):
            own = Chain(dve, dve_own)

            def mean_sq(t, b):
                dve.wait_ge(ssq_ok, t + 1)
                nc.vector.tensor_scalar(msq[:, b:b + 1], ssq[:, b:b + 1], 1.0 / D_MODEL, EPS, ALU.mult, ALU.add).then_inc(msq_ok, 1)

            def norm_h(t, b):
                dve.wait_ge(rstd_ok, t + 1)
                nc.vector.scalar_tensor_tensor(out=x_b[b][:, :], in0=x_b[b][:, :], scalar=rstd[:, b:b + 1],
                                               in1=pre_b[:, :], op0=ALU.mult, op1=ALU.mult).then_inc(h_ok, 1)

            def h_lo(t, b):
                dve.wait_ge(hs_hi, t + 1)
                nc.vector.tensor_tensor(w_lo[b][:, :], ps_t[:, :], w_hi[b][:, :].bitcast(f32), ALU.subtract).then_inc(hs_lo, 1)

            def mix_read(t, b):
                dve.wait_ge(mix_lo_out, t + 1)
                for q, ps in enumerate((ps_m, ps_t)):
                    part = mix_b[b][:, q * HALF:(q + 1) * HALF].rearrange("p (g t) -> p g t", g=4)
                    last = nc.vector.tensor_tensor(part, ps[:, :].rearrange("p (g x t) -> p g x t", g=4, x=2)[:, :, 0, :],
                                                   part, ALU.add)
                last.then_inc(mix_ok, 1)

            def ln_stats(ht, b):
                dve.wait_ge(acc_free[b], ht + 1)
                for hf in range(2):
                    last = nc.vector.bn_stats(bn6[:, 6 * hf:6 * hf + 6], v_buf[b][:, hf * HALF:(hf + 1) * HALF])
                own.link(last)
                stand_alone(dve)
                own.link(nc.vector.bn_aggr(mean_var[:, :], bn6[:, :].rearrange("p (a s) -> p a s", s=6)))
                nc.vector.tensor_scalar(var_eps[:, :], mean_var[:, 1:2], EPS, None, ALU.add).then_inc(var_ok, 1)

            def ln_apply(t, b):
                v = v_buf[b]
                dve.wait_ge(lnr_ok, t + 1)
                own.link(nc.vector.tensor_scalar(v[:, :], v[:, :], mean_var[:, 0:1], ln_rstd[:, 0:1],
                                                 ALU.subtract, ALU.mult))
                own.link(nc.vector.tensor_tensor(v[:, :], v[:, :], lng_b[:, :], ALU.mult))
                nc.vector.tensor_tensor(v[:, :], v[:, :], lnb_b[:, :], ALU.add).then_inc(vn_ok, 1)

            LN_LINKS = 4
            def vb_lo(k):
                dve.wait_ge(hi_done, k + 1)
                nc.vector.tensor_tensor(tile(g_lo, k), land[k % 4][:, :], tile(g_hi, k).bitcast(f32), ALU.subtract).then_inc(vb_lo_dve, 1)

            def step(t, ht, b, mixes=True):
                ln_stats(ht, 1 - b)
                mean_sq(t + 1, 1 - b)
                norm_h(t + 1, 1 - b)
                if mixes:
                    mix_read(t - 2, b)
                ln_apply(t - 1, 1 - b)
                h_lo(t + 1, 1 - b)

            mean_sq(0, 0)
            dve.wait_ge(pre_in, 16)
            norm_h(0, 0)
            vb_lo(0)
            h_lo(0, 0)
            vb_lo(1)
            vb_lo(2)
            vb_lo(3)
            mean_sq(1, 1)
            norm_h(1, 1)
            vb_lo(5)
            vb_lo(6)
            vb_lo(7)
            h_lo(1, 1)
            dve.wait_ge(wsh_ok, 1)
            ws4f = ws_st[:, :].bitcast(f32).rearrange("p (g x t) -> p g x t", g=KT, x=2)
            nc.vector.tensor_tensor(ws4[:, :, 1, :], ps_m[:, :].rearrange("p (g t) -> p g t", g=KT),
                                    ws4f[:, :, 0, :], ALU.subtract).then_inc(wsl_ok, 1)
            dve.wait_ge(ln_in, 32)
            step(1, 0, 1, mixes=False)
            step(2, 0, 0)
            with dve.Fori(1, NT // 2 - 1) as i:
                own.at(2 * LN_LINKS * i)
                for b in (1, 0):
                    step(2 * i + 2 - b, i, b)
            own.at(LN_LINKS * (NT - 2))
            ln_stats(NT // 2 - 1, 0)
            mix_read(NT - 3, 1)
            ln_apply(NT - 2, 0)
            ln_stats(NT // 2 - 1, 1)
            ln_apply(NT - 1, 1)
            mix_read(NT - 2, 0)
            mix_read(NT - 1, 1)

            with dve.Fori(0, KT) as g:
                dve.wait_ge(acc_free[0], half(N_U + 2, g, 2))
                dve.wait_ge(mix_in, 16 * (g + 1))
                nc.vector.tensor_tensor(buf_a[:, :], buf_a[:, :], buf_b[:, :], ALU.mult).then_inc(um_ok, 1)
                dve.wait_ge(gate_t_ok, g + 1)
                nc.vector.scalar_tensor_tensor(out=buf_t[:, :], in0=buf_t[:, :], scalar=1.0, in1=acc[1][:, :],
                                               op0=ALU.add, op1=ALU.mult).then_inc(acc_free[1], 1)
                dve.wait_ge(um_ok, g + 1)
                dve.wait_ge(acc_free[1], half(N_U + 2, g, 2))
                nc.vector.scalar_tensor_tensor(out=buf_t[:, :], in0=buf_t[:, :], scalar=0.5, in1=buf_a[:, :],
                                               op0=ALU.mult, op1=ALU.mult).then_inc(prod_ok, 1)
                dve.wait_ge(prod_ok, g + 1)
                dve.wait_ge(ghi_ok, g + 1)
                nc.vector.tensor_tensor(tile(g_lo, g), buf_t[:, :], tile(g_hi, g).bitcast(f32), ALU.subtract).then_inc(g_ready, 1)
            base = own.base + own.k
            with dve.Fori(0, KT) as j:
                own.at(base + j)
                dve.wait_ge(acc_free[0], half(N_MB + 2, j, 2))
                own.link(nc.vector.tensor_scalar(buf_t[:, :], buf_t[:, :], 0.5, 0.5, ALU.mult, ALU.add))
                dve.wait_ge(unit_done, N_MB + 2 + 2 * j)
                dve.wait_ge(spill_out, 16 * (j + 1))
                nc.vector.tensor_tensor(buf_a[:, :], acc[1][:, :], buf_t[:, :], ALU.mult).then_inc(acc_free[1], 1)
            base = base + KT
            dve.wait_ge(khi_ok, 1)
            for kv in range(N_KV):
                rows = slice(kv * HEAD_DIM, (kv + 1) * HEAD_DIM)
                cols = slice(kv * SEQ, (kv + 1) * SEQ)
                for hf in range(2):
                    last = nc.vector.tensor_tensor(k_lo[hf * HEAD_DIM:(hf + 1) * HEAD_DIM, cols], buf_a[rows, :],
                                                   k_hi[rows, cols].bitcast(f32), ALU.subtract)
            last.then_inc(klo_ok, 1)
            dve.wait_ge(vhi_ok, 1)
            v5 = v_st[:, :].rearrange("p (v t x d) -> p v t x d", v=N_KV, t=NT, x=2)
            v5f = v_st[:, :].bitcast(f32).rearrange("p (v t x d) -> p v t x d", v=N_KV, t=NT, x=2)
            for kv in range(N_KV):
                last = nc.vector.tensor_tensor(
                    v5[:, kv, :, 1, :], ps_m[:, :].rearrange("p (t v d) -> p t v d", t=NT, v=N_KV)[:, :, kv, :],
                    v5f[:, kv, :, 0, :], ALU.subtract)
            last.then_inc(scores_used, 1)
            dve.wait_ge(sink_in, 16)

            def q_lo(p, r):
                dve.wait_ge(q_hi_ok, 2 * p + 1)
                nc.vector.tensor_tensor(q_st[0][64:128, :], acc[r][0:64, :], q_st[0][0:64, :].bitcast(f32), ALU.subtract)
                dve.wait_ge(q_hi_ok, 2 * p + 2)
                nc.vector.tensor_tensor(q_st[1][0:64, :], acc[r][64:128, :], q_st[1][64:128, :].bitcast(f32),
                                        ALU.subtract).then_inc(acc_free[r], 1)

            q_lo(0, 0)
            dve.wait_ge(before_ok, 1)
            before_i = before[:, :].bitcast(mybir.dt.int32)
            heads = lambda t: t.rearrange("p (h j) -> p h j", h=2)
            blocks = lambda t: t.rearrange("p (h b j) -> p h b j", h=2, b=2)
            PAIR_LINKS = 3 + (NT - 1) + NT

            def pair(p, i, c, r, final=False):
                own.link(nc.vector.tensor_copy(sink_p[:, :], sink_b[:, bass.ds(2 * p, 2)]))
                dve.wait_ge(bias_in, 16 * (p + 1))
                stand_alone(dve)
                own.link(nc.vector.tensor_copy(heads(bias_p[:, :]), blocks(bias_t[:, :])[:, :, 1, :]))
                stand_alone(dve)
                own.link(nc.vector.copy_predicated(heads(bias_p[:, :]), heads(before_i), blocks(bias_t[:, :])[:, :, 0, :]))
                for k in range(13):
                    if 1 <= k < 9:
                        m2 = slice(2 * k - 2, 2 * k)
                        dve.wait_ge(exp_ok, 8 * p + k)
                        own.link(nc.vector.tensor_tensor(denom[:, m2], row_sum[:, m2], sink_e[:, m2], ALU.add))
                        nc.vector.reciprocal(inv_den[:, m2], denom[:, m2]).then_inc(inv_ok, 1)
                    if 2 <= k < 10:
                        dve.wait_ge(pth_ok, 8 * p + k - 1)
                        nc.vector.tensor_tensor(pt_packed[:, 256:512], ps_p, pt_packed[:, 0:256].bitcast(f32),
                                                ALU.subtract).then_inc(ptl_ok, 1)
                    if k < 8:
                        c2 = slice(2 * k, 2 * k + 2)
                        dve.wait_ge(scores_ok, 8 * p + k + 1)
                        stand_alone(dve)
                        if k > 0:
                            own.link(nc.vector.copy_predicated(blocks(ps_s)[:, :, 1, :], heads(before_i), blocks(ps_s)[:, :, 0, :]))
                            stand_alone(dve)
                        for h in range(2):
                            cs = slice(h * P, (h + 1) * P)
                            bias = bias_p[:, cs] if k else bias_t[:, h * 256 + P:(h + 1) * 256]
                            last = nc.vector.tensor_tensor_reduce(
                                out=prob[k % 3][:, cs], in0=ps_s[:, h * 256 + P:(h + 1) * 256], in1=bias, scale=HEAD_DIM ** -0.5,
                                scalar=sink_p[:, h:h + 1], op0=ALU.add, op1=ALU.max,
                                accum_out=row_max[:, 2 * k + h:2 * k + h + 1])
                        last.then_inc(scores_used, 1)
                        dve.wait_ge(scores_used, 8 * p + k + 2)
                        nc.vector.tensor_scalar(neg_max[:, c2], row_max[:, c2], -1.0, None, ALU.mult)
                        nc.vector.tensor_tensor(sink_d[:, c2], sink_p[:, :], row_max[:, c2],
                                                ALU.subtract).then_inc(max_ok, 1)
                    if k >= 6 and k % 2 == 0:
                        g = (k - 6) // 2
                        if g == 0:
                            dve.wait_ge(g_ready, KT + p)
                        dve.wait_ge(otmp_ok, 4 * p + g + 1)
                        o = ps_m[:, (g % 2) * 512:(g % 2 + 1) * 512]
                        cols = slice(g * 256, (g + 1) * 256)
                        nc.vector.tensor_tensor(buf_b[0:64, cols], o[0:64, 0:256], o_tmp[g % 2][0:64, :], ALU.add)
                        nc.vector.tensor_tensor(buf_b[64:128, cols], o[64:128, 256:512], o_tmp[g % 2][64:128, :],
                                                ALU.add).then_inc(oadd_ok, 1)
                    if k in (3, 4):
                        hs = slice((k - 3) * HALF, (k - 2) * HALF)
                        if k == 3:
                            dve.wait_ge(g_ready, KT + p)
                            dve.wait_ge(gtan_ok, p + 1)
                        last = nc.vector.scalar_tensor_tensor(out=buf_a[:, hs], in0=buf_t[:, hs], scalar=1.0,
                                                              in1=acc[1 - r][:, hs], op0=ALU.add, op1=ALU.mult)
                        if k == 4:
                            last.then_inc(acc_free[1 - r], 1)
                if final:
                    dve.wait_ge(oadd_ok, 4 * p + 4)
                    nc.vector.tensor_tensor(buf_b[:, :], buf_b[:, :], buf_a[:, :], ALU.mult).then_inc(og_ok, 1)
                    dve.wait_ge(ghi_ok, KT + p + 1)
                    nc.vector.tensor_tensor(tile(g_lo, p), buf_b[:, :], tile(g_hi, p).bitcast(f32), ALU.subtract).then_inc(g_ready, 1)
                else:
                    q_lo(p + 1, 1 - r)

            with dve.Fori(0, PAIRS // 2 - 1) as i:
                own.at(base + 2 * PAIR_LINKS * i)
                for r in range(2):
                    pair(2 * i + r, i, N_ATT + 3 * r, r)
            own.at(base + 2 * PAIR_LINKS * (PAIRS // 2 - 1))
            for r in range(2):
                pair(PAIRS - 2 + r, PAIRS // 2 - 1, N_ATT + 3 * r, r, final=(r == 1))
            def tile_lo(t, b, k0=0, k1=KT):
                dve.wait_ge(unit_done, N_OUT + t - 1)
                nc.vector.tensor_copy(w_lo[b][:, k0 * P:k1 * P].rearrange("p (k s) -> p k s", k=k1 - k0),
                                      ht_lo[:, :].bitcast(f32).rearrange("p (k s) -> p k s", k=KT)[:, k0:k1, bass.ds(t * P, P)]
                                      ).then_inc(mt_lo, 1)

            def merge(j, i, b):
                    dve.wait_ge(unit_done, N_YA + 1 + b + 2 * i)
                    dve.wait_ge(sigr_in, 16 * (j + 1))
                    nc.vector.tensor_tensor(buf_b[:, :], acc[b][:, :], buf_t[:, :], ALU.mult).then_inc(acc_free[b], 1)
                    dve.wait_ge(acc_free[b], half(N_YA + 2, i, 2))
                    dve.wait_ge(accr_in, 16 * (j + 1))
                    nc.vector.tensor_tensor(buf_b[:, :], buf_b[:, :], buf_a[:, :], ALU.add).then_inc(mrg_ok, 1)
                    dve.wait_ge(mhi_ok, j + 1)
                    nc.vector.tensor_tensor(tile(ht_lo, j), buf_b[:, :], tile(ht_hi, j).bitcast(f32), ALU.subtract).then_inc(g_ready, 1)

            dve.wait_ge(g_ready, 2 * KT)
            with dve.Fori(0, KT // 2 - 1) as i:
                for b in range(2):
                    merge(2 * i + b, i, b)
            merge(KT - 2, KT // 2 - 1, 0)
            dve.wait_ge(g_ready, 3 * KT - 1)
            tile_lo(0, 0, 0, KT - 1)
            tile_lo(1, 1, 0, KT - 1)
            merge(KT - 1, KT // 2 - 1, 1)
            dve.wait_ge(g_ready, 3 * KT)
            for b in range(2):
                tile_lo(b, b, KT - 1, KT)

            for s in (5, 7):
                dve.wait_ge(hi_done, N_OUT + s + 1)
                nc.vector.tensor_tensor(tile(g_hi, s), wo_land(s)[:, :], tile(g_hi, s - 4).bitcast(f32), ALU.subtract).then_inc(wo_lo_dve, 1)
            dve.wait_ge(post_in, 16)
            ys = (buf_a, buf_b)

            def weigh(b, cols=slice(0, D_MODEL)):
                return nc.vector.tensor_tensor(ys[b][:, cols], acc[b][:, cols], buf_t[:, cols], ALU.mult).then_inc(yw_ok, 1)

            def mean_sq_out(b):
                nc.vector.tensor_scalar(msq[:, b:b + 1], ssq[:, b:b + 1], 1.0 / D_MODEL, EPS, ALU.mult, ALU.add).then_inc(oms_ok, 1)

            def norm_out(b, cols=slice(0, D_MODEL)):
                nc.vector.scalar_tensor_tensor(out=ys[b][:, cols], in0=ys[b][:, cols], scalar=rstd[:, b:b + 1],
                                               in1=x_r[b][:, cols], op0=ALU.mult, op1=ALU.add).then_inc(y_ok, 1)

            def out_tile(t, b, ht, first):
                if not first:
                    dve.wait_ge(y_out[b], 16 * ht)
                dve.wait_ge(osq_ok, t + 1)
                mean_sq_out(b)
                nc.vector.tensor_tensor(ys[b][:, :], acc[b][:, :], buf_t[:, :], ALU.mult).then_inc(acc_free[b], 1)
                dve.wait_ge(acc_free[b], N_OUT // 2 + 1 + ht)
                dve.wait_ge(xr_in[b], 16 * (ht + 1))
                dve.wait_ge(ors_ok, t + 1)
                norm_out(b)

            out_tile(0, 0, 0, True)
            tile_lo(2, 0)
            out_tile(1, 1, 0, True)
            tile_lo(3, 1)
            with dve.Fori(1, NT // 2 - 1) as i:
                for b in range(2):
                    out_tile(2 * i + b, b, i, False)
                    tile_lo(2 * i + b + 2, b)
            out_tile(NT - 2, 0, NT // 2 - 1, False)
            dve.wait_ge(y_out[1], 16 * (NT // 2 - 1))
            dve.wait_ge(osq_ok, NT)
            weigh(1, slice(0, HALF))
            dve.wait_ge(osq_ok, NT + 1)
            nc.vector.tensor_tensor(ssq[:, 1:2], ssq_h[:, 0:1], ssq_h[:, 1:2], ALU.add).then_inc(ssum_ok, 1)
            dve.wait_ge(ssum_ok, 1)
            mean_sq_out(1)
            weigh(1, slice(HALF, D_MODEL))
            dve.wait_ge(yw_ok, 2)
            dve.wait_ge(xr_in[1], 16 * NT // 2)
            dve.wait_ge(ors_ok, NT)
            for hf in range(2):
                norm_out(1, slice(hf * HALF, (hf + 1) * HALF))


INPUTS = ("x", "rel_bias", "pre_norm", "post_norm", "w_in", "sinks", "sgu_ln_g", "sgu_ln_b", "w_spatial",
          "b_spatial", "w_branch_a", "w_branch_b", "w_out")


def kernel(**inputs):
    import concourse.bacc as bacc
    from concourse.bass_utils import run_bass_kernel_spmd

    nc = bacc.Bacc("TRN2", target_bir_lowering=False, num_devices=1, dynamic_dma_scratch_size=1024)
    arrays, args = {}, []
    for name in INPUTS:
        a = np.ascontiguousarray(inputs[name])
        arrays["in_" + name] = a
        args.append(nc.dram_tensor("in_" + name, a.shape, mybir.dt.from_np(a.dtype), kind="ExternalInput").ap())
    args.append(nc.dram_tensor("out", inputs["x"].shape, mybir.dt.float32, kind="ExternalOutput").ap())
    build(nc, *args)
    r = run_bass_kernel_spmd(nc, [arrays], core_ids=[0])
    return r.results[0]["out"]
```
